# Optimizing a Trainium2 kernel written in Bass

```python
import jax, jax.numpy as jnp
from jax import lax
import numpy as np

D_MODEL = 1024
BATCH = 1
SEQ = 1024
DEPTH = 1

RET_HEADS = 4
RET_HEAD_DIM = D_MODEL // 2 // RET_HEADS
RET_WIDTH = RET_HEADS * RET_HEAD_DIM
RET_CHUNK = 128
DN_HEADS = 4
DN_HEAD_DIM = D_MODEL // 2 // DN_HEADS
DN_WIDTH = DN_HEADS * DN_HEAD_DIM
DN_CHUNK = 64
CONV_WIDTH = 4
ROPE_THETA = 10000.0
N_GROUPS = 4
EXPERTS_PER_GROUP = 8
N_EXPERTS = N_GROUPS * EXPERTS_PER_GROUP
TOP_K = 2
D_EXPERT = D_MODEL // 2
N_MOD = 6
NORM_EPS = 1e-6
IN_COLS = 4 * RET_WIDTH + 4 * DN_WIDTH + 2 * DN_HEADS


def rmsnorm(x, w=None):
    xf = x.astype(jnp.float32)
    y = xf * lax.rsqrt(jnp.mean(xf * xf, axis=-1, keepdims=True) + NORM_EPS)
    if w is not None:
        y = y * w.astype(jnp.float32)
    return y.astype(x.dtype)

def l2norm(x):
    return x * lax.rsqrt(jnp.sum(x * x, axis=-1, keepdims=True) + NORM_EPS)

def modulate(h, shift, scale):
    return h * (1.0 + scale[:, None, :]) + shift[:, None, :]

def rotary(x, positions):
    dh = x.shape[-1]
    inv_freq = ROPE_THETA ** (-jnp.arange(0, dh, 2, dtype=jnp.float32) / dh)
    ang = positions.astype(jnp.float32)[..., None] * inv_freq
    cos, sin = jnp.cos(ang)[:, :, None, :], jnp.sin(ang)[:, :, None, :]
    xf = x.astype(jnp.float32)
    x1, x2 = xf[..., : dh // 2], xf[..., dh // 2:]
    return jnp.concatenate([x1 * cos - x2 * sin, x2 * cos + x1 * sin], axis=-1)

def retention(q, k, v):
    B, T, H, Dh = q.shape
    C = RET_CHUNK
    N = T // C
    log_gamma = jnp.log1p(-jnp.power(2.0, -5.0 - jnp.arange(H, dtype=jnp.float32)))
    q = q.astype(jnp.float32).reshape(B, N, C, H, Dh)
    k = (k.astype(jnp.float32) * Dh ** -0.5).reshape(B, N, C, H, Dh)
    v = v.astype(jnp.float32).reshape(B, N, C, H, Dh)
    idx = jnp.arange(C, dtype=jnp.float32)
    rel = idx[:, None] - idx[None, :]
    causal = rel >= 0
    decay = jnp.where(causal[None], jnp.exp(log_gamma[:, None, None] * jnp.where(causal, rel, 0.0)[None]), 0.0)
    scores = jnp.einsum('bnihd,bnjhd->bnhij', q, k) * decay[None, None]
    inner = jnp.einsum('bnhij,bnjhd->bnihd', scores, v)
    k_w = k * jnp.exp(log_gamma[None, :] * (C - 1 - idx)[:, None])[:, :, None]
    incr = jnp.einsum('bnjhk,bnjhv->nbhkv', k_w, v)
    chunk_decay = jnp.exp(log_gamma * C)[None, :, None, None]

    def step(state, incr_n):
        return chunk_decay * state + incr_n, state

    _, s_prev = lax.scan(step, jnp.zeros((B, H, Dh, Dh), jnp.float32), incr)
    q_w = q * jnp.exp(log_gamma[None, :] * (idx + 1.0)[:, None])[:, :, None]
    cross = jnp.einsum('bnihk,nbhkv->bnihv', q_w, s_prev)
    return (inner + cross).reshape(B, T, H, Dh)

def causal_dwconv(x, w):
    k = w.shape[0]
    return lax.conv_general_dilated(x, w[:, None, :].astype(x.dtype), window_strides=(1,), padding=((k - 1, 0),),
                                    dimension_numbers=('NWC', 'WIO', 'NWC'), feature_group_count=x.shape[-1])

def gated_delta_rule(q, k, v, g, beta):
    B, T, H, Dh = q.shape
    C = DN_CHUNK
    N = T // C
    to_chunks = lambda t: t.reshape(B, N, C, H, -1).transpose(0, 3, 1, 2, 4)
    q, k, v = to_chunks(q), to_chunks(k), to_chunks(v)
    g = jnp.cumsum(g.reshape(B, N, C, H).transpose(0, 3, 1, 2), axis=-1)
    beta = beta.reshape(B, N, C, H).transpose(0, 3, 1, 2)
    k_beta = k * beta[..., None]
    v_beta = v * beta[..., None]
    tri_incl = jnp.tril(jnp.ones((C, C), bool))
    tri_strict = jnp.tril(jnp.ones((C, C), bool), -1)
    decay = jnp.exp(jnp.where(tri_incl, g[..., :, None] - g[..., None, :], -jnp.inf))
    a_mat = jnp.where(tri_strict, (k_beta @ jnp.swapaxes(k, -1, -2)) * decay, 0.0)
    eye = jnp.eye(C, dtype=jnp.float32)
    t_mat = lax.linalg.triangular_solve(eye + a_mat, jnp.broadcast_to(eye, a_mat.shape),
                                        left_side=True, lower=True, unit_diagonal=True)
    u = t_mat @ v_beta
    w = t_mat @ (k_beta * jnp.exp(g)[..., None])
    attn = (q @ jnp.swapaxes(k, -1, -2)) * decay
    q_g = q * jnp.exp(g)[..., None]
    k_tail = k * jnp.exp(g[..., -1:] - g)[..., None]
    g_last = jnp.exp(g[..., -1])
    lead = lambda t: jnp.moveaxis(t, 2, 0)

    def step(state, inp):
        u_n, w_n, qg_n, kt_n, attn_n, gl_n = inp
        v_new = u_n - w_n @ state
        o_n = qg_n @ state + attn_n @ v_new
        state = state * gl_n[..., None, None] + jnp.swapaxes(kt_n, -1, -2) @ v_new
        return state, o_n

    _, o = lax.scan(step, jnp.zeros((B, H, Dh, Dh), jnp.float32),
                    (lead(u), lead(w), lead(q_g), lead(k_tail), lead(attn), lead(g_last)))
    return o.transpose(1, 0, 3, 2, 4).reshape(B, T, H, Dh)

def hierarchical_moe(h, w_group, b_group, w_expert, b_expert, w1, w3, w2):
    B, T, D = h.shape
    xf = h.reshape(-1, D)
    n = xf.shape[0]
    group_probs = jax.nn.softmax((xf @ w_group + b_group).astype(jnp.float32), axis=-1)
    p_group, g_idx = lax.top_k(group_probs, 1)
    e_logits = (xf @ w_expert + b_expert).astype(jnp.float32).reshape(n, N_GROUPS, EXPERTS_PER_GROUP)
    e_logits = jnp.take_along_axis(e_logits, g_idx[:, :, None], axis=1)[:, 0]
    p_exp, e_local = lax.top_k(jax.nn.softmax(e_logits, axis=-1), TOP_K)
    gate = p_group * p_exp / jnp.sum(p_exp, axis=-1, keepdims=True)
    flat_e = (g_idx * EXPERTS_PER_GROUP + e_local).reshape(-1)
    order = jnp.argsort(flat_e)
    tok = order // TOP_K
    group_sizes = jnp.bincount(flat_e, length=N_EXPERTS).astype(jnp.int32)
    xs = xf[tok]
    hid = jax.nn.silu(lax.ragged_dot(xs, w1, group_sizes)) * lax.ragged_dot(xs, w3, group_sizes)
    ys = lax.ragged_dot(hid.astype(xs.dtype), w2, group_sizes) * gate.reshape(-1)[order][:, None].astype(xs.dtype)
    return jax.ops.segment_sum(ys, tok, num_segments=n).reshape(B, T, D)

def first_inputs(seed: int = 0) -> dict:
    key = jax.random.key(seed)
    ks = jax.random.split(key, 24)
    f32 = jnp.float32
    nrm = lambda k, shape, s: jax.random.normal(k, shape, f32) * s
    dt = jnp.exp(jax.random.uniform(ks[9], (DEPTH, DN_HEADS), f32, np.log(1e-3), np.log(1e-1)))
    return {
        'x': nrm(ks[0], (BATCH, SEQ, D_MODEL), 1.0),
        'c': nrm(ks[1], (BATCH, D_MODEL), 1.0),
        'positions': jnp.broadcast_to(jnp.arange(SEQ, dtype=jnp.int32)[None], (BATCH, SEQ)),
        'w_ada': nrm(ks[2], (DEPTH, D_MODEL, N_MOD * D_MODEL), D_MODEL ** -0.5),
        'b_ada': nrm(ks[3], (DEPTH, N_MOD * D_MODEL), 0.01),
        'norm1_w': 1.0 + nrm(ks[4], (DEPTH, D_MODEL), 0.01),
        'w_in': nrm(ks[5], (DEPTH, D_MODEL, IN_COLS), D_MODEL ** -0.5),
        'conv_w': nrm(ks[6], (DEPTH, CONV_WIDTH, 3 * DN_WIDTH), CONV_WIDTH ** -0.5),
        'a_log': jnp.log(jax.random.uniform(ks[7], (DEPTH, DN_HEADS), f32, 1.0, 16.0)),
        'dt_bias': dt + jnp.log(-jnp.expm1(-dt)),
        'dn_norm_w': 1.0 + nrm(ks[8], (DEPTH, DN_HEAD_DIM), 0.01),
        'w_out': nrm(ks[10], (DEPTH, D_MODEL, D_MODEL), D_MODEL ** -0.5),
        'norm2_w': 1.0 + nrm(ks[11], (DEPTH, D_MODEL), 0.01),
        'w_group': nrm(ks[12], (DEPTH, D_MODEL, N_GROUPS), D_MODEL ** -0.5),
        'b_group': nrm(ks[13], (DEPTH, N_GROUPS), 0.01),
        'w_expert': nrm(ks[14], (DEPTH, D_MODEL, N_EXPERTS), D_MODEL ** -0.5),
        'b_expert': nrm(ks[15], (DEPTH, N_EXPERTS), 0.01),
        'w1': nrm(ks[16], (DEPTH, N_EXPERTS, D_MODEL, D_EXPERT), D_MODEL ** -0.5),
        'w3': nrm(ks[17], (DEPTH, N_EXPERTS, D_MODEL, D_EXPERT), D_MODEL ** -0.5),
        'w2': nrm(ks[18], (DEPTH, N_EXPERTS, D_EXPERT, D_MODEL), D_EXPERT ** -0.5),
        'final_norm_w': 1.0 + nrm(ks[19], (D_MODEL,), 0.01),
    }

def first_block(x, c, positions, w_ada, b_ada, norm1_w, w_in, conv_w, a_log, dt_bias, dn_norm_w, w_out,
              norm2_w, w_group, b_group, w_expert, b_expert, w1, w3, w2, final_norm_w):
    B, T, D = x.shape
    cuts = [RET_WIDTH, 2 * RET_WIDTH, 3 * RET_WIDTH, 4 * RET_WIDTH,
            4 * RET_WIDTH + DN_WIDTH, 4 * RET_WIDTH + 2 * DN_WIDTH, 4 * RET_WIDTH + 3 * DN_WIDTH,
            4 * RET_WIDTH + 4 * DN_WIDTH, 4 * RET_WIDTH + 4 * DN_WIDTH + DN_HEADS]
    for l in range(DEPTH):
        mod = jax.nn.silu(c) @ w_ada[l] + b_ada[l]
        shift1, scale1, gate1, shift2, scale2, gate2 = jnp.split(mod, N_MOD, axis=-1)

        h = modulate(rmsnorm(x, norm1_w[l]), shift1, scale1)
        proj = h @ w_in[l]
        r_q, r_k, r_v, r_g, d_q, d_k, d_v, d_z, d_a, d_b = jnp.split(proj, cuts, axis=-1)

        heads = lambda t, nh: t.reshape(B, T, nh, -1)
        rq = rotary(heads(r_q, RET_HEADS), positions)
        rk = rotary(heads(r_k, RET_HEADS), positions)
        ret = retention(rq, rk, heads(r_v, RET_HEADS))
        ret = rmsnorm(ret).reshape(B, T, RET_WIDTH) * jax.nn.silu(r_g.astype(jnp.float32))

        qkv = jax.nn.silu(causal_dwconv(jnp.concatenate([d_q, d_k, d_v], axis=-1), conv_w[l]))
        cq, ck, cv = jnp.split(qkv.astype(jnp.float32), 3, axis=-1)
        dq = l2norm(heads(cq, DN_HEADS)) * DN_HEAD_DIM ** -0.5
        dk = l2norm(heads(ck, DN_HEADS))
        beta = jax.nn.sigmoid(d_b.astype(jnp.float32))
        g = -jnp.exp(a_log[l].astype(jnp.float32)) * jax.nn.softplus((d_a + dt_bias[l]).astype(jnp.float32))
        dn = gated_delta_rule(dq, dk, heads(cv, DN_HEADS), g, beta)
        dn = rmsnorm(dn, dn_norm_w[l]).reshape(B, T, DN_WIDTH) * jax.nn.silu(d_z.astype(jnp.float32))

        mix = jnp.concatenate([ret, dn], axis=-1).astype(x.dtype) @ w_out[l]
        x = x + gate1[:, None, :] * mix

        h2 = modulate(rmsnorm(x, norm2_w[l]), shift2, scale2)
        ffn = hierarchical_moe(h2, w_group[l], b_group[l], w_expert[l], b_expert[l], w1[l], w3[l], w2[l])
        x = x + gate2[:, None, :] * ffn.astype(x.dtype)
    return rmsnorm(x, final_norm_w)


GRID_W = 64
NA_HEAD_DIM = 64
NA_WIDTH = D_MODEL // 2
NA_HEADS = NA_WIDTH // NA_HEAD_DIM
NA_KH = 8
NA_KW = 16
GLA_HEADS = 4
GLA_VAL_WIDTH = D_MODEL - NA_WIDTH
GLA_DV = GLA_VAL_WIDTH // GLA_HEADS
GLA_DK = GLA_DV // 2
GLA_KEY_WIDTH = GLA_HEADS * GLA_DK
GLA_GATE_RANK = 16
GLA_GATE_NORM = 16.0
GLA_CHUNK = 64
D_MIX = NA_WIDTH + GLA_VAL_WIDTH
D_FF = 4 * D_MODEL
IN_SPLITS = [NA_WIDTH, NA_WIDTH, NA_WIDTH,
             GLA_KEY_WIDTH, GLA_KEY_WIDTH, GLA_VAL_WIDTH, GLA_VAL_WIDTH,
             GLA_GATE_RANK, GLA_GATE_RANK]
D_IN = sum(IN_SPLITS)
EPS = 1e-6


def rmsnorm_2(x, g):
    xf = x.astype(jnp.float32)
    y = xf * lax.rsqrt(jnp.mean(xf * xf, axis=-1, keepdims=True) + EPS)
    return (y * g.astype(jnp.float32)).astype(x.dtype)

def neighbourhood_attention(q, k, v, rpb):
    B, T, H, dh = q.shape
    R = T // GRID_W
    W = GRID_W
    KH = min(NA_KH, R)
    KW = NA_KW
    grid = lambda t: t.reshape(B, R, W, H, dh).transpose(0, 3, 1, 2, 4)
    qg, kg, vg = grid(q), grid(k), grid(v)
    rows = jnp.arange(R)
    row_start = jnp.clip(rows - KH // 2, 0, R - KH)
    row_idx = row_start[:, None] + jnp.arange(KH)[None, :]
    k_rows = kg[:, :, row_idx]
    v_rows = vg[:, :, row_idx]
    scores = jnp.einsum('bhrqd,bhrikd->bhrqik', qg, k_rows).astype(jnp.float32)
    scores = scores * (dh ** -0.5)
    dr_idx = row_idx - rows[:, None] + (NA_KH - 1)
    cols = jnp.arange(W)
    dc = cols[None, :] - cols[:, None]
    dc_idx = jnp.clip(dc, -(KW - 1), KW - 1) + (KW - 1)
    bias = rpb.astype(jnp.float32)[:, dr_idx[:, None, :, None], dc_idx[None, :, None, :]]
    col_start = jnp.clip(cols - KW // 2, 0, W - KW)
    in_win = (cols[None, :] >= col_start[:, None]) & (cols[None, :] < col_start[:, None] + KW)
    scores = jnp.where(in_win[None, None, None, :, None, :], scores + bias[None], -jnp.inf)
    p = jax.nn.softmax(scores.reshape(B, H, R, W, KH * W), axis=-1).reshape(B, H, R, W, KH, W)
    out = jnp.einsum('bhrqik,bhrikd->bhrqd', p.astype(v.dtype), v_rows)
    return out.transpose(0, 2, 3, 1, 4).reshape(B, T, H * dh)

def gla_chunked(q, k, v, log_a, strict):
    B, H, T, dk = q.shape
    dv = v.shape[-1]
    C = GLA_CHUNK
    N = T // C
    q = q.reshape(B, H, N, C, dk)
    k = k.reshape(B, H, N, C, dk)
    v = v.reshape(B, H, N, C, dv)
    b = jnp.cumsum(log_a.reshape(B, H, N, C, dk), axis=-2)
    q_dec = q * jnp.exp(b)
    k_inv = k * jnp.exp(-b)
    mask = jnp.tril(jnp.ones((C, C), dtype=bool), k=-1 if strict else 0)
    A = jnp.where(mask, jnp.einsum('bhnid,bhnjd->bhnij', q_dec, k_inv), 0.0)
    o_intra = jnp.einsum('bhnij,bhnje->bhnie', A, v)
    b_last = b[..., -1:, :]
    contrib = jnp.einsum('bhncd,bhnce->bhnde', k * jnp.exp(b_last - b), v)
    decay = jnp.exp(b_last[..., 0, :])

    def step(S, inp):
        g, c = inp
        return g[..., None] * S + c, S

    S0 = jnp.zeros((B, H, dk, dv), dtype=contrib.dtype)
    _, S_prev = lax.scan(step, S0, (jnp.moveaxis(decay, 2, 0), jnp.moveaxis(contrib, 2, 0)))
    S_prev = jnp.moveaxis(S_prev, 0, 2)
    o = o_intra + jnp.einsum('bhncd,bhnde->bhnce', q_dec, S_prev)
    return o.reshape(B, H, T, dv)

def bidirectional_gla(q, k, v, r, z_f, z_b, gu_f, gb_f, gu_b, gb_b, norm_g):
    B, T, _ = q.shape
    bhtd = lambda t, d: t.reshape(B, T, GLA_HEADS, d).transpose(0, 2, 1, 3)
    qh = bhtd(q, GLA_DK) * (GLA_DK ** -0.5)
    kh = bhtd(k, GLA_DK)
    vh = bhtd(v, GLA_DV)
    log_a_f = jax.nn.log_sigmoid((z_f @ gu_f + gb_f).astype(jnp.float32)) / GLA_GATE_NORM
    log_a_b = jax.nn.log_sigmoid((z_b @ gu_b + gb_b).astype(jnp.float32)) / GLA_GATE_NORM
    la_f = bhtd(log_a_f, GLA_DK)
    la_b = bhtd(log_a_b, GLA_DK)
    fwd = gla_chunked(qh, kh, vh, la_f, strict=False)
    flip = lambda t: jnp.flip(t, axis=2)
    bwd = flip(gla_chunked(flip(qh), flip(kh), flip(vh), flip(la_b), strict=True))
    o = (fwd + bwd).astype(v.dtype).transpose(0, 2, 1, 3)
    o = rmsnorm_2(o, norm_g) * jax.nn.silu(r.reshape(B, T, GLA_HEADS, GLA_DV))
    return o.reshape(B, T, GLA_VAL_WIDTH)

def hybrid_mixer(h, ln_g, w_in, rpb, gu_f, gb_f, gu_b, gb_b, norm_g, w_out):
    B, T, _ = h.shape
    n = rmsnorm_2(h, ln_g)
    proj = n @ w_in
    offsets = [int(o) for o in np.cumsum(IN_SPLITS)[:-1]]
    qa, ka, va, qg, kg, vg, rg, zf, zb = jnp.split(proj, offsets, axis=-1)
    na_heads = lambda t: t.reshape(B, T, NA_HEADS, NA_HEAD_DIM)
    y_na = neighbourhood_attention(na_heads(qa), na_heads(ka), na_heads(va), rpb)
    y_gla = bidirectional_gla(qg, kg, vg, rg, zf, zb, gu_f, gb_f, gu_b, gb_b, norm_g)
    return jnp.concatenate([y_na, y_gla], axis=-1) @ w_out

def sqrelu_mlp(h, ln_g, w1, w2):
    u = rmsnorm_2(h, ln_g) @ w1
    return jnp.square(jax.nn.relu(u)) @ w2

def second_inputs(seed: int = 0) -> dict:
    key = jax.random.key(seed)
    ks = jax.random.split(key, 16)
    nrm = lambda k, shape, s: jax.random.normal(k, shape, jnp.float32) * s
    L = DEPTH
    return {
        "x": nrm(ks[0], (BATCH, SEQ, D_MODEL), 1.0),
        "ln_mix_g": 1.0 + nrm(ks[1], (L, D_MODEL), 0.02),
        "w_in": nrm(ks[2], (L, D_MODEL, D_IN), D_MODEL ** -0.5),
        "na_rpb": nrm(ks[3], (L, NA_HEADS, 2 * NA_KH - 1, 2 * NA_KW - 1), 0.02),
        "gla_gate_up_fwd": nrm(ks[4], (L, GLA_GATE_RANK, GLA_KEY_WIDTH), GLA_GATE_RANK ** -0.5),
        "gla_gate_bias_fwd": nrm(ks[5], (L, GLA_KEY_WIDTH), 0.1),
        "gla_gate_up_bwd": nrm(ks[6], (L, GLA_GATE_RANK, GLA_KEY_WIDTH), GLA_GATE_RANK ** -0.5),
        "gla_gate_bias_bwd": nrm(ks[7], (L, GLA_KEY_WIDTH), 0.1),
        "gla_norm_g": 1.0 + nrm(ks[8], (L, GLA_DV), 0.02),
        "w_out": nrm(ks[9], (L, D_MIX, D_MODEL), D_MIX ** -0.5),
        "ln_ff_g": 1.0 + nrm(ks[10], (L, D_MODEL), 0.02),
        "w_ff1": nrm(ks[11], (L, D_MODEL, D_FF), D_MODEL ** -0.5),
        "w_ff2": nrm(ks[12], (L, D_FF, D_MODEL), D_FF ** -0.5),
        "ln_final_g": 1.0 + nrm(ks[13], (D_MODEL,), 0.02),
    }

def second_block(x, ln_mix_g, w_in, na_rpb, gla_gate_up_fwd, gla_gate_bias_fwd,
              gla_gate_up_bwd, gla_gate_bias_bwd, gla_norm_g, w_out,
              ln_ff_g, w_ff1, w_ff2, ln_final_g):
    h = x
    for l in range(DEPTH):
        h = h + hybrid_mixer(h, ln_mix_g[l], w_in[l], na_rpb[l],
                             gla_gate_up_fwd[l], gla_gate_bias_fwd[l],
                             gla_gate_up_bwd[l], gla_gate_bias_bwd[l],
                             gla_norm_g[l], w_out[l])
        h = h + sqrelu_mlp(h, ln_ff_g[l], w_ff1[l], w_ff2[l])
    return rmsnorm_2(h, ln_final_g)


def setup_inputs(seed=0):
    out = dict(first_inputs(seed))
    for name, value in second_inputs(seed + 1).items():
        if name != "x":
            out[name + "_2"] = value
    return out


def reference(
    x, c, positions, w_ada, b_ada, norm1_w, w_in, conv_w, a_log, dt_bias, dn_norm_w, w_out,
    norm2_w, w_group, b_group, w_expert, b_expert, w1, w3, w2, final_norm_w, ln_mix_g_2, w_in_2,
    na_rpb_2, gla_gate_up_fwd_2, gla_gate_bias_fwd_2, gla_gate_up_bwd_2, gla_gate_bias_bwd_2,
    gla_norm_g_2, w_out_2, ln_ff_g_2, w_ff1_2, w_ff2_2, ln_final_g_2,
):
    x = first_block(
        x, c, positions, w_ada, b_ada, norm1_w, w_in, conv_w, a_log, dt_bias, dn_norm_w, w_out,
        norm2_w, w_group, b_group, w_expert, b_expert, w1, w3, w2, final_norm_w,
    )
    return second_block(
        x, ln_mix_g_2, w_in_2, na_rpb_2, gla_gate_up_fwd_2, gla_gate_bias_fwd_2,
        gla_gate_up_bwd_2, gla_gate_bias_bwd_2, gla_norm_g_2, w_out_2, ln_ff_g_2, w_ff1_2,
        w_ff2_2, ln_final_g_2,
    )


_drawn_inputs = setup_inputs


def setup_inputs(seed=0):
    import zlib

    import numpy as np

    out = dict(_drawn_inputs(seed))
    spreads = {}
    factors = {'dn_norm_w': 3.976,
     'norm2_w': 2.831,
     'b_group': 3.707,
     'b_expert': 5.624,
     'final_norm_w': 4.217,
     'ln_mix_g_2': 3.141,
     'na_rpb_2': 143.125,
     'gla_gate_bias_fwd_2': 4.309,
     'gla_gate_bias_bwd_2': 4.503,
     'gla_norm_g_2': 20.675,
     'ln_ff_g_2': 10.845,
     'ln_final_g_2': 21.625}
    for name, (base, spread) in spreads.items():
        noise = np.random.default_rng([zlib.crc32(name.encode()), seed]).standard_normal(out[name].shape)
        drawn = base * np.exp(spread * noise) if base else spread * noise
        out[name] = __import__('jax').numpy.asarray(drawn.astype(out[name].dtype))
    for name, factor in factors.items():
        out[name] = (out[name] * factor).astype(out[name].dtype)
    return out
```

```python
from contextlib import ExitStack, contextmanager

import numpy as np

import concourse.bass as bass
from concourse import mybir

F32 = mybir.dt.float32
I32 = mybir.dt.int32
U32 = mybir.dt.uint32
ALU = mybir.AluOpType
ACT = mybir.ActivationFunctionType
AX = mybir.AxisListType
ds = bass.ds

P = 128
T = 1024
D = 1024
NT = T // P
NK = D // P
BANK = 512
NEG = -1.0e30
EPS = 1e-6

RH = 4
DH = 128
RC = 128
DC = 64
GROUPS, PER_GROUP = 4, 8
NE = GROUPS * PER_GROUP
DE = D // 2
BLOCKS = 2 * T // P + NE
ROWS, W = 16, 64
KH, KW = 8, 16
NAH, NAD = 8, 64
DK, DV = 64, 128
DFF = 4 * D
NF = DFF // P
IN1 = 8 * 512 + 8
IN2 = 3 * 512 + 2 * 256 + 2 * 512 + 32

LEVELS = (1, 2, 4, 8, 16, 32)


def shape_constants():
    i = np.arange(P)
    j = i[:, None]
    same = (i[None, :] // DC) == (j // DC)
    gamma = 1.0 - 2.0 ** (-5.0 - np.arange(RH))
    c = {}
    c["ident"] = np.eye(P)
    c["ones"] = np.ones((P, P))
    c["upto"] = same & (j <= i[None, :])
    c["after"] = same & (j >= i[None, :])
    c["behind"] = same & (j > i[None, :])
    c["chunk"] = same
    c["before"] = j < i[None, :]
    for b in LEVELS:
        c[f"level{b}"] = (i[None, :] // (2 * b) == j // (2 * b)) & (i[None, :] % (2 * b) >= b) & (j % (2 * b) < b)
    c["ret_mask"] = np.concatenate([np.where(i[None, :] >= j, g ** -(j + 1.0), 0.0) * DH ** -0.5 for g in gamma], 1)
    c["ret_out"] = np.stack([g ** (i + 1.0) for g in gamma], 1)
    c["ret_key"] = np.stack([g ** (RC - 1.0 - i) * DH ** -0.5 for g in gamma], 1)
    c["halves"] = np.stack([i < DC, i >= DC], 1)
    c["half0"] = np.repeat((i < DC)[:, None], P, 1)
    c["half1"] = np.repeat((i >= DC)[:, None], P, 1)
    c["row"] = np.repeat(i[None, :], P, 0)
    c["token"] = j + P * np.arange(NT)[None, :]
    c["steps"] = np.repeat(P * np.arange(NT)[None, :], P, 0)
    c["inv_freq"] = np.repeat((np.float32(10000.0) ** (-np.arange(0, DH, 2, dtype=np.float32) / np.float32(DH)))[None, :], P, 0)
    q = i % W
    start = np.clip(q - KW // 2, 0, W - KW)[:, None]
    k = np.arange(W)[None, :]
    c["window"] = np.where((k >= start) & (k < start + KW), 0.0, NEG)
    c["qk_scale"] = np.repeat(np.array([DH ** -0.5] * RH + [1.0] * RH)[None, :], P, 0)
    return {n: np.asarray(v, np.float32).reshape(P, -1) for n, v in c.items()}


class Line:

    def __init__(self, k, name, step=1, credit=0, engine=None):
        self.k, self.step, self.count, self.engine = k, step, credit, engine
        self.sem = k.ctx.enter_context(k.nc.semaphore(name))
        self.name = name
        k.lines.append(self)

    def __call__(self, instruction):
        instruction.then_inc(self.sem, self.step)
        self.count += self.step
        loop = self.k.loop
        assert loop is None or self in loop.per, f"{self.name} is not among the loop's lines"
        return Mark(self, self.count, loop)


class Mark:

    def __init__(self, line, at, loop, ago=0):
        self.line, self.at, self.loop, self.ago = line, at, loop, ago

    def before(self, rounds):
        return Mark(self.line, self.at, self.loop, self.ago + rounds)

    def order(self):
        back = self.ago * self.loop.per[self.line] * self.line.step if self.loop else 0
        return (self.at - back) if self.loop is None or not self.loop.over else self.value()

    def value(self):
        if self.loop is None:
            return self.at
        per = self.loop.per[self.line] * self.line.step
        if self.loop.over:
            return self.at + (self.loop.n - 1) * per
        return self.loop.i * per + (self.at - self.ago * per)


class Rounds:

    def __init__(self, k, n, per):
        self.k, self.n, self.per, self.over = k, n, dict(per), False

    def __enter__(self):
        assert self.k.loop is None
        self.k.loop = self
        self.base = {line: line.count for line in self.per}
        self.fori = self.k.nc.Fori(0, self.n)
        self.i = self.fori.__enter__()
        return self

    def last(self, line, ago=1):
        return Mark(line, self.base[line] + self.per[line] * line.step, self, ago)

    def step(self, line, nth, ago=1):
        return Mark(line, self.base[line] + nth * line.step, self, ago)

    def __exit__(self, *failed):
        self.fori.__exit__(*failed)
        if failed[0] is None:
            made = {line: (line.count - self.base[line]) // line.step for line in self.per}
            assert made == self.per, "steps a round: " + ", ".join(f"{x.name} {n}" for x, n in made.items())
            for line, per in self.per.items():
                line.count = self.base[line] + self.n * per * line.step
            self.over = True
            self.k.loop = None


class Program:
    CREDIT = 256

    def __init__(self, nc, ctx, io, tap=None):
        self.nc, self.ctx, self.io, self.lines, self.loop, self.areas = nc, ctx, io, [], None, 0
        self.tap = tap
        self.v = Line(self, "vector_steps", credit=self.CREDIT, engine=nc.vector)
        self.a = Line(self, "scalar_steps", credit=self.CREDIT, engine=nc.scalar)
        self.p = Line(self, "tensor_steps", credit=self.CREDIT, engine=nc.tensor)
        self.g = Line(self, "gpsimd_steps", credit=self.CREDIT, engine=nc.gpsimd)
        self.slot = [Line(self, f"load_slot{n}", step=16, credit=self.CREDIT, engine=nc.sync) for n in range(10)]
        self.store = Line(self, "stores", step=16, credit=self.CREDIT, engine=nc.sync)
        for line in self.lines:
            line.engine.sem_inc(line.sem, self.CREDIT)
        self.soft = [Line(self, f"soft_slot{n}", step=16) for n in range(5)]
        self.passed = ctx.enter_context(nc.semaphore("waits_passed"))

    def area(self, shape, dtype=F32):
        self.areas += 1
        return self.nc.sbuf_tensor(f"area{self.areas}", list(shape), dtype)

    def wait(self, engine, *marks):
        latest = {}
        for m in marks:
            if m.line not in latest or m.order() > latest[m.line].order():
                latest[m.line] = m
        for m in latest.values():
            engine.wait_ge(m.line.sem, m.value())

    @contextmanager
    def only(self, engine, cond, line, steps, after=()):
        before = self.now(line)
        with engine.If(cond):
            yield
        assert line.count == before[0].at + steps * line.step
        with engine.Else():
            self.wait(engine, *before, *after)
            engine.sem_inc(line.sem, steps * line.step)

    def settled(self, engine):
        engine.sem_inc(self.passed, 1)

    def now(self, *lines):
        return [Mark(x, x.count, self.loop) for x in lines]

    def meet(self):
        assert self.loop is None
        for engine in (self.nc.sync, self.nc.vector, self.nc.scalar, self.nc.tensor, self.nc.gpsimd):
            for line in self.lines:
                if line.count:
                    engine.wait_ge(line.sem, line.count)

    def rounds(self, n, **per):
        return Rounds(self, n, {self.named(k): c for k, c in per.items() if c})

    def named(self, k):
        lines = {"v": self.v, "a": self.a, "p": self.p, "g": self.g, "store": self.store}
        lines.update({f"s{n}": x for n, x in enumerate(self.slot)})
        lines.update({f"q{n}": x for n, x in enumerate(self.soft)})
        return lines[k]

    def take(self, line, after, chain):
        own = self.now(line) if chain else [m for m in after if m.line is line]
        self.wait(line.engine, *own, *[m for m in after if m.line is not line])

    def V(self, instruction, *args, after=(), chain=True, **kw):
        self.take(self.v, after, chain)
        return self.v(instruction(*args, **kw))

    def A(self, out, in_, func, after=(), chain=True, **kw):
        self.take(self.a, after, chain)
        return self.a(self.nc.scalar.activation(out, in_, func, **kw))

    def G(self, instruction, *args, after=(), **kw):
        self.take(self.g, after, True)
        return self.g(instruction(*args, **kw))


def wide(ap, axis, n):
    shape = list(ap.shape)
    shape.insert(axis, n)
    return ap.unsqueeze(axis).broadcast_to(shape)


def interleave(*streams):
    streams = list(streams)
    while streams:
        streams = [x for x in streams if next(x, x) is not x]


def spread(dram, n, parts=P):
    return bass.AP(dram.tensor, dram.offset, [[0, parts], [1, n]])


def rstd(k, out, total, n, m, eps=EPS):
    v = k.nc.vector
    m = k.V(v.tensor_scalar, out, total, 1.0 / n, eps, ALU.mult, ALU.add, after=[m])
    m = k.V(v.reciprocal, out, out, after=[m])
    return k.A(out, out, ACT.Sqrt, after=[m])


def norm_transpose(k, x, xT, scale, shift, xn_dram=None):
    nc = k.nc
    with ExitStack() as c:
        sq = c.enter_context(k.area([P, D], F32))
        xn = c.enter_context(k.area([P, D], F32))
        ss = c.enter_context(k.area([P, 2], F32))
        store = 1 if xn_dram is not None else 0
        with k.rounds(NT, a=2 + NK // 2, v=3 + NK // 2, p=2, q4=store) as r:
            i = r.i
            m = k.A(sq[:, :], x[:, ds(i, 1), :].squeeze(1), ACT.Square, accum_out=ss[:, 0:1], after=[r.step(k.v, 2)])
            m = rstd(k, ss[:, 1:2], ss[:, 0:1], D, m)
            before = [r.last(k.p)] + ([r.last(k.soft[4])] if store else [])
            m = k.V(nc.vector.tensor_scalar, xn[:, :], x[:, ds(i, 1), :].squeeze(1), ss[:, 1:2], None, ALU.mult,
                    after=[m] + before)
            if store:
                k.wait(nc.gpsimd, m)
                k.soft[4](nc.gpsimd.dma_start(xn_dram[ds(i * P, P), :], xn[:, :]))
            for half in range(2):
                bank = k.bank[half]
                k.wait(nc.tensor, m, r.last(k.v), r.last(k.a))
                for q in range(4):
                    f = half * 4 + q
                    t = nc.tensor.transpose(bank[:, q * P:(q + 1) * P], xn[:, f * P:(f + 1) * P], k.c("ident"))
                t = k.p(t)
                for q in range(4):
                    f = half * 4 + q
                    dst = xT[:, f, ds(i * P, P)]
                    src = bank[:, q * P:(q + 1) * P]
                    if half == 0:
                        k.A(dst, src, ACT.Identity, scale=scale[:, f:f + 1],
                            bias=shift[:, f:f + 1] if shift is not None else 0.0, after=[t])
                    elif shift is not None:
                        k.V(nc.vector.tensor_scalar, dst, src, scale[:, f:f + 1], shift[:, f:f + 1],
                            ALU.mult, ALU.add, after=[t])
                    else:
                        k.V(nc.vector.tensor_scalar, dst, src, scale[:, f:f + 1], None, ALU.mult, after=[t])
    k.meet()


def load_columns(k, slot, wbuf, w, col, n, after=()):
    k.wait(k.nc.sync, *after)
    return k.slot[slot](k.nc.sync.dma_start(wbuf, w[:, ds(col, n)].rearrange("(k p) c -> p k c", p=P)))


def project(k, xT, w, col0, chunks, evacuate, v=0, a=0, g=0):
    nc = k.nc
    with ExitStack() as c:
        wbuf = [c.enter_context(k.area([P, NK, BANK], F32)) for _ in range(2)]

        def chunk(s, at, before, used):
            loaded = load_columns(k, s, wbuf[s][:, :, :], w, at * BANK + col0, BANK, after=used)
            for m in range(NT):
                k.wait(nc.tensor, *before(m))
                if m == 0:
                    k.wait(nc.tensor, loaded)
                for f in range(NK):
                    t = nc.tensor.matmul(k.bank[m][:, :], xT[:, f, m * P:(m + 1) * P], wbuf[s][:, f, :],
                                         start=f == 0, stop=f == NK - 1)
                evacuate(at, m, k.bank[m], k.p(t))

        if chunks % 2 == 0 and chunks > 2:
            with k.rounds(chunks // 2, p=2 * NT, v=2 * v, a=2 * a, g=2 * g, s0=1, s1=1) as r:
                chunk(0, r.i * 2, lambda m: [r.last(k.v), r.last(k.a)], [r.step(k.p, NT)])
                made = k.now(k.v, k.a)
                chunk(1, r.i * 2 + 1, lambda m: made, [r.last(k.p)])
        else:
            for n in range(chunks):
                made = k.now(k.v, k.a)
                chunk(n % 2, n, lambda m: made, k.now(k.p) if n > 1 else [])
    k.meet()


def modulation(k, mod, gates):
    nc, io = k.nc, k.io
    third = 2 * D
    with ExitStack() as c:
        acc = c.enter_context(k.area([P, 6 * D], F32))
        wa = [c.enter_context(k.area([P, third], F32)) for _ in range(6)]
        cT = c.enter_context(k.area([P, NK], F32))
        zero = k.V(nc.vector.memset, acc[:, :], 0.0)
        k.wait(nc.sync, zero)
        bias = k.slot[6](nc.sync.dma_start(acc[0:1, :], io["b_ada"]))
        cl = k.slot[7](nc.sync.dma_start(cT[:, :], io["cT"]))
        silu = k.A(cT[:, :], cT[:, :], ACT.Silu, after=[cl])
        k.wait(nc.vector, bias, silu)
        with k.rounds(NK // 2, v=6, s0=1, s1=1, s2=1, s3=1, s4=1, s5=1) as r:
            for h in range(2):
                for j in range(3):
                    s = 3 * h + j
                    k.wait(nc.sync, r.step(k.v, s + 1))
                    m = k.slot[s](nc.sync.dma_start(wa[s][:, :], io["w_ada"][ds((r.i * 2 + h) * P, P), j * third:(j + 1) * third]))
                    part = acc[:, j * third:(j + 1) * third]
                    k.V(nc.vector.scalar_tensor_tensor, part, wa[s][:, :], cT[:, ds(r.i * 2 + h, 1)], part, ALU.mult, ALU.add,
                        after=[m, r.step(k.v, s - 2, ago=0) if h else r.step(k.v, s + 4)])
        done = k.now(k.v)
        k.wait(nc.tensor, *done)
        for j in range(6 * NK):
            t = nc.tensor.matmul(k.bank[0][:, j:j + 1], acc[:, j * P:(j + 1) * P], k.c("ones")[:, 0:1], start=True, stop=True)
        t = k.p(t)
        k.V(nc.vector.tensor_copy, mod[:, :], k.bank[0][:, 0:6 * NK], after=[t])
        for n, (gate, at) in enumerate(((gates[0], 2), (gates[1], 5))):
            for h in range(2):
                b = 1 + 2 * n + h
                t = k.p(nc.tensor.matmul(k.bank[b][:, :], k.c("ones"), acc[:, at * D + h * BANK:at * D + (h + 1) * BANK],
                                         start=True, stop=True))
                k.V(nc.vector.tensor_copy, gate[:, h * BANK:(h + 1) * BANK], k.bank[b][:, :], after=[t])
    k.meet()


def rotary_tables(k, cos, sin):
    nc, io = k.nc, k.io
    v = nc.vector
    two_pi = 2.0 * np.pi
    parts, rest = [], two_pi
    for bits in (6, 17):
        parts.append(np.floor(rest * 2.0 ** bits) / 2.0 ** bits)
        rest -= parts[-1]
    parts.append(rest)
    magic = 1.5 * 2.0 ** 23
    with ExitStack() as c:
        pos = c.enter_context(k.area([P, NT], I32))
        posf = c.enter_context(k.area([P, NT], F32))
        ang = c.enter_context(k.area([P, NT, DH // 2], F32))
        cnt = c.enter_context(k.area([P, NT, DH // 2], F32))
        red = c.enter_context(k.area([P, NT, DH // 2], F32))
        m = k.slot[0](nc.sync.dma_start(pos[:, :], io["positions"]))
        m = k.V(v.tensor_copy, posf[:, :], pos[:, :], after=[m])
        m = k.V(v.tensor_tensor, ang[:, :, :], wide(posf[:, :], 2, DH // 2), wide(k.c("inv_freq"), 1, NT), ALU.mult, after=[m])
        for out, turn in ((sin, 0.0), (cos, 0.25)):
            m = k.V(v.tensor_scalar, cnt[:, :, :], ang[:, :, :], 1.0 / two_pi, turn, ALU.mult, ALU.add, after=[m])
            m = k.V(v.tensor_scalar, cnt[:, :, :], cnt[:, :, :], magic, -magic, ALU.add, ALU.add, after=[m])
            src = ang
            for part in parts:
                m = k.V(v.scalar_tensor_tensor, red[:, :, :], cnt[:, :, :], -float(part), src[:, :, :], ALU.mult, ALU.add, after=[m])
                src = red
            m = k.V(v.tensor_scalar, red[:, :, :], red[:, :, :], turn * two_pi, np.pi, ALU.add, ALU.min, after=[m])
            m = k.V(v.tensor_scalar, red[:, :, :], red[:, :, :], -np.pi, None, ALU.max, after=[m])
            m = k.A(out[:, :, :], red[:, :, :], ACT.Sin, after=[m])
    k.meet()


def heads_norm(k, o, sq, ss, weight, gate, n, m, gate_mark):
    v = k.nc.vector
    h = o.shape[1]
    m = k.V(v.tensor_tensor, sq, o, o, ALU.mult, after=[m])
    m = k.V(v.tensor_reduce, ss, sq, AX.X, ALU.add, after=[m])
    m = rstd(k, ss, ss, n, m)
    m = k.V(v.tensor_tensor, o, o, wide(ss, 2, n), ALU.mult, after=[m])
    if weight is not None:
        m = k.V(v.tensor_tensor, o, o, wide(weight, 1, h), ALU.mult, after=[m])
    return k.V(v.tensor_tensor, o, o, gate, ALU.mult, after=[m, gate_mark])


def transposes(k, bank, src, n=4, after=()):
    nc = k.nc
    k.wait(nc.tensor, *after)
    for h in range(n):
        t = nc.tensor.transpose(bank[:, h * P:(h + 1) * P], src[:, h * P:(h + 1) * P], k.c("ident"))
    return k.p(t)


def retention(k, hT, mixT, cos, sin):
    nc, io = k.nc, k.io
    v = nc.vector
    with ExitStack() as c:
        sb = lambda *s: c.enter_context(k.area(list(s), F32))
        qkvg = sb(P, NT, 4 * BANK)

        def evacuate(chunk, m, bank, mark):
            dst = qkvg[:, m, ds(chunk * BANK, BANK)]
            if m % 2:
                k.V(v.tensor_copy, dst, bank[:, :], after=[mark])
            else:
                k.A(dst, bank[:, :], ACT.Copy, after=[mark])
        project(k, hT, io["w_in"], 0, 4, evacuate, v=4, a=4)

        qk, qkT, kw, t1, sT = sb(P, 2 * BANK), sb(P, 2 * BANK), sb(P, BANK), sb(P, 2 * BANK), sb(P, BANK)
        state, o, sq, sg, ss = sb(P, BANK), sb(P, BANK), sb(P, BANK), sb(P, BANK), sb(P, RH)
        zero = k.V(v.memset, state[:, :], 0.0)
        k.wait(nc.tensor, zero)
        k.wait(nc.gpsimd, zero)
        gamma = [1.0 - 2.0 ** (-5.0 - h) for h in range(RH)]
        with k.rounds(NT, v=17, a=5, g=3, p=5) as r:
            i = r.i
            row = qkvg[:, ds(i, 1), :].squeeze(1)
            x = row[:, 0:2 * BANK].rearrange("p (h t d) -> p h t d", h=2 * RH, t=2)
            x1, x2 = x[:, :, 0, :], x[:, :, 1, :]
            y = qk[:, :].rearrange("p (h t d) -> p h t d", h=2 * RH, t=2)
            t4 = t1[:, :].rearrange("p (t h d) -> p t h d", t=2, h=2 * RH)
            co = wide(cos[:, ds(i, 1), :].squeeze(1), 1, 2 * RH)
            si = wide(sin[:, ds(i, 1), :].squeeze(1), 1, 2 * RH)
            m1 = k.V(v.tensor_tensor, t4[:, 0], x2, si, ALU.mult)
            m = k.V(v.tensor_tensor, y[:, :, 0, :], x1, co, ALU.mult, after=[r.last(k.p)])
            first = k.V(v.tensor_tensor, y[:, :, 0, :], y[:, :, 0, :], t4[:, 0], ALU.subtract, after=[m, m1])
            m1 = k.G(nc.gpsimd.tensor_tensor, t4[:, 1], x1, si, ALU.mult)
            m = k.G(nc.gpsimd.tensor_tensor, y[:, :, 1, :], x2, co, ALU.mult, after=[r.last(k.p), r.last(k.v)])
            second = k.G(nc.gpsimd.tensor_tensor, y[:, :, 1, :], y[:, :, 1, :], t4[:, 1], ALU.add, after=[m, m1])
            kwm = k.V(v.tensor_tensor, kw[:, :].rearrange("p (h d) -> p h d", h=RH),
                      qk[:, BANK:].rearrange("p (h d) -> p h d", h=RH), wide(k.c("ret_key"), 2, DH), ALU.mult, after=[first, second])
            ta = transposes(k, k.bank[0], qk[:, 0:BANK], after=[first, second, r.last(k.v), r.last(k.a)])
            tb = transposes(k, k.bank[1], qk[:, BANK:])
            ea = k.A(qkT[:, 0:BANK], k.bank[0][:, :], ACT.Copy, after=[ta])
            eb = k.V(v.tensor_copy, qkT[:, BANK:], k.bank[1][:, :], after=[tb])
            k.wait(nc.tensor, ea, eb)
            for h in range(RH):
                s = slice(h * P, (h + 1) * P)
                t = nc.tensor.matmul(k.bank[2][:, s], qkT[:, BANK + h * P:BANK + (h + 1) * P], qkT[:, s], start=True, stop=True)
            t = k.p(t)
            ms = k.V(v.tensor_tensor, sT[:, :], k.bank[2][:, :], k.c("ret_mask"), ALU.mult, after=[t])
            k.wait(nc.tensor, ms, kwm)
            for h in range(RH):
                s = slice(h * P, (h + 1) * P)
                val = qkvg[:, ds(i, 1), 2 * BANK + h * P:2 * BANK + (h + 1) * P].squeeze(1)
                nc.tensor.matmul(k.bank[3][:, s], sT[:, s], val, start=True, stop=False)
                nc.tensor.matmul(k.bank[3][:, s], qkT[:, s], state[:, s], start=False, stop=True)
                t = nc.tensor.matmul(k.bank[4][:, s], kw[:, s], val, start=True, stop=True)
            t = k.p(t)
            for h in range(RH):
                s = slice(h * P, (h + 1) * P)
                k.V(v.scalar_tensor_tensor, state[:, s], state[:, s], float(gamma[h] ** RC), k.bank[4][:, s], ALU.mult, ALU.add,
                    after=[t] if h == 0 else [])
            o3 = o[:, :].rearrange("p (h d) -> p h d", h=RH)
            m = k.V(v.tensor_tensor, o3, k.bank[3][:, :].rearrange("p (h d) -> p h d", h=RH), wide(k.c("ret_out"), 2, DH), ALU.mult)
            gm = k.A(sg[:, :], row[:, 3 * BANK:], ACT.Silu, after=[r.last(k.v)])
            m = heads_norm(k, o3, sq[:, :].rearrange("p (h d) -> p h d", h=RH), ss[:, :], None,
                           sg[:, :].rearrange("p (h d) -> p h d", h=RH), DH, m, gm)
            t = transposes(k, k.bank[5], o[:, :], after=[m])
            k.A(mixT[:, 0:2, ds(i * P, P)], k.bank[5][:, 0:2 * P].rearrange("p (h t) -> p h t", h=2), ACT.Copy, after=[t])
            k.A(mixT[:, 2:4, ds(i * P, P)], k.bank[5][:, 2 * P:].rearrange("p (h t) -> p h t", h=2), ACT.Copy)
    k.meet()


def channels(k, xT, w, col0, n_chunks, use, bank0=0, **per):
    nc = k.nc
    with ExitStack() as c:
        wbuf = [c.enter_context(k.area([P, NK, P], F32)) for _ in range(2)]
        with k.rounds(n_chunks // 2, s0=1, s1=1, **per) as r:
            for s in range(2):
                loaded = load_columns(k, s, wbuf[s][:, :, :], w, r.i * 2 * P + (col0 + s * P), P, after=[r.last(k.p)])
                k.wait(nc.tensor, loaded, r.last(k.v), r.last(k.a))
                banks = [k.bank[bank0 + 2 * s], k.bank[bank0 + 2 * s + 1]]
                for h in range(2):
                    for f in range(NK):
                        t = nc.tensor.matmul(banks[h][:, :], wbuf[s][:, f, :], xT[:, f, h * BANK:(h + 1) * BANK],
                                             start=f == 0, stop=f == NK - 1)
                use(r, r.i * 2 + s, s, banks, k.p(t))


def delta(k, hT, mixT):
    nc, io = k.nc, k.io
    v, g = nc.vector, nc.gpsimd
    hd = lambda ap: ap.rearrange("p (h d) -> p h d", d=DH)
    with ExitStack() as c:
        sb = lambda *s: c.enter_context(k.area(list(s), F32))
        dtok = sb(P, NT, 3 * BANK)
        z = sb(P, NT, BANK)
        ab = sb(P, NT, 2 * RH)

        def keep_z(chunk, m, bank, mark):
            k.A(z[:, m, :], bank[:, :], ACT.Silu, after=[mark])
        project(k, hT, io["w_in"], 7 * BANK, 1, keep_z, a=NT)

        with ExitStack() as c2:
            tail = c2.enter_context(k.area([P, NK, 2 * RH], F32))
            loaded = load_columns(k, 0, tail[:, :, :], io["w_in"], 8 * BANK, 2 * RH)
            k.wait(nc.tensor, loaded)
            for m in range(NT):
                for f in range(NK):
                    t = nc.tensor.matmul(k.bank[0][:, m * 8:m * 8 + 8], hT[:, f, m * P:(m + 1) * P], tail[:, f, :],
                                         start=f == 0, stop=f == NK - 1)
            t = k.p(t)
            k.V(v.tensor_copy, ab[:, :, :], k.bank[0][:, 0:NT * 8].rearrange("p (m e) -> p m e", m=NT), after=[t])
            k.meet()

        with ExitStack() as c2:
            sb2 = lambda *s: c2.enter_context(k.area(list(s), F32))
            cw = sb2(P, 12, 4)
            raw = [sb2(P, T + 3) for _ in range(2)]
            conv = [sb2(P, T) for _ in range(2)]
            m = k.slot[2](nc.sync.dma_start(cw[:, :, :], io["conv"]))
            for s in range(2):
                k.V(v.memset, raw[s][:, 0:3], 0.0, after=[m])
            k.wait(nc.scalar, *k.now(k.v))

            def use(r, j, s, banks, mark):
                m = k.A(raw[s][:, 3:3 + BANK], banks[0][:, :], ACT.Copy, after=[mark, r.last(k.v)])
                m = k.A(raw[s][:, 3 + BANK:], banks[1][:, :], ACT.Copy)
                w4 = cw[:, ds(j, 1), :].squeeze(1)
                m = k.V(v.tensor_scalar, conv[s][:, :], raw[s][:, 0:T], w4[:, 0:1], None, ALU.mult, after=[m, r.last(k.p)])
                for tap in range(1, 4):
                    m = k.V(v.scalar_tensor_tensor, conv[s][:, :], raw[s][:, tap:tap + T], w4[:, tap:tap + 1], conv[s][:, :],
                            ALU.mult, ALU.add, after=[m])
                m = k.A(conv[s][:, :], conv[s][:, :], ACT.Silu, after=[m])
                for h in range(2):
                    t = transposes(k, k.bank[4 + 2 * s + h], conv[s][:, h * BANK:(h + 1) * BANK], after=[m])
                    dst = dtok[:, 4 * h:4 * h + 4, ds(j * P, P)]
                    src = k.bank[4 + 2 * s + h][:, :].rearrange("p (m d) -> p m d", d=P)
                    if h:
                        k.V(v.tensor_copy, dst, src, after=[t])
                    else:
                        k.A(dst, src, ACT.Copy, after=[t])
            channels(k, hT, io["w_in"], 4 * BANK, 12, use, p=6, v=10, a=8)
            k.meet()

        beta, gl, gcum, egc, etail = (sb(P, NT, RH) for _ in range(5))
        gtot = sb(P, 2, NT, RH)
        u = [sb(P, NT, RH) for _ in range(3)]
        alog, dtb, dnw = sb(P, RH), sb(P, RH), sb(P, DH)
        k.slot[0](nc.sync.dma_start(alog[:, :], spread(io["a_log"], RH)))
        k.slot[0](nc.sync.dma_start(dtb[:, :], spread(io["dt_bias"], RH)))
        m = k.slot[0](nc.sync.dma_start(dnw[:, :], spread(io["dn_norm_w"], DH)))
        mb = k.A(beta[:, :, :], ab[:, :, RH:], ACT.Sigmoid, after=k.now(k.v))
        mx = k.V(v.tensor_tensor, u[0][:, :, :], ab[:, :, 0:RH], wide(dtb[:, :], 1, NT), ALU.add, after=[m])
        me = k.A(alog[:, :], alog[:, :], ACT.Exp, after=[m])
        m = k.A(u[1][:, :, :], u[0][:, :, :], ACT.Abs, after=[mx])
        m = k.A(u[1][:, :, :], u[1][:, :, :], ACT.Exp, scale=-1.0, after=[m])
        m = k.A(u[1][:, :, :], u[1][:, :, :], ACT.Ln, bias=1.0, after=[m])
        m = k.V(v.scalar_tensor_tensor, u[0][:, :, :], u[0][:, :, :], 0.0, u[1][:, :, :], ALU.max, ALU.add, after=[m])
        m = k.V(v.scalar_tensor_tensor, gl[:, :, :], u[0][:, :, :], -1.0, wide(alog[:, :], 1, NT), ALU.mult, ALU.mult, after=[m, me])
        k.wait(nc.tensor, m)
        glf = gl[:, :, :].rearrange("p m h -> p (m h)")
        for n, table in enumerate(("upto", "chunk", "half0", "half1")):
            t = nc.tensor.matmul(k.bank[0][:, n * 32:n * 32 + 32], k.c(table), glf, start=True, stop=True)
        t = k.p(t)
        part = lambda n: k.bank[0][:, n * 32:n * 32 + 32].rearrange("p (m h) -> p m h", h=RH)
        m = k.V(v.tensor_copy, gcum[:, :, :], part(0), after=[t])
        k.A(egc[:, :, :], gcum[:, :, :], ACT.Exp, after=[m])
        m = k.V(v.tensor_tensor, u[2][:, :, :], part(1), gcum[:, :, :], ALU.subtract, after=[m])
        k.A(etail[:, :, :], u[2][:, :, :], ACT.Exp, after=[m])
        k.A(gtot[:, 0], part(2), ACT.Exp)
        k.A(gtot[:, 1], part(3), ACT.Exp)

        qk, t1 = sb(P, 2 * BANK), sb(P, 2 * BANK)
        kb, kbg, vb, kt, gb = (sb(P, BANK) for _ in range(5))
        qT, kT, kbT, qgT, eg, dec, B, at = (sb(P, BANK) for _ in range(8))
        BM, U, X, Y, nw, vn = (sb(P, BANK) for _ in range(6))
        state, o, sq, ss, ss8 = sb(P, BANK), sb(P, BANK), sb(P, BANK), sb(P, RH), sb(P, 2 * RH)
        k.V(v.memset, state[:, :], 0.0)
        k.meet()
        col = lambda ap, i: ap[:, ds(i, 1), :].squeeze(1)
        with k.rounds(NT, v=44, a=18, g=5, p=24) as r:
            i = r.i
            row = dtok[:, ds(i, 1), :].squeeze(1)
            bi, gi = col(beta, i), col(gcum, i)
            m = k.A(t1[:, :], row[:, 0:2 * BANK], ACT.Square, after=[r.last(k.v)])
            m = k.V(v.tensor_reduce, ss8[:, :], hd(t1[:, :]), AX.X, ALU.add, after=[m])
            m = rstd(k, ss8[:, :], ss8[:, :], 1, m)
            m = k.V(v.tensor_tensor, ss8[:, :], ss8[:, :], k.c("qk_scale"), ALU.mult, after=[m])
            mq = k.V(v.tensor_tensor, hd(qk[:, :]), hd(row[:, 0:2 * BANK]), wide(ss8[:, :], 2, DH), ALU.mult,
                     after=[m, r.last(k.p), r.last(k.g)])
            mkb = k.V(v.tensor_tensor, hd(kb[:, :]), hd(qk[:, BANK:]), wide(bi, 2, DH), ALU.mult, after=[mq])
            mg = k.G(g.tensor_tensor, hd(gb[:, :]), wide(k.c("ones"), 1, RH), wide(col(gl, i), 2, P), ALU.mult, after=[r.last(k.p)])
            mvb = k.G(g.tensor_tensor, hd(vb[:, :]), hd(row[:, 2 * BANK:]), wide(bi, 2, DH), ALU.mult)
            mkt = k.G(g.tensor_tensor, hd(kt[:, :]), hd(qk[:, BANK:]), wide(col(etail, i), 2, DH), ALU.mult, after=[mq])
            mkg = k.G(g.tensor_tensor, hd(kbg[:, :]), hd(kb[:, :]), wide(col(egc, i), 2, DH), ALU.mult, after=[mkb])
            k.wait(nc.tensor, mg, r.last(k.v), r.last(k.a))
            for h in range(RH):
                t = nc.tensor.matmul(k.bank[3][:, h * P:(h + 1) * P], gb[:, h * P:(h + 1) * P], k.c("upto"), start=True, stop=True)
            t = k.p(t)
            me = k.A(eg[:, :], k.bank[3][:, :], ACT.Exp, after=[t, mq])
            m = k.V(v.tensor_tensor, hd(dec[:, :]), hd(k.bank[3][:, :]), wide(gi, 2, P), ALU.subtract, after=[t, me])
            m = k.V(v.tensor_scalar, dec[:, :], dec[:, :], 0.0, None, ALU.min, after=[m])
            m = k.A(dec[:, :], dec[:, :], ACT.Exp, after=[m])
            md = k.G(g.tensor_tensor, hd(dec[:, :]), hd(dec[:, :]), wide(k.c("upto"), 1, RH), ALU.mult, after=[m])
            ta = transposes(k, k.bank[0], qk[:, 0:BANK], after=[mq])
            tb = transposes(k, k.bank[1], qk[:, BANK:])
            tc = transposes(k, k.bank[2], kb[:, :], after=[mkb])
            ea = k.A(qT[:, :], k.bank[0][:, :], ACT.Copy, after=[ta])
            eb = k.A(kT[:, :], k.bank[1][:, :], ACT.Copy, after=[tb])
            ec = k.A(kbT[:, :], k.bank[2][:, :], ACT.Copy, after=[tc])
            mqg = k.V(v.tensor_tensor, qgT[:, :], k.bank[0][:, :], eg[:, :], ALU.mult, after=[ta, me, ea])
            k.wait(nc.tensor, ea, eb, ec)
            for h in range(RH):
                s = slice(h * P, (h + 1) * P)
                nc.tensor.matmul(k.bank[4][:, s], kT[:, s], kbT[:, s], start=True, stop=True)
                t = nc.tensor.matmul(k.bank[5][:, s], kT[:, s], qT[:, s], start=True, stop=True)
            t = k.p(t)
            mB = k.V(v.tensor_tensor, B[:, :], k.bank[4][:, :], dec[:, :], ALU.mult, after=[t, md])
            mat = k.V(v.tensor_tensor, at[:, :], k.bank[5][:, :], dec[:, :], ALU.mult)
            mm = k.V(v.tensor_tensor, hd(BM[:, :]), hd(B[:, :]), wide(k.c("level1"), 1, RH), ALU.mult, after=[mB])
            mu = k.V(v.scalar_tensor_tensor, hd(U[:, :]), hd(BM[:, :]), -1.0, wide(k.c("ident"), 1, RH), ALU.mult, ALU.add, after=[mm])
            t = transposes(k, k.bank[6], BM[:, :], after=[mm])
            mx = k.V(v.scalar_tensor_tensor, hd(X[:, :]), hd(k.bank[6][:, :]), -1.0, wide(k.c("ident"), 1, RH), ALU.mult, ALU.add, after=[t])
            for b in LEVELS[1:]:
                last = b == LEVELS[-1]
                mm = k.V(v.tensor_tensor, hd(BM[:, :]), hd(B[:, :]), wide(k.c(f"level{b}"), 1, RH), ALU.mult)
                k.wait(nc.tensor, mm, mx, mu)
                for h in range(RH):
                    s = slice(h * P, (h + 1) * P)
                    t = nc.tensor.matmul(k.bank[7][:, s], BM[:, s], X[:, s], start=True, stop=True)
                t = k.p(t)
                my = k.A(Y[:, :], k.bank[7][:, :], ACT.Copy, after=[t])
                k.wait(nc.tensor, my)
                for h in range(RH):
                    s = slice(h * P, (h + 1) * P)
                    if not last:
                        nc.tensor.matmul(k.bank[6][:, s], U[:, s], Y[:, s], start=True, stop=True)
                    t = nc.tensor.matmul(k.bank[3][:, s], Y[:, s], U[:, s], start=True, stop=True)
                t = k.p(t)
                mu = k.V(v.tensor_tensor, U[:, :], U[:, :], k.bank[3][:, :], ALU.subtract, after=[t])
                if not last:
                    mx = k.V(v.tensor_tensor, X[:, :], X[:, :], k.bank[6][:, :], ALU.subtract)
            k.wait(nc.tensor, mu, mkg, mvb, mkt)
            for h in range(RH):
                s = slice(h * P, (h + 1) * P)
                t = nc.tensor.matmul(k.bank[7][:, s], kbg[:, s], U[:, s], start=True, stop=True)
            t = k.p(t)
            mw = k.A(nw[:, :], k.bank[7][:, :], ACT.Copy, scale=-1.0, after=[t])
            k.wait(nc.tensor, mw, mqg, mat)
            for q in range(2):
                rows = slice(q * DC, (q + 1) * DC)
                for h in range(RH):
                    s = slice(h * P, (h + 1) * P)
                    cs = slice(h * P + q * DC, h * P + (q + 1) * DC)
                    nc.tensor.matmul(k.bank[0][rows, s], U[:, cs], vb[:, s], start=True, stop=False)
                    t = nc.tensor.matmul(k.bank[0][rows, s], nw[:, cs], state[:, s], start=False, stop=True)
                t = k.p(t)
                mv = k.A(vn[rows, :], k.bank[0][rows, :], ACT.Copy, after=[t])
                k.wait(nc.tensor, mv)
                for h in range(RH):
                    s = slice(h * P, (h + 1) * P)
                    cs = slice(h * P + q * DC, h * P + (q + 1) * DC)
                    t = nc.tensor.matmul(k.bank[1 + q][:, s], kt[rows, s], vn[rows, s], start=True, stop=True)
                t = k.p(t)
                for h in range(RH):
                    s = slice(h * P, (h + 1) * P)
                    cs = slice(h * P + q * DC, h * P + (q + 1) * DC)
                    nc.tensor.matmul(k.bank[4][rows, s], qgT[:, cs], state[:, s], start=True, stop=False)
                    to = nc.tensor.matmul(k.bank[4][rows, s], at[rows, cs], vn[rows, s], start=False, stop=True)
                to = k.p(to)
                for h in range(RH):
                    s = slice(h * P, (h + 1) * P)
                    ms = k.V(v.scalar_tensor_tensor, state[:, s], state[:, s], gtot[:, q, ds(i, 1), h:h + 1].squeeze(1),
                             k.bank[1 + q][:, s], ALU.mult, ALU.add, after=[t, to] if h == 0 else [])
                k.wait(nc.tensor, ms)
            m = k.V(v.tensor_copy, o[:, :], k.bank[4][:, :], after=[to])
            m = heads_norm(k, hd(o[:, :]), hd(sq[:, :]), ss[:, :], dnw[:, :], hd(col(z, i)), DH, m, to)
            t = transposes(k, k.bank[5], o[:, :], after=[m])
            k.A(mixT[:, 4:6, ds(i * P, P)], k.bank[5][:, 0:2 * P].rearrange("p (h t) -> p h t", h=2), ACT.Copy, after=[t])
            k.A(mixT[:, 6:8, ds(i * P, P)], k.bank[5][:, 2 * P:].rearrange("p (h t) -> p h t", h=2), ACT.Copy)
    k.meet()


def residual(k, mixT, w, x, gate):
    nc = k.nc
    with ExitStack() as c:
        tmp = [c.enter_context(k.area([P, BANK], F32)) for _ in range(2)]

        pending = {0: [], 1: []}

        def add(chunk, m, bank, mark):
            dst = x[:, m, chunk * BANK:(chunk + 1) * BANK]
            if gate is None:
                k.V(nc.vector.tensor_tensor, dst, dst, bank[:, :], ALU.add, after=[mark])
                return
            t = tmp[m % 2]
            a = k.V(nc.vector.tensor_tensor, t[:, :], bank[:, :], gate[:, chunk * BANK:(chunk + 1) * BANK], ALU.mult,
                    after=[mark] + pending[m % 2])
            pending[m % 2] = [k.G(nc.gpsimd.tensor_tensor, dst, dst, t[:, :], ALU.add, after=[a])]
        project(k, mixT, w, 0, 2, add)


def route(k, h2T, gates, where, tokens, experts):
    nc, io = k.nc, k.io
    v = nc.vector
    NL = GROUPS + NE
    with ExitStack() as c:
        sb = lambda *s, dt=F32: c.enter_context(k.area(list(s), dt))
        wr, br = sb(P, NK, NL), sb(P, NL)
        lg, eq = sb(P, NT, NL), sb(P, NT, NE)
        gp, top, ix, ixf = sb(P, NT, 8), sb(P, NT, 8), sb(P, NT, 8, dt=U32), sb(P, NT, 8)
        sel = sb(P, NT, PER_GROUP)
        hot = sb(P, 2, NT, NE)
        both = sb(P, NT, NE)
        a1, a2, a3 = sb(P, NT), sb(P, NT), sb(P, NT)
        k.slot[0](nc.sync.dma_start(wr[:, :, 0:GROUPS], io["w_group"].rearrange("(k p) c -> p k c", p=P)))
        k.slot[0](nc.sync.dma_start(wr[:, :, GROUPS:], io["w_expert"].rearrange("(k p) c -> p k c", p=P)))
        k.slot[0](nc.sync.dma_start(br[:, 0:GROUPS], spread(io["b_group"], GROUPS)))
        loaded = k.slot[0](nc.sync.dma_start(br[:, GROUPS:], spread(io["b_expert"], NE)))
        k.wait(nc.tensor, loaded)
        for m in range(NT):
            for f in range(NK):
                t = nc.tensor.matmul(k.bank[0][:, m * NL:(m + 1) * NL], h2T[:, f, m * P:(m + 1) * P], wr[:, f, :],
                                     start=f == 0, stop=f == NK - 1)
        t = k.p(t)
        m = k.V(v.tensor_tensor, lg[:, :, :], k.bank[0][:, 0:NT * NL].rearrange("p (m e) -> p m e", m=NT),
                wide(br[:, :], 1, NT), ALU.add, after=[t, loaded])
        m1 = k.V(v.memset, gp[:, :, :], NEG)
        m = k.V(v.tensor_copy, gp[:, :, 0:GROUPS], lg[:, :, 0:GROUPS], after=[m, m1])
        for n in range(NT):
            mt = k.V(v.max, top[:, n, :], gp[:, n, :], after=[m])
            mi = k.V(v.max_index, ix[:, n, :], top[:, n, :], gp[:, n, :], after=[mt])
        m = k.V(v.tensor_copy, ixf[:, :, 0:1], ix[:, :, 0:1], after=[mi])
        m2 = k.V(v.tensor_tensor, gp[:, :, 0:GROUPS], gp[:, :, 0:GROUPS], top[:, :, 0:1].broadcast_to([P, NT, GROUPS]), ALU.subtract, after=[mi])
        m2 = k.A(gp[:, :, 0:GROUPS], gp[:, :, 0:GROUPS], ACT.Exp, after=[m2])
        mz = k.V(v.tensor_reduce, a1[:, :], gp[:, :, 0:GROUPS], AX.X, ALU.add, after=[m2])
        me = k.V(v.tensor_tensor, eq[:, :, 0:GROUPS], wide(k.c("row")[:, 0:GROUPS], 1, NT), ixf[:, :, 0:1].broadcast_to([P, NT, GROUPS]), ALU.is_equal, after=[m])
        for n in range(GROUPS):
            src = lg[:, :, GROUPS + n * PER_GROUP:GROUPS + (n + 1) * PER_GROUP]
            pick = eq[:, :, n:n + 1].broadcast_to([P, NT, PER_GROUP])
            if n == 0:
                ms = k.V(v.tensor_tensor, sel[:, :, :], src, pick, ALU.mult, after=[me])
            else:
                mp = k.V(v.tensor_tensor, both[:, :, 0:PER_GROUP], src, pick, ALU.mult, after=[ms])
                ms = k.V(v.tensor_tensor, sel[:, :, :], sel[:, :, :], both[:, :, 0:PER_GROUP], ALU.add, after=[mp])
        base = k.V(v.tensor_scalar, a2[:, :], ixf[:, :, 0:1].squeeze(2), float(PER_GROUP), None, ALU.mult, after=[ms])
        for n in range(NT):
            mt = k.V(v.max, top[:, n, :], sel[:, n, :], after=[ms, base])
            mi = k.V(v.max_index, ix[:, n, :], top[:, n, :], sel[:, n, :], after=[mt])
        m = k.V(v.tensor_copy, ixf[:, :, 0:2], ix[:, :, 0:2], after=[mi])
        m = k.V(v.tensor_tensor, ixf[:, :, 0:2], ixf[:, :, 0:2], wide(a2[:, :], 2, 2), ALU.add, after=[m])
        md = k.V(v.tensor_tensor, a2[:, :], top[:, :, 1:2].squeeze(2), top[:, :, 0:1].squeeze(2), ALU.subtract, after=[m])
        md = k.A(a2[:, :], a2[:, :], ACT.Exp, after=[md])
        ms = k.V(v.scalar_tensor_tensor, a3[:, :], a2[:, :], 1.0, a1[:, :], ALU.add, ALU.mult, after=[md, mz])
        ms = k.V(v.reciprocal, gates[:, :, 0:1].squeeze(2), a3[:, :], after=[ms])
        k.V(v.tensor_tensor, gates[:, :, 1:2].squeeze(2), gates[:, :, 0:1].squeeze(2), a2[:, :], ALU.mult, after=[ms])
        for j in range(2):
            mh = k.V(v.tensor_tensor, hot[:, j], wide(k.c("row")[:, 0:NE], 1, NT), ixf[:, :, j:j + 1].broadcast_to([P, NT, NE]), ALU.is_equal, after=[m])
        m = k.V(v.tensor_tensor, both[:, :, :], hot[:, 0], hot[:, 1], ALU.add, after=[mh])
        k.wait(nc.tensor, m)
        for n in range(NT):
            for q in range(n + 1):
                t = nc.tensor.matmul(k.bank[1][:, n * NE:(n + 1) * NE], k.c("before" if q == n else "ones"), both[:, q, :],
                                     start=q == 0, stop=q == n)
        for q in range(NT):
            t = nc.tensor.matmul(k.bank[2][:, 0:NE], k.c("ones"), both[:, q, :], start=q == 0, stop=q == NT - 1)
        t = k.p(t)
        cnt, full = sb(P, NE, NT), sb(P, NE)
        upto = [sb(P, NE + 16) for _ in range(2)]
        first = sb(P, NE)
        m = k.V(v.tensor_tensor, cnt[:, :, :], k.bank[2][:, 0:NE].unsqueeze(2).broadcast_to([P, NE, NT]), wide(k.c("steps"), 1, NE), ALU.is_gt, after=[t])
        m = k.V(v.tensor_reduce, full[:, :], cnt[:, :, :], AX.X, ALU.add, after=[m])
        m = k.V(v.memset, upto[0][:, 0:16], 0.0)
        m = k.V(v.memset, upto[1][:, 0:16], 0.0)
        m = k.V(v.tensor_copy, upto[0][:, 16:], full[:, :], after=[m])
        for n, d in enumerate((1, 2, 4, 8, 16)):
            src, dst = upto[n % 2], upto[(n + 1) % 2]
            m = k.V(v.tensor_tensor, dst[:, 16:], src[:, 16:], src[:, 16 - d:16 - d + NE], ALU.add, after=[m])
        total = dst[:, 16:]
        m = k.V(v.tensor_tensor, first[:, :], total, full[:, :], ALU.subtract, after=[m])
        blk = sb(P, BLOCKS, NE)
        ef = sb(P, BLOCKS)
        m1 = k.V(v.tensor_tensor, blk[:, :, :], wide(total, 1, BLOCKS), k.c("row")[:, 0:BLOCKS].unsqueeze(2).broadcast_to([P, BLOCKS, NE]), ALU.is_le, after=[m])
        m1 = k.V(v.tensor_reduce, ef[:, :], blk[:, :, :], AX.X, ALU.add, after=[m1])
        m1 = k.V(v.tensor_scalar, ef[:, :], ef[:, :], float(NE - 1), None, ALU.min, after=[m1])
        k.V(v.tensor_copy, experts[:, 0:BLOCKS], ef[:, :], after=[m1])
        k.V(v.tensor_copy, experts[:, BLOCKS:], total[:, NE - 1:NE])
        rank, div, w2 = sb(P, NT), sb(P, NT), sb(P, NT, NE)
        row_of, blk_of = sb(P, NT, 2), sb(P, NT, 2)
        hp, hb = [sb(P, P) for _ in range(2)], [sb(P, BLOCKS) for _ in range(2)]
        pos = sb(P, NT, 2)
        ranks = k.bank[1][:, 0:NT * NE].rearrange("p (m e) -> p m e", m=NT)
        for j in range(2):
            m = k.V(v.tensor_tensor, w2[:, :, :], ranks, hot[:, j], ALU.mult, after=[m])
            mr = k.V(v.tensor_reduce, rank[:, :], w2[:, :, :], AX.X, ALU.add, after=[m])
            m = k.V(v.tensor_tensor, w2[:, :, :], wide(first[:, :], 1, NT), hot[:, j], ALU.mult, after=[mr])
            m = k.V(v.tensor_reduce, a1[:, :], w2[:, :, :], AX.X, ALU.add, after=[m])
            m = k.V(v.tensor_tensor, w2[:, :, 0:NT - 1], wide(rank[:, :], 2, NT - 1), wide(k.c("steps")[:, 1:NT], 1, NT), ALU.is_ge, after=[m])
            m = k.V(v.tensor_reduce, div[:, :], w2[:, :, 0:NT - 1], AX.X, ALU.add, after=[m])
            m = k.V(v.scalar_tensor_tensor, row_of[:, :, j:j + 1].squeeze(2), div[:, :], -float(P), rank[:, :], ALU.mult, ALU.add, after=[m])
            m = k.V(v.tensor_tensor, blk_of[:, :, j:j + 1].squeeze(2), div[:, :], a1[:, :], ALU.add, after=[m])
        m = k.V(v.scalar_tensor_tensor, pos[:, :, :], blk_of[:, :, :], float(P), row_of[:, :, :], ALU.mult, ALU.add, after=[m])
        k.V(v.tensor_copy, where[:, :, :], pos[:, :, :], after=[m])
        t = None
        for n in range(NT):
            for j in range(2):
                free = [t] if t is not None else []
                m1 = k.V(v.tensor_scalar, hp[j][:, :], k.c("row"), row_of[:, n, j:j + 1], None, ALU.is_equal, after=[m] + free)
                m2 = k.V(v.tensor_scalar, hb[j][:, :], k.c("row")[:, 0:BLOCKS], blk_of[:, n, j:j + 1], k.c("token")[:, n:n + 1],
                         ALU.is_equal, ALU.mult)
                k.wait(nc.tensor, m1, m2)
                t = k.p(nc.tensor.matmul(k.bank[3][:, 0:BLOCKS], hp[j][:, :], hb[j][:, :], start=n + j == 0, stop=n + j == NT))
        k.V(v.tensor_copy, tokens[:, 0:BLOCKS], k.bank[3][:, 0:BLOCKS], after=[t])
        k.V(v.memset, tokens[:, BLOCKS:], 0)
    k.meet()


def experts_pass(k, scale, shift, tokens, experts, xn, ys):
    nc, io = k.nc, k.io
    v, pe, sy, gp = nc.vector, nc.tensor, nc.sync, nc.gpsimd
    with ExitStack() as c:
        sb = lambda *s, dt=F32: c.enter_context(k.area(list(s), dt))
        w1 = [sb(P, NK, DE) for _ in range(2)]
        w3 = [sb(P, NK, DE) for _ in range(2)]
        w2 = [sb(P, DE // P, D) for _ in range(2)]
        rows = [sb(P, D) for _ in range(2)]
        idx = [sb(P, 1, dt=U32) for _ in range(2)]
        xsT = [sb(P, NK, P) for _ in range(2)]
        act, hid, hidT = (sb(P, DE) for _ in range(3))
        y = [sb(P, D) for _ in range(2)]

        PE_STEPS, ACT_STEPS, VEC_STEPS = 6, 7, 6

        def gather(at, s, after):
            m = k.G(gp.tensor_copy, idx[s][:, :], tokens[:, ds(at, 1)], after=after)
            k.wait(gp, m)
            k.settled(gp)
            return k.soft[s](gp.indirect_dma_start(out=rows[s][:, :], out_offset=None, in_=xn[:, :],
                                                   in_offset=bass.IndirectOffsetOnAxis(ap=idx[s][:, 0:1], axis=0)))

        def turn(s, half):
            return transposes(k, k.bank[half], rows[s][:, half * BANK:(half + 1) * BANK])

        def rows_out(s, half, t, before):
            for q in range(4):
                f = half * 4 + q
                src = k.bank[half][:, q * P:(q + 1) * P]
                if half:
                    m = k.V(v.tensor_scalar, xsT[s][:, f, :], src, scale[:, f:f + 1], shift[:, f:f + 1], ALU.mult, ALU.add,
                            after=[t] + before)
                else:
                    m = k.A(xsT[s][:, f, :], src, ACT.Identity, scale=scale[:, f:f + 1], bias=shift[:, f:f + 1], after=[t] + before)
            return m

        used_t = pe.value_load(experts[0:1, BLOCKS:BLOCKS + 1], min_val=0, max_val=BLOCKS)
        used_s = sy.value_load(experts[0:1, BLOCKS:BLOCKS + 1], min_val=0, max_val=BLOCKS)
        got = gather(0, 0, [])
        k.wait(pe, got)
        for half in range(2):
            rows_out(0, half, turn(0, half), [])
        k.wait(pe, *k.now(k.v, k.a))
        k.wait(gp, *k.now(k.p))
        with k.rounds(BLOCKS // 2, s0=2, s1=2, s2=1, s3=1, s4=1, s5=1, q0=1, q1=1, g=2,
                      v=2 * VEC_STEPS, a=2 * ACT_STEPS, p=2 * PE_STEPS) as r:
            for s in range(2):
                at = r.i * 2 + s
                n = 1 - s
                there = used_s > at
                e = sy.value_load(experts[0:1, ds(at, 1)], min_val=0, max_val=NE - 1)
                for m in (r.step(k.p, PE_STEPS * s + 2), *k.now(k.slot[s], k.slot[2 + s])):
                    k.wait(sy, m)
                    k.settled(sy)
                k.slot[s](sy.dma_start(w1[s][:, :, :], io["w1"][ds(e, 1)].squeeze(0).rearrange("(k p) f -> p k f", p=P),
                                       cond=there, bounds_check="skip_entire_dma"))
                up = k.slot[s](sy.dma_start(w3[s][:, :, :], io["w3"][ds(e, 1)].squeeze(0).rearrange("(k p) f -> p k f", p=P),
                                            cond=there, bounds_check="skip_entire_dma"))
                k.wait(sy, r.step(k.p, PE_STEPS * s + 6))
                k.settled(sy)
                down = k.slot[2 + s](sy.dma_start(w2[s][:, :, :], io["w2"][ds(e, 1)].squeeze(0).rearrange("(k p) f -> p k f", p=P),
                                                  cond=there, bounds_check="skip_entire_dma"))
                got = gather(at + 1, n, [r.step(k.p, PE_STEPS * s + 5)])
                with k.only(pe, used_t > at, k.p, PE_STEPS, after=[got]):
                    if s:
                        k.wait(pe, up, rowed[0], rowed[1])
                    else:
                        k.wait(pe, up, r.step(k.a, ACT_STEPS + 5), r.step(k.v, VEC_STEPS + 5))
                    ts = []
                    for j, w in enumerate((w1[s], w3[s])):
                        for f in range(NK):
                            t = pe.matmul(k.bank[2 + j][:, :], xsT[s][:, f, :], w[:, f, :], start=f == 0, stop=f == NK - 1)
                        ts.append(k.p(t))
                    k.wait(pe, got)
                    t0 = turn(n, 0)
                    k.wait(pe, Mark(k.v, k.v.count + 1, r))
                    th = transposes(k, k.bank[4], hid[:, :])
                    t1 = turn(n, 1)
                    k.wait(pe, Mark(k.a, k.a.count + 6, r), down)
                    for h in range(2):
                        for f in range(DE // P):
                            t = pe.matmul(k.bank[5 + h][:, :], hidT[:, f * P:(f + 1) * P], w2[s][:, f, h * BANK:(h + 1) * BANK],
                                          start=f == 0, stop=f == DE // P - 1)
                    td = k.p(t)
                ma = k.A(act[:, :], k.bank[2][:, :], ACT.Silu, after=[ts[0], Mark(k.v, k.v.count - 5, r)])
                k.V(v.tensor_tensor, hid[:, :], act[:, :], k.bank[3][:, :], ALU.mult, after=[ma, ts[1]])
                rowed = [rows_out(n, 0, t0, [ts[1]]), rows_out(n, 1, t1, [ts[1]])]
                k.A(hidT[:, :], k.bank[4][:, :], ACT.Copy, after=[th])
                m1 = k.A(y[s][:, 0:BANK], k.bank[5][:, :], ACT.Copy, after=[td, r.last(k.slot[4 + s])])
                m2 = k.V(v.tensor_copy, y[s][:, BANK:], k.bank[6][:, :], after=[td, r.last(k.slot[4 + s])])
                k.wait(nc.scalar, m1, m2)
                k.slot[4 + s](nc.scalar.dma_start(ys[ds(at * P, P), :], y[s][:, :]))
    k.meet()


def combine(k, x, gates, where, ys, gate2, norm_w):
    nc = k.nc
    v = nc.vector
    with ExitStack() as c:
        sb = lambda *s, dt=F32: c.enter_context(k.area(list(s), dt))
        y = [[sb(P, D) for _ in range(2)] for _ in range(2)]
        idx = [[sb(P, 1, dt=U32) for _ in range(2)] for _ in range(2)]
        sq, ss = sb(P, D), sb(P, 2)
        with k.rounds(NT // 2, q0=2, q1=2, v=18, a=4) as r:
            for s in range(2):
                n = r.i * 2 + s
                xt = x[:, ds(n, 1), :].squeeze(1)
                for j in range(2):
                    mi = k.V(v.tensor_copy, idx[s][j][:, :], where[:, ds(n, 1), j:j + 1].squeeze(1), after=[r.last(k.soft[s])])
                    k.wait(nc.gpsimd, mi)
                    k.settled(nc.gpsimd)
                    got = k.soft[s](nc.gpsimd.indirect_dma_start(
                        out=y[s][j][:, :], out_offset=None, in_=ys[:, :],
                        in_offset=bass.IndirectOffsetOnAxis(ap=idx[s][j][:, 0:1], axis=0)))
                gt = gates[:, ds(n, 1), :].squeeze(1)
                m = k.V(v.tensor_scalar, y[s][0][:, :], y[s][0][:, :], gt[:, 0:1], None, ALU.mult, after=[got])
                m = k.V(v.scalar_tensor_tensor, y[s][0][:, :], y[s][1][:, :], gt[:, 1:2], y[s][0][:, :], ALU.mult, ALU.add, after=[m])
                m = k.V(v.tensor_tensor, y[s][0][:, :], y[s][0][:, :], gate2[:, :], ALU.mult, after=[m])
                mx = k.V(v.tensor_tensor, xt, xt, y[s][0][:, :], ALU.add, after=[m])
                m = k.A(sq[:, :], xt, ACT.Square, accum_out=ss[:, 0:1], after=[mx])
                m = rstd(k, ss[:, 1:2], ss[:, 0:1], D, m)
                k.V(v.scalar_tensor_tensor, xt, xt, ss[:, 1:2], norm_w[:, :], ALU.mult, ALU.mult, after=[m])
    k.meet()


def neighbourhood(k, nT, mixT, scratch):
    nc, io = k.nc, k.io
    v = nc.vector
    pairs = NAH // 2
    dr_w = (2 * KH - 1) * W
    with ExitStack() as c:
        sb = lambda *s: c.enter_context(k.area(list(s), F32))
        qkT = sb(P, 2 * pairs, T)
        val = sb(P, ROWS, BANK)

        def keep(r, j, s, banks, mark):
            m = k.A(qkT[:, ds(j, 1), 0:BANK].squeeze(1), banks[0][:, :], ACT.Copy, after=[mark])
            k.V(v.tensor_copy, qkT[:, ds(j, 1), BANK:].squeeze(1), banks[1][:, :], after=[mark])
        channels(k, nT, io["w_in_2"], 0, 2 * pairs, keep, p=2, v=2, a=2)
        k.meet()

        def keep_v(chunk, m, bank, mark):
            k.A(val[:, 2 * m, :], bank[:, :], ACT.Copy, after=[mark])
        project(k, nT, io["w_in_2"], 2 * BANK, 1, keep_v, a=NT)
        vv = val[:, :, :].rearrange("p (m t) c -> p m t c", t=2)
        for lo, hi, src in ((0, W, vv[W:P, 0:NT, 0, :]), (W, P, vv[0:W, 1:NT, 0, :])):
            n = NT if lo == 0 else NT - 1
            m = k.slot[0](nc.sync.dma_start(vv[lo:hi, 0:n, 1, :], src))
        bias = sb(P, pairs, dr_w)
        RW = 2 * W - 1
        k.slot[1](nc.sync.dma_start(scratch, wide(io["rpb"], 2, W)))
        k.wait(nc.sync, *k.now(k.slot[1]))
        for h in range(NAH):
            src = bass.AP(scratch.tensor, scratch.offset + h * (2 * KH - 1) * W * RW + W - 1, [[RW - 1, W], [W * RW, 2 * KH - 1], [1, W]])
            dst = bias[(h % 2) * W:(h % 2 + 1) * W, h // 2, :].rearrange("p (r c) -> p r c", c=W)
            m = k.slot[0](nc.sync.dma_start(dst, src))
        q2 = [sb(P, P) for _ in range(2)]
        sc = [sb(P, KH * W) for _ in range(2)]
        pT = [sb(P, KH * W) for _ in range(2)]
        ob = [sb(P, P) for _ in range(2)]
        st = [sb(P, 4) for _ in range(2)]
        for s in range(2):
            k.V(v.memset, q2[s][:, :], 0.0, after=[m])
        for p in range(pairs):
            b3 = bias[:, p, :].rearrange("p (r c) -> p r c", c=W)
            k.V(v.tensor_tensor, b3, b3, wide(k.c("window"), 1, 2 * KH - 1), ALU.add)
        k.meet()
        with k.rounds(ROWS, p=4 * pairs, v=5 * pairs, a=6 * pairs) as r:
            done = {}
            i = r.i
            lo = window_start(k, i)
            dr = k.nc.snap(lo - i + (KH - 1), min_val=0, max_val=KH - 1)
            for p in range(pairs):
                s = p % 2
                b = 4 * s
                before = done.get(s, [r.last(k.p)])
                k.A(q2[s][0:W, 0:W], qkT[0:W, p, ds(i * W, W)], ACT.Copy, scale=NAD ** -0.5, after=before)
                m = k.A(q2[s][W:P, W:P], qkT[W:P, p, ds(i * W, W)], ACT.Copy, scale=NAD ** -0.5)
                k.wait(nc.tensor, m, *(done.get(s) or [r.last(k.v), r.last(k.a)]))
                t = k.p(nc.tensor.matmul(k.bank[b][:, :], q2[s][:, :], qkT[:, pairs + p, ds(lo * W, KH * W)], start=True, stop=True))
                m = k.V(v.tensor_tensor, sc[s][:, :], k.bank[b][:, :], bias[:, p, ds(dr * W, KH * W)], ALU.add, after=[t])
                m = k.V(v.tensor_reduce, st[s][:, 0:1], sc[s][:, :], AX.X, ALU.max, after=[m])
                m = k.V(v.tensor_scalar, st[s][:, 1:2], st[s][:, 0:1], -1.0, None, ALU.mult, after=[m])
                m = k.A(sc[s][:, :], sc[s][:, :], ACT.Exp, bias=st[s][:, 1:2], accum_out=st[s][:, 2:3], after=[m])
                mr = k.V(v.reciprocal, st[s][:, 3:4], st[s][:, 2:3], after=[m])
                t = transposes(k, k.bank[b + 1], sc[s][:, :], after=[m])
                m = k.V(v.tensor_copy, pT[s][:, :], k.bank[b + 1][:, :], after=[t])
                k.wait(nc.tensor, m)
                for q in range(4):
                    t = nc.tensor.matmul(k.bank[b + 2][:, 0:P], pT[s][:, q * P:(q + 1) * P],
                                         val[:, ds(lo + 2 * q, 1), p * P:(p + 1) * P].squeeze(1), start=q == 0, stop=q == 3)
                t = k.p(t)
                m = k.A(ob[s][:, :], k.bank[b + 2][:, 0:P], ACT.Copy, scale=st[s][:, 3:4], after=[t, mr])
                k.wait(nc.tensor, m)
                t = k.p(nc.tensor.transpose(k.bank[b + 3][:, 0:P], ob[s][:, :], k.c("ident")))
                k.A(mixT[0:W, p, ds(i * W, W)], k.bank[b + 3][0:W, 0:W], ACT.Copy, after=[t])
                m = k.A(mixT[W:P, p, ds(i * W, W)], k.bank[b + 3][W:P, W:P], ACT.Copy)
                done[s] = [m, mr, t]
    k.meet()


def window_start(k, i):
    lo = (i - KH // 2) * (i >= KH // 2) - (i - (ROWS - KH // 2)) * (i >= ROWS - KH // 2)
    return k.nc.snap(lo, min_val=0, max_val=ROWS - KH)


def log_sigmoid(k, out, x, t, m):
    v = k.nc.vector
    m = k.A(t, x, ACT.Abs, after=[m])
    m = k.A(t, t, ACT.Exp, scale=-1.0, after=[m])
    m = k.A(t, t, ACT.Ln, bias=1.0, after=[m])
    m = k.V(v.scalar_tensor_tensor, out, x, 0.0, t, ALU.min, ALU.subtract, after=[m])
    return k.V(v.tensor_scalar, out, out, 1.0 / 16.0, None, ALU.mult, after=[m])


def gla(k, nT, mixT):
    nc, io = k.nc, k.io
    v, g = nc.vector, nc.gpsimd
    KW2 = RH * DK
    RANK = 16
    hd = lambda ap, d=DH: ap.rearrange("p (h d) -> p h d", d=d)
    with ExitStack() as c:
        sb = lambda *s: c.enter_context(k.area(list(s), F32))
        qkvr = sb(P, NT, 3 * BANK)

        def keep(chunk, m, bank, mark):
            if chunk == 2:
                k.A(qkvr[:, m, 2 * BANK:], bank[:, :], ACT.Silu, after=[mark])
            else:
                k.V(v.tensor_copy, qkvr[:, m, chunk * BANK:(chunk + 1) * BANK], bank[:, :], after=[mark])
        project(k, nT, io["w_in_2"], 3 * BANK, 3, keep)
        oacc = sb(P, NT, BANK)
        la = [sb(P, NT, KW2) for _ in range(2)]
        ng = sb(P, DV)
        with ExitStack() as c2:
            sb2 = lambda *s: c2.enter_context(k.area(list(s), F32))
            wz, zT, gu, gbias = sb2(P, NK, 2 * RANK), [sb2(RANK, T) for _ in range(2)], sb2(RANK, 2, KW2), sb2(P, 2, KW2)
            x, t = [sb2(P, KW2) for _ in range(2)], [sb2(P, KW2) for _ in range(2)]
            load_columns(k, 0, wz[:, :, :], io["w_in_2"], 6 * BANK, 2 * RANK)
            for n, way in enumerate(("fwd", "bwd")):
                k.slot[0](nc.sync.dma_start(gu[:, n, :], io[f"gate_up_{way}"]))
                k.slot[0](nc.sync.dma_start(gbias[:, n, :], spread(io[f"gate_bias_{way}"], KW2)))
            loaded = k.slot[0](nc.sync.dma_start(ng[:, :], spread(io["gla_norm_g"], DV)))
            k.wait(nc.tensor, loaded)
            for n in range(2):
                for h in range(2):
                    b = k.bank[2 * n + h]
                    for f in range(NK):
                        tt = nc.tensor.matmul(b[0:RANK, :], wz[:, f, n * RANK:(n + 1) * RANK], nT[:, f, h * BANK:(h + 1) * BANK],
                                              start=f == 0, stop=f == NK - 1)
                    m = k.V(v.tensor_copy, zT[n][:, h * BANK:(h + 1) * BANK], b[0:RANK, :], after=[k.p(tt)])
            k.wait(nc.tensor, m)
            k.wait(nc.vector, loaded)
            last = {}
            for m in range(NT):
                for n in range(2):
                    b = k.bank[4 + 2 * n + m % 2]
                    k.wait(nc.tensor, *last.get((n, m % 2), []))
                    tt = k.p(nc.tensor.matmul(b[:, 0:KW2], zT[n][:, m * P:(m + 1) * P], gu[:, n, :], start=True, stop=True))
                    mm = k.V(v.tensor_tensor, x[n][:, :], b[:, 0:KW2], gbias[:, n, :], ALU.add, after=[tt] + last.get((n, (m + 1) % 2), []))
                    last[(n, m % 2)] = [log_sigmoid(k, la[n][:, m, :], x[n][:, :], t[n][:, :], mm)]
            k.meet()

        lt, eb, enb, ek, qd, ki, kt = (sb(P, KW2) for _ in range(7))
        vt, qkT, AT, o, sq, ss = sb(P, BANK), sb(P, BANK), sb(P, BANK), sb(P, BANK), sb(P, BANK), sb(P, RH)
        dec, state = sb(P, 2, 2), sb(P, 2, DV)
        for back in (False, True):
            sums, mask = ("after", "behind") if back else ("upto", "upto")
            zero = k.V(v.memset, state[:, :, :], 0.0, after=k.now(k.p))
            k.wait(nc.tensor, zero)
            with k.rounds(NT, p=9 if back else 8, v=25 if back else 18, a=8 if back else 5, g=1) as r:
                i = nc.snap((NT - 1) - r.i, min_val=0, max_val=NT - 1) if back else r.i
                row = qkvr[:, ds(i, 1), :].squeeze(1)
                ml = k.V(v.tensor_copy, lt[:, :], la[int(back)][:, ds(i, 1), :].squeeze(1), after=[r.last(k.p)])
                mv = k.A(vt[:, :], row[:, BANK:2 * BANK], ACT.Copy, after=[r.last(k.p)])
                k.wait(nc.tensor, ml, mv, r.last(k.v), r.last(k.a))
                nc.tensor.matmul(k.bank[0][:, 0:KW2], k.c(sums), lt[:, :], start=True, stop=True)
                nc.tensor.matmul(k.bank[0][:, KW2:], k.c("chunk"), lt[:, :], start=True, stop=True)
                for p in range(2):
                    t = nc.tensor.matmul(k.bank[1][:, 2 * p:2 * p + 2], lt[:, p * P:(p + 1) * P], k.c("halves"), start=True, stop=True)
                t = k.p(t)
                me = k.A(eb[:, :], k.bank[0][:, 0:KW2], ACT.Exp, after=[t, r.last(k.v)])
                mn = k.A(enb[:, :], k.bank[0][:, 0:KW2], ACT.Exp, scale=-1.0, after=[r.last(k.g)])
                md = k.A(dec[:, :, :], k.bank[1][:, 0:4].rearrange("p (a b) -> p a b", b=2), ACT.Exp)
                mb = k.V(v.tensor_copy, ek[:, :], k.bank[0][:, 0:KW2], after=[t, r.last(k.g), mn])
                m = k.V(v.tensor_tensor, ek[:, :], k.bank[0][:, KW2:], ek[:, :], ALU.subtract, after=[mb])
                mk = k.A(ek[:, :], ek[:, :], ACT.Exp, after=[m])
                mq = k.V(v.scalar_tensor_tensor, qd[:, :], row[:, 0:KW2], DK ** -0.5, eb[:, :], ALU.mult, ALU.mult, after=[me])
                mi = k.V(v.tensor_tensor, ki[:, :], row[:, KW2:BANK], enb[:, :], ALU.mult, after=[mn])
                mt = k.G(g.tensor_tensor, kt[:, :], row[:, KW2:BANK], ek[:, :], ALU.mult, after=[mk, r.last(k.p)])
                k.wait(nc.tensor, mq, mi)
                for p in range(2):
                    nc.tensor.transpose(k.bank[2][:, p * P:(p + 1) * P], qd[:, p * P:(p + 1) * P], k.c("ident"))
                    t = nc.tensor.transpose(k.bank[2][:, (2 + p) * P:(3 + p) * P], ki[:, p * P:(p + 1) * P], k.c("ident"))
                t = k.p(t)
                m = k.V(v.tensor_copy, qkT[:, :], k.bank[2][:, :], after=[t])
                k.wait(nc.tensor, m, mt)
                for u in range(2):
                    ch = slice(u * DK, (u + 1) * DK)
                    for p in range(2):
                        t = nc.tensor.matmul(k.bank[3 + u][:, p * P:(p + 1) * P], qkT[ch, (2 + p) * P:(3 + p) * P], qkT[ch, p * P:(p + 1) * P],
                                             start=True, stop=True)
                    t = k.p(t)
                    m = k.V(v.tensor_tensor, AT[:, :].rearrange("p (a u d) -> p a u d", a=2, u=2)[:, :, u, :],
                            hd(k.bank[3 + u][:, 0:2 * P]), wide(k.c(mask), 1, 2), ALU.mult, after=[t])
                k.wait(nc.tensor, m)
                for q in range(2):
                    rows = slice(q * DC, (q + 1) * DC)
                    for p in range(2):
                        t = nc.tensor.matmul(k.bank[6 + q][:, p * 2 * DV:(p + 1) * 2 * DV], kt[rows, p * P:(p + 1) * P],
                                             vt[rows, p * 2 * DV:(p + 1) * 2 * DV], start=True, stop=True)
                    tc = k.p(t)
                ob = (k.bank[5], k.bank[4])
                for h in range(RH):
                    nc.tensor.matmul(ob[h % 2][:, h // 2 * DV:(h // 2 + 1) * DV], AT[:, h * P:(h + 1) * P], vt[:, h * DV:(h + 1) * DV], start=h < 2, stop=False,
                                     skip_group_check=True)
                for q in ((1, 0) if back else (0, 1)):
                    rows = slice(q * DC, (q + 1) * DC)
                    k.settled(nc.tensor)
                    for h in range(RH):
                        p, u = h // 2, h % 2
                        ch = slice(u * DK, (u + 1) * DK)
                        t = nc.tensor.matmul(ob[u][rows, p * DV:(p + 1) * DV], qkT[ch, p * P + q * DC:p * P + (q + 1) * DC], state[ch, p, :],
                                             start=False, stop=True, skip_group_check=True)
                    t = k.p(t)
                    for h in range(RH):
                        p, u = h // 2, h % 2
                        ch = slice(u * DK, (u + 1) * DK)
                        m = k.V(v.scalar_tensor_tensor, state[ch, p, :], state[ch, p, :], dec[ch, p, q:q + 1],
                                k.bank[6 + q][ch, h * DV:(h + 1) * DV], ALU.mult, ALU.add, after=[t, tc, md])
                    k.wait(nc.tensor, m)
                acc = oacc[:, ds(i, 1), :].squeeze(1)
                two = lambda ap, u: ap.rearrange("p (a u d) -> p a u d", a=2, u=2)[:, :, u, :]
                for u in range(2):
                    src = hd(ob[u][:, 0:2 * DV])
                    if not back:
                        m = k.V(v.tensor_copy, two(acc, u), src, after=[t])
                    else:
                        m = k.V(v.tensor_tensor, two(o[:, :], u), src, two(acc, u), ALU.add, after=[t])
                if back:
                    m = heads_norm(k, hd(o[:, :]), hd(sq[:, :]), ss[:, :], ng[:, :], hd(row[:, 2 * BANK:]), DV, m, t)
                    t = transposes(k, k.bank[2], o[:, :], after=[m])
                    k.A(mixT[:, 4:6, ds(i * P, P)], k.bank[2][:, 0:2 * P].rearrange("p (h t) -> p h t", h=2), ACT.Copy, after=[t])
                    k.A(mixT[:, 6:8, ds(i * P, P)], k.bank[2][:, 2 * P:].rearrange("p (h t) -> p h t", h=2), ACT.Copy)
            k.meet()


def mlp_up(k, nT, uT):
    nc = k.nc

    def use(r, j, s, banks, mark):
        for h in range(2):
            dst = uT[:, ds(j, 1), h * BANK:(h + 1) * BANK].squeeze(1)
            m = k.A(dst, banks[h][:, :], ACT.Relu, after=[mark])
            k.V(nc.vector.tensor_tensor, dst, dst, banks[h][:, :], ALU.mult, after=[m])
    channels(k, nT, k.io["w_ff1"], 0, NF, use, p=2, v=4, a=4)
    k.meet()


def mlp_down(k, uT, x_dram, out_dram):
    nc = k.nc
    v = nc.vector
    with ExitStack() as c:
        sb = lambda *s: c.enter_context(k.area(list(s), F32))
        w = [sb(P, NF // 2, P) for _ in range(2)]
        yT = sb(P, T)
        xc = sb(P, NT, P)
        with k.rounds(NK, s0=1, s1=1, s2=1, q4=1, p=4, a=1, v=3) as r:
            cols = ds(r.i * P, P)
            t = None
            k.wait(nc.sync, r.last(k.soft[4]))
            mx = k.slot[2](nc.sync.dma_start(xc[:, :, :], x_dram[:, cols].rearrange("(m p) c -> p m c", p=P)))
            for s in range(2):
                k.wait(nc.sync, r.step(k.p, s + 1))
                rows = k.io["w_ff2"][s * (DFF // 2):(s + 1) * (DFF // 2), cols]
                loaded = k.slot[s](nc.sync.dma_start(w[s][:, :, :], rows.rearrange("(f p) c -> p f c", p=P)))
                k.wait(nc.tensor, loaded, *([r.last(k.v), r.last(k.a)] if s == 0 else []))
                for f in range(NF // 2):
                    for h in range(2):
                        ff = s * (NF // 2) + f
                        t = nc.tensor.matmul(k.bank[h][:, :], w[s][:, f, :], uT[:, ff, h * BANK:(h + 1) * BANK],
                                             start=ff == 0, stop=ff == NF - 1)
                t = k.p(t)
            ma = k.A(yT[:, 0:BANK], k.bank[0][:, :], ACT.Copy, after=[t])
            mb = k.V(v.tensor_copy, yT[:, BANK:], k.bank[1][:, :], after=[t])
            for h in range(2):
                t = transposes(k, k.bank[2 + h], yT[:, h * BANK:(h + 1) * BANK], after=[(ma, mb)[h]])
                part = xc[:, 4 * h:4 * h + 4, :]
                m = k.V(v.tensor_tensor, part, part, k.bank[2 + h][:, :].rearrange("p (m c) -> p m c", c=P), ALU.add, after=[t, mx])
            k.wait(nc.gpsimd, m)
            k.soft[4](nc.gpsimd.dma_start(out_dram[:, cols].rearrange("(m p) c -> p m c", p=P), xc[:, :, :]))
    k.meet()


def final_norm(k, x, norm_w, out):
    nc = k.nc
    v = nc.vector
    with ExitStack() as c:
        sq = c.enter_context(k.area([P, D], F32))
        ss = c.enter_context(k.area([P, 2 * NT], F32))
        for n in range(NT):
            s0, s1 = ss[:, 2 * n:2 * n + 1], ss[:, 2 * n + 1:2 * n + 2]
            m = k.A(sq[:, :], x[:, n, :], ACT.Square, accum_out=s0)
            m = rstd(k, s1, s0, D, m)
            m = k.V(v.scalar_tensor_tensor, x[:, n, :], x[:, n, :], s1, norm_w[:, :], ALU.mult, ALU.mult, after=[m])
            k.wait(nc.sync, m)
            k.store(nc.sync.dma_start(out[0, n * P:(n + 1) * P, :], x[:, n, :]))


def load_rows(k, x, dram):
    return k.slot[8](k.nc.sync.dma_start(x[:, :, :], dram.rearrange("(m p) c -> p m c", p=P)))


def build(nc, io, out, tap=None):
    with ExitStack() as ctx:
        k = Program(nc, ctx, io)
        tap = tap or (lambda *a: None)
        sb = lambda *s, dt=F32: ctx.enter_context(k.area(list(s), dt))
        k.bank = [ctx.enter_context(nc.psum_tensor(f"bank{n}", [P, BANK], F32)) for n in range(8)]
        table = shape_constants()
        width = sum(a.shape[1] for a in table.values())
        consts = sb(P, width)
        k.slot[0](nc.sync.dma_start(consts[:, :], io["constants"]))
        at, where_const = 0, {}
        for name, a in table.items():
            where_const[name] = consts[:, at:at + a.shape[1]]
            at += a.shape[1]
        k.c = lambda name: where_const[name]

        xn_rows = nc.dram_tensor("xn_rows", [T, D], F32, kind="Internal").ap()
        y_rows = nc.dram_tensor("y_rows", [BLOCKS * P, D], F32, kind="Internal").ap()
        x_rows = [nc.dram_tensor(f"x_rows{n}", [T, D], F32, kind="Internal").ap() for n in range(4)]

        rpb_rows = nc.dram_tensor("rpb_rows", [NAH, 2 * KH - 1, W, 2 * W - 1], F32, kind="Internal").ap()

        cols = sb(P, 4, NK)
        k.slot[1](nc.sync.dma_start(cols[:, :, :], io["norm_columns"]))
        k.meet()
        mod = sb(P, 6 * NK)
        affine = sb(P, 4, NK)
        gate1, gate2 = sb(P, D), sb(P, D)
        gates = sb(P, NT, 2)
        where, tokens = sb(P, NT, 2, dt=U32), sb(P, BLOCKS + 1, dt=U32)
        experts = sb(P, BLOCKS + 1, dt=I32)
        hT = sb(P, NK, T)

        def with_x(source, *steps):
            with k.area([P, NT, D], F32) as x:
                loaded = load_rows(k, x, source)
                k.wait(nc.vector, loaded)
                k.wait(nc.scalar, loaded)
                for step in steps:
                    step(x)
                k.meet()

        def to(dram):
            def step(x):
                k.wait(nc.sync, *k.now(k.v, k.g))
                k.store(nc.sync.dma_start(dram.rearrange("(m p) c -> p m c", p=P), x[:, :, :]))
            return step

        modulation(k, mod, (gate1, gate2))
        for n, j in ((0, 0), (1, 3)):
            k.V(nc.vector.scalar_tensor_tensor, affine[:, 2 * n, :], mod[:, (j + 1) * NK:(j + 2) * NK], 1.0, cols[:, n, :], ALU.add, ALU.mult)
            k.V(nc.vector.tensor_copy, affine[:, 2 * n + 1, :], mod[:, j * NK:(j + 1) * NK])
        k.meet()
        with_x(io["x"], lambda x: norm_transpose(k, x, hT, affine[:, 0, :], affine[:, 1, :]))
        tap("hT", hT)
        with k.area([P, NK, T], F32) as mixT:
            with k.area([P, NT, DH // 2], F32) as cos, k.area([P, NT, DH // 2], F32) as sin:
                rotary_tables(k, cos, sin)
                tap("cos", cos)
                tap("sin", sin)
                retention(k, hT, mixT, cos, sin)
            delta(k, hT, mixT)
            tap("mixT", mixT)
            with_x(io["x"], lambda x: residual(k, mixT, io["w_out"], x, gate1), to(x_rows[0]),
                   lambda x: norm_transpose(k, x, hT, affine[:, 2, :], affine[:, 3, :], xn_dram=xn_rows))
        route(k, hT, gates, where, tokens, experts)
        for name, value in (("gates", gates), ("where", where), ("tokens", tokens), ("experts", experts)):
            tap(name, value)
        experts_pass(k, affine[:, 2, :], affine[:, 3, :], tokens, experts, xn_rows, y_rows)
        with k.area([P, D], F32) as norm_w:
            k.slot[2](nc.sync.dma_start(norm_w[:, :], spread(io["final_norm_w"], D)))
            k.meet()
            with_x(x_rows[0], lambda x: combine(k, x, gates, where, y_rows, gate2, norm_w), to(x_rows[1]), lambda x: tap("x3", x),
                   lambda x: norm_transpose(k, x, hT, cols[:, 2, :], None))
        with k.area([P, NK, T], F32) as mixT:
            neighbourhood(k, hT, mixT, rpb_rows)
            gla(k, hT, mixT)
            tap("mixT2", mixT)
            with_x(x_rows[1], lambda x: residual(k, mixT, io["w_out_2"], x, None), to(x_rows[2]),
                   lambda x: norm_transpose(k, x, hT, cols[:, 3, :], None))
        with k.area([P, NF, T], F32) as uT:
            mlp_up(k, hT, uT)
            mlp_down(k, uT, x_rows[2], x_rows[3])
        with k.area([P, D], F32) as norm_w:
            k.slot[2](nc.sync.dma_start(norm_w[:, :], spread(io["ln_final_g_2"], D)))
            k.meet()
            with_x(x_rows[3], lambda x: final_norm(k, x, norm_w, out))


def arrays_of(inputs):
    a = {n: np.ascontiguousarray(v) for n, v in inputs.items()}
    by_feature = lambda v: v.reshape(NK, P).T
    vec = lambda n: a[n].reshape(-1)
    io = {n: a[n][0] for n in ("x", "w_ada", "w_in", "w_out", "w_group", "w_expert", "w1", "w3", "w2",
                               "w_in_2", "w_out_2", "w_ff1_2", "w_ff2_2")}
    io["w_ff1"], io["w_ff2"] = io.pop("w_ff1_2"), io.pop("w_ff2_2")
    io["b_ada"] = a["b_ada"].reshape(1, -1)
    io["cT"] = by_feature(a["c"].reshape(-1))
    io["positions"] = a["positions"].reshape(NT, P).T
    io["norm_columns"] = np.stack([by_feature(a[n].reshape(-1)) for n in ("norm1_w", "norm2_w", "ln_mix_g_2", "ln_ff_g_2")], 1)
    io["conv"] = a["conv_w"][0].reshape(4, 12, P).transpose(2, 1, 0)
    for n, src in (("a_log", "a_log"), ("dt_bias", "dt_bias"), ("dn_norm_w", "dn_norm_w"), ("b_group", "b_group"),
                   ("b_expert", "b_expert"), ("final_norm_w", "final_norm_w"), ("ln_final_g_2", "ln_final_g_2"),
                   ("gla_norm_g", "gla_norm_g_2"), ("gate_bias_fwd", "gla_gate_bias_fwd_2"), ("gate_bias_bwd", "gla_gate_bias_bwd_2")):
        io[n] = vec(src)
    io["gate_up_fwd"], io["gate_up_bwd"] = a["gla_gate_up_fwd_2"][0], a["gla_gate_up_bwd_2"][0]
    rpb = np.zeros((NAH, 2 * KH - 1, 2 * W - 1), np.float32)
    rpb[:, :, W - KW:W - KW + 2 * KW - 1] = a["na_rpb_2"][0]
    io["rpb"] = rpb
    io["constants"] = np.concatenate(list(shape_constants().values()), 1)
    return {n: np.ascontiguousarray(v) for n, v in io.items()}


def kernel(**inputs):
    import concourse.bacc as bacc
    from concourse.bass_utils import run_bass_kernel_spmd as run

    arrays = arrays_of({n: np.asarray(v) for n, v in inputs.items()})
    nc = bacc.Bacc("TRN2", target_bir_lowering=False, num_devices=1)
    io = {n: nc.dram_tensor(f"in_{n}", a.shape, mybir.dt.from_np(a.dtype), kind="ExternalInput").ap() for n, a in arrays.items()}
    out = nc.dram_tensor("out", [1, T, D], F32, kind="ExternalOutput").ap()
    build(nc, io, out)
    result = run(nc, [{f"in_{n}": a for n, a in arrays.items()}], core_ids=[0])
    return result.results[0]["out"]
```

```python
from contextlib import ExitStack, contextmanager

import numpy as np

import concourse.bass as bass
from concourse import mybir

F32 = mybir.dt.float32
I32 = mybir.dt.int32
U32 = mybir.dt.uint32
ALU = mybir.AluOpType
ACT = mybir.ActivationFunctionType
AX = mybir.AxisListType
ds = bass.ds

P = 128
T = 1024
D = 1024
NT = T // P
NK = D // P
BANK = 512
NEG = -1.0e30
EPS = 1e-6

RH = 4
DH = 128
RC = 128
DC = 64
GROUPS, PER_GROUP = 4, 8
NE = GROUPS * PER_GROUP
DE = D // 2
BLOCKS = 2 * T // P + NE
ROWS, W = 16, 64
KH, KW = 8, 16
NAH, NAD = 8, 64
DK, DV = 64, 128
DFF = 4 * D
NF = DFF // P
IN1 = 8 * 512 + 8
IN2 = 3 * 512 + 2 * 256 + 2 * 512 + 32

LEVELS = (1, 2, 4, 8, 16, 32)


def shape_constants():
    i = np.arange(P)
    j = i[:, None]
    same = (i[None, :] // DC) == (j // DC)
    gamma = 1.0 - 2.0 ** (-5.0 - np.arange(RH))
    c = {}
    c["ident"] = np.eye(P)
    c["ones"] = np.ones((P, P))
    c["upto"] = same & (j <= i[None, :])
    c["after"] = same & (j >= i[None, :])
    c["behind"] = same & (j > i[None, :])
    c["chunk"] = same
    c["before"] = j < i[None, :]
    for b in LEVELS:
        c[f"level{b}"] = (i[None, :] // (2 * b) == j // (2 * b)) & (i[None, :] % (2 * b) >= b) & (j % (2 * b) < b)
    c["ret_mask"] = np.concatenate([np.where(i[None, :] >= j, g ** -(j + 1.0), 0.0) * DH ** -0.5 for g in gamma], 1)
    c["ret_out"] = np.stack([g ** (i + 1.0) for g in gamma], 1)
    c["ret_key"] = np.stack([g ** (RC - 1.0 - i) * DH ** -0.5 for g in gamma], 1)
    c["halves"] = np.stack([i < DC, i >= DC], 1)
    c["half0"] = np.repeat((i < DC)[:, None], P, 1)
    c["half1"] = np.repeat((i >= DC)[:, None], P, 1)
    c["row"] = np.repeat(i[None, :], P, 0)
    c["token"] = j + P * np.arange(NT)[None, :]
    c["steps"] = np.repeat(P * np.arange(NT)[None, :], P, 0)
    c["inv_freq"] = np.repeat((np.float32(10000.0) ** (-np.arange(0, DH, 2, dtype=np.float32) / np.float32(DH)))[None, :], P, 0)
    q = i % W
    start = np.clip(q - KW // 2, 0, W - KW)[:, None]
    k = np.arange(W)[None, :]
    c["window"] = np.where((k >= start) & (k < start + KW), 0.0, NEG)
    c["qk_scale"] = np.repeat(np.array([DH ** -0.5] * RH + [1.0] * RH)[None, :], P, 0)
    return {n: np.asarray(v, np.float32).reshape(P, -1) for n, v in c.items()}


class Line:

    def __init__(self, k, name, step=1, credit=0, engine=None):
        self.k, self.step, self.count, self.engine = k, step, credit, engine
        self.sem = k.ctx.enter_context(k.nc.semaphore(name))
        self.name = name
        k.lines.append(self)

    def __call__(self, instruction):
        instruction.then_inc(self.sem, self.step)
        self.count += self.step
        loop = self.k.loop
        assert loop is None or self in loop.per, f"{self.name} is not among the loop's lines"
        return Mark(self, self.count, loop)


class Mark:

    def __init__(self, line, at, loop, ago=0):
        self.line, self.at, self.loop, self.ago = line, at, loop, ago

    def before(self, rounds):
        return Mark(self.line, self.at, self.loop, self.ago + rounds)

    def order(self):
        back = self.ago * self.loop.per[self.line] * self.line.step if self.loop else 0
        return (self.at - back) if self.loop is None or not self.loop.over else self.value()

    def value(self):
        if self.loop is None:
            return self.at
        per = self.loop.per[self.line] * self.line.step
        if self.loop.over:
            return self.at + (self.loop.n - 1) * per
        return self.loop.i * per + (self.at - self.ago * per)


class Rounds:

    def __init__(self, k, n, per):
        self.k, self.n, self.per, self.over = k, n, dict(per), False

    def __enter__(self):
        assert self.k.loop is None
        self.k.loop = self
        self.base = {line: line.count for line in self.per}
        self.fori = self.k.nc.Fori(0, self.n)
        self.i = self.fori.__enter__()
        return self

    def last(self, line, ago=1):
        return Mark(line, self.base[line] + self.per[line] * line.step, self, ago)

    def step(self, line, nth, ago=1):
        return Mark(line, self.base[line] + nth * line.step, self, ago)

    def __exit__(self, *failed):
        self.fori.__exit__(*failed)
        if failed[0] is None:
            made = {line: (line.count - self.base[line]) // line.step for line in self.per}
            assert made == self.per, "steps a round: " + ", ".join(f"{x.name} {n}" for x, n in made.items())
            for line, per in self.per.items():
                line.count = self.base[line] + self.n * per * line.step
            self.over = True
            self.k.loop = None


class Program:
    CREDIT = 256

    def __init__(self, nc, ctx, io, tap=None):
        self.nc, self.ctx, self.io, self.lines, self.loop, self.areas = nc, ctx, io, [], None, 0
        self.tap = tap
        self.v = Line(self, "vector_steps", credit=self.CREDIT, engine=nc.vector)
        self.a = Line(self, "scalar_steps", credit=self.CREDIT, engine=nc.scalar)
        self.p = Line(self, "tensor_steps", credit=self.CREDIT, engine=nc.tensor)
        self.g = Line(self, "gpsimd_steps", credit=self.CREDIT, engine=nc.gpsimd)
        self.slot = [Line(self, f"load_slot{n}", step=16, credit=self.CREDIT, engine=nc.sync) for n in range(10)]
        self.store = Line(self, "stores", step=16, credit=self.CREDIT, engine=nc.sync)
        for line in self.lines:
            line.engine.sem_inc(line.sem, self.CREDIT)
        self.soft = [Line(self, f"soft_slot{n}", step=16) for n in range(5)]
        self.passed = ctx.enter_context(nc.semaphore("waits_passed"))

    def area(self, shape, dtype=F32):
        self.areas += 1
        return self.nc.sbuf_tensor(f"area{self.areas}", list(shape), dtype)

    def wait(self, engine, *marks):
        latest = {}
        for m in marks:
            if m.line not in latest or m.order() > latest[m.line].order():
                latest[m.line] = m
        for m in latest.values():
            engine.wait_ge(m.line.sem, m.value())

    @contextmanager
    def only(self, engine, cond, line, steps, after=()):
        before = self.now(line)
        with engine.If(cond):
            yield
        assert line.count == before[0].at + steps * line.step
        with engine.Else():
            self.wait(engine, *before, *after)
            engine.sem_inc(line.sem, steps * line.step)

    def settled(self, engine):
        engine.sem_inc(self.passed, 1)

    def now(self, *lines):
        return [Mark(x, x.count, self.loop) for x in lines]

    def meet(self):
        assert self.loop is None
        for engine in (self.nc.sync, self.nc.vector, self.nc.scalar, self.nc.tensor, self.nc.gpsimd):
            for line in self.lines:
                if line.count:
                    engine.wait_ge(line.sem, line.count)

    def rounds(self, n, **per):
        return Rounds(self, n, {self.named(k): c for k, c in per.items() if c})

    def named(self, k):
        lines = {"v": self.v, "a": self.a, "p": self.p, "g": self.g, "store": self.store}
        lines.update({f"s{n}": x for n, x in enumerate(self.slot)})
        lines.update({f"q{n}": x for n, x in enumerate(self.soft)})
        return lines[k]

    def take(self, line, after, chain):
        own = self.now(line) if chain else [m for m in after if m.line is line]
        self.wait(line.engine, *own, *[m for m in after if m.line is not line])

    def V(self, instruction, *args, after=(), chain=True, **kw):
        self.take(self.v, after, chain)
        return self.v(instruction(*args, **kw))

    def A(self, out, in_, func, after=(), chain=True, **kw):
        self.take(self.a, after, chain)
        return self.a(self.nc.scalar.activation(out, in_, func, **kw))

    def G(self, instruction, *args, after=(), **kw):
        self.take(self.g, after, True)
        return self.g(instruction(*args, **kw))


def wide(ap, axis, n):
    shape = list(ap.shape)
    shape.insert(axis, n)
    return ap.unsqueeze(axis).broadcast_to(shape)


def interleave(*streams):
    streams = list(streams)
    while streams:
        streams = [x for x in streams if next(x, x) is not x]


def spread(dram, n, parts=P):
    return bass.AP(dram.tensor, dram.offset, [[0, parts], [1, n]])


def rstd(k, out, total, n, m, eps=EPS):
    v = k.nc.vector
    m = k.V(v.tensor_scalar, out, total, 1.0 / n, eps, ALU.mult, ALU.add, after=[m])
    m = k.V(v.reciprocal, out, out, after=[m])
    return k.A(out, out, ACT.Sqrt, after=[m])


def norm_transpose(k, x, xT, scale, shift, xn_dram=None):
    nc = k.nc
    with ExitStack() as c:
        sq = c.enter_context(k.area([P, D], F32))
        xn = c.enter_context(k.area([P, D], F32))
        ss = c.enter_context(k.area([P, 2], F32))
        store = 1 if xn_dram is not None else 0
        with k.rounds(NT, a=2 + NK // 2, v=3 + NK // 2, p=2, q4=store) as r:
            i = r.i
            m = k.A(sq[:, :], x[:, ds(i, 1), :].squeeze(1), ACT.Square, accum_out=ss[:, 0:1], after=[r.step(k.v, 2)])
            m = rstd(k, ss[:, 1:2], ss[:, 0:1], D, m)
            before = [r.last(k.p)] + ([r.last(k.soft[4])] if store else [])
            m = k.V(nc.vector.tensor_scalar, xn[:, :], x[:, ds(i, 1), :].squeeze(1), ss[:, 1:2], None, ALU.mult,
                    after=[m] + before)
            if store:
                k.wait(nc.gpsimd, m)
                k.soft[4](nc.gpsimd.dma_start(xn_dram[ds(i * P, P), :], xn[:, :]))
            for half in range(2):
                bank = k.bank[half]
                k.wait(nc.tensor, m, r.last(k.v), r.last(k.a))
                for q in range(4):
                    f = half * 4 + q
                    t = nc.tensor.transpose(bank[:, q * P:(q + 1) * P], xn[:, f * P:(f + 1) * P], k.c("ident"))
                t = k.p(t)
                for q in range(4):
                    f = half * 4 + q
                    dst = xT[:, f, ds(i * P, P)]
                    src = bank[:, q * P:(q + 1) * P]
                    if half == 0:
                        k.A(dst, src, ACT.Identity, scale=scale[:, f:f + 1],
                            bias=shift[:, f:f + 1] if shift is not None else 0.0, after=[t])
                    elif shift is not None:
                        k.V(nc.vector.tensor_scalar, dst, src, scale[:, f:f + 1], shift[:, f:f + 1],
                            ALU.mult, ALU.add, after=[t])
                    else:
                        k.V(nc.vector.tensor_scalar, dst, src, scale[:, f:f + 1], None, ALU.mult, after=[t])
    k.meet()


def load_columns(k, slot, wbuf, w, col, n, after=()):
    k.wait(k.nc.sync, *after)
    return k.slot[slot](k.nc.sync.dma_start(wbuf, w[:, ds(col, n)].rearrange("(k p) c -> p k c", p=P)))


def project(k, xT, w, col0, chunks, evacuate, v=0, a=0, g=0):
    nc = k.nc
    with ExitStack() as c:
        wbuf = [c.enter_context(k.area([P, NK, BANK], F32)) for _ in range(2)]

        def chunk(s, at, before, used):
            loaded = load_columns(k, s, wbuf[s][:, :, :], w, at * BANK + col0, BANK, after=used)
            for m in range(NT):
                k.wait(nc.tensor, *before(m))
                if m == 0:
                    k.wait(nc.tensor, loaded)
                for f in range(NK):
                    t = nc.tensor.matmul(k.bank[m][:, :], xT[:, f, m * P:(m + 1) * P], wbuf[s][:, f, :],
                                         start=f == 0, stop=f == NK - 1)
                evacuate(at, m, k.bank[m], k.p(t))

        if chunks % 2 == 0 and chunks > 2:
            with k.rounds(chunks // 2, p=2 * NT, v=2 * v, a=2 * a, g=2 * g, s0=1, s1=1) as r:
                chunk(0, r.i * 2, lambda m: [r.last(k.v), r.last(k.a)], [r.step(k.p, NT)])
                made = k.now(k.v, k.a)
                chunk(1, r.i * 2 + 1, lambda m: made, [r.last(k.p)])
        else:
            for n in range(chunks):
                made = k.now(k.v, k.a)
                chunk(n % 2, n, lambda m: made, k.now(k.p) if n > 1 else [])
    k.meet()


def modulation(k, mod, gates):
    nc, io = k.nc, k.io
    third = 2 * D
    with ExitStack() as c:
        acc = c.enter_context(k.area([P, 6 * D], F32))
        wa = [c.enter_context(k.area([P, third], F32)) for _ in range(6)]
        cT = c.enter_context(k.area([P, NK], F32))
        zero = k.V(nc.vector.memset, acc[:, :], 0.0)
        k.wait(nc.sync, zero)
        bias = k.slot[6](nc.sync.dma_start(acc[0:1, :], io["b_ada"]))
        cl = k.slot[7](nc.sync.dma_start(cT[:, :], io["cT"]))
        silu = k.A(cT[:, :], cT[:, :], ACT.Silu, after=[cl])
        k.wait(nc.vector, bias, silu)
        with k.rounds(NK // 2, v=6, s0=1, s1=1, s2=1, s3=1, s4=1, s5=1) as r:
            for h in range(2):
                for j in range(3):
                    s = 3 * h + j
                    k.wait(nc.sync, r.step(k.v, s + 1))
                    m = k.slot[s](nc.sync.dma_start(wa[s][:, :], io["w_ada"][ds((r.i * 2 + h) * P, P), j * third:(j + 1) * third]))
                    part = acc[:, j * third:(j + 1) * third]
                    k.V(nc.vector.scalar_tensor_tensor, part, wa[s][:, :], cT[:, ds(r.i * 2 + h, 1)], part, ALU.mult, ALU.add,
                        after=[m, r.step(k.v, s - 2, ago=0) if h else r.step(k.v, s + 4)])
        done = k.now(k.v)
        k.wait(nc.tensor, *done)
        for j in range(6 * NK):
            t = nc.tensor.matmul(k.bank[0][:, j:j + 1], acc[:, j * P:(j + 1) * P], k.c("ones")[:, 0:1], start=True, stop=True)
        t = k.p(t)
        k.V(nc.vector.tensor_copy, mod[:, :], k.bank[0][:, 0:6 * NK], after=[t])
        for n, (gate, at) in enumerate(((gates[0], 2), (gates[1], 5))):
            for h in range(2):
                b = 1 + 2 * n + h
                t = k.p(nc.tensor.matmul(k.bank[b][:, :], k.c("ones"), acc[:, at * D + h * BANK:at * D + (h + 1) * BANK],
                                         start=True, stop=True))
                k.V(nc.vector.tensor_copy, gate[:, h * BANK:(h + 1) * BANK], k.bank[b][:, :], after=[t])
    k.meet()


def rotary_tables(k, cos, sin):
    nc, io = k.nc, k.io
    v = nc.vector
    two_pi = 2.0 * np.pi
    parts, rest = [], two_pi
    for bits in (6, 17):
        parts.append(np.floor(rest * 2.0 ** bits) / 2.0 ** bits)
        rest -= parts[-1]
    parts.append(rest)
    magic = 1.5 * 2.0 ** 23
    with ExitStack() as c:
        pos = c.enter_context(k.area([P, NT], I32))
        posf = c.enter_context(k.area([P, NT], F32))
        ang = c.enter_context(k.area([P, NT, DH // 2], F32))
        cnt = c.enter_context(k.area([P, NT, DH // 2], F32))
        red = c.enter_context(k.area([P, NT, DH // 2], F32))
        m = k.slot[0](nc.sync.dma_start(pos[:, :], io["positions"]))
        m = k.V(v.tensor_copy, posf[:, :], pos[:, :], after=[m])
        m = k.V(v.tensor_tensor, ang[:, :, :], wide(posf[:, :], 2, DH // 2), wide(k.c("inv_freq"), 1, NT), ALU.mult, after=[m])
        for out, turn in ((sin, 0.0), (cos, 0.25)):
            m = k.V(v.tensor_scalar, cnt[:, :, :], ang[:, :, :], 1.0 / two_pi, turn, ALU.mult, ALU.add, after=[m])
            m = k.V(v.tensor_scalar, cnt[:, :, :], cnt[:, :, :], magic, -magic, ALU.add, ALU.add, after=[m])
            src = ang
            for part in parts:
                m = k.V(v.scalar_tensor_tensor, red[:, :, :], cnt[:, :, :], -float(part), src[:, :, :], ALU.mult, ALU.add, after=[m])
                src = red
            m = k.V(v.tensor_scalar, red[:, :, :], red[:, :, :], turn * two_pi, np.pi, ALU.add, ALU.min, after=[m])
            m = k.V(v.tensor_scalar, red[:, :, :], red[:, :, :], -np.pi, None, ALU.max, after=[m])
            m = k.A(out[:, :, :], red[:, :, :], ACT.Sin, after=[m])
    k.meet()


def heads_norm(k, o, sq, ss, weight, gate, n, m, gate_mark):
    v = k.nc.vector
    h = o.shape[1]
    m = k.V(v.tensor_tensor, sq, o, o, ALU.mult, after=[m])
    yield
    m = k.V(v.tensor_reduce, ss, sq, AX.X, ALU.add, after=[m])
    yield
    m = rstd(k, ss, ss, n, m)
    yield
    m = k.V(v.tensor_tensor, o, o, wide(ss, 2, n), ALU.mult, after=[m])
    if weight is not None:
        yield
        m = k.V(v.tensor_tensor, o, o, wide(weight, 1, h), ALU.mult, after=[m])
    yield
    return k.V(v.tensor_tensor, o, o, gate, ALU.mult, after=[m, gate_mark])


def transposes(k, bank, src, n=4, after=()):
    nc = k.nc
    k.wait(nc.tensor, *after)
    for h in range(n):
        t = nc.tensor.transpose(bank[:, h * P:(h + 1) * P], src[:, h * P:(h + 1) * P], k.c("ident"))
    return k.p(t)


def retention(k, hT, mixT, cos, sin):
    nc, io = k.nc, k.io
    v = nc.vector
    with ExitStack() as c:
        sb = lambda *s: c.enter_context(k.area(list(s), F32))
        qkvg = sb(P, NT, 4 * BANK)

        def evacuate(chunk, m, bank, mark):
            dst = qkvg[:, m, ds(chunk * BANK, BANK)]
            if m % 2:
                k.V(v.tensor_copy, dst, bank[:, :], after=[mark])
            else:
                k.A(dst, bank[:, :], ACT.Copy, after=[mark])
        project(k, hT, io["w_in"], 0, 4, evacuate, v=4, a=4)

        two_of = lambda n: [sb(P, n) for _ in range(2)]
        qk, qkT, t1 = two_of(2 * BANK), two_of(2 * BANK), two_of(2 * BANK)
        kw, sT, o, sq, sg = (two_of(BANK) for _ in range(5))
        ss, state = two_of(RH), sb(P, BANK)
        zero = k.V(v.memset, state[:, :], 0.0)
        k.wait(nc.tensor, zero)
        k.wait(nc.gpsimd, zero)
        gamma = [1.0 - 2.0 ** (-5.0 - h) for h in range(RH)]
        kept = {}

        def tile(r, n, i):
            bank = k.bank[4 * n:4 * n + 4]
            row = qkvg[:, ds(i, 1), :].squeeze(1)
            x = row[:, 0:2 * BANK].rearrange("p (h t d) -> p h t d", h=2 * RH, t=2)
            x1, x2 = x[:, :, 0, :], x[:, :, 1, :]
            y = qk[n][:, :].rearrange("p (h t d) -> p h t d", h=2 * RH, t=2)
            t4 = t1[n][:, :].rearrange("p (t h d) -> p t h d", t=2, h=2 * RH)
            co = wide(cos[:, ds(i, 1), :].squeeze(1), 1, 2 * RH)
            si = wide(sin[:, ds(i, 1), :].squeeze(1), 1, 2 * RH)
            m1 = k.V(v.tensor_tensor, t4[:, 0], x2, si, ALU.mult)
            m = k.V(v.tensor_tensor, y[:, :, 0, :], x1, co, ALU.mult, after=[r.last(k.p)])
            first = k.V(v.tensor_tensor, y[:, :, 0, :], y[:, :, 0, :], t4[:, 0], ALU.subtract, after=[m, m1])
            m1 = k.G(nc.gpsimd.tensor_tensor, t4[:, 1], x1, si, ALU.mult)
            m = k.G(nc.gpsimd.tensor_tensor, y[:, :, 1, :], x2, co, ALU.mult, after=[r.last(k.p), r.last(k.v)])
            second = k.G(nc.gpsimd.tensor_tensor, y[:, :, 1, :], y[:, :, 1, :], t4[:, 1], ALU.add, after=[m, m1])
            gm = k.A(sg[n][:, :], row[:, 3 * BANK:], ACT.Silu, after=[r.last(k.v)])
            yield
            kwm = k.V(v.tensor_tensor, kw[n][:, :].rearrange("p (h d) -> p h d", h=RH),
                      qk[n][:, BANK:].rearrange("p (h d) -> p h d", h=RH), wide(k.c("ret_key"), 2, DH), ALU.mult, after=[first, second])
            ta = transposes(k, bank[0], qk[n][:, 0:BANK], after=[first, second, r.last(k.v), r.last(k.a)])
            tb = transposes(k, bank[1], qk[n][:, BANK:])
            ea = k.A(qkT[n][:, 0:BANK], bank[0][:, :], ACT.Copy, after=[ta])
            eb = k.V(v.tensor_copy, qkT[n][:, BANK:], bank[1][:, :], after=[tb])
            yield
            k.wait(nc.tensor, ea, eb)
            for h in range(RH):
                s = slice(h * P, (h + 1) * P)
                t = nc.tensor.matmul(bank[2][:, s], qkT[n][:, BANK + h * P:BANK + (h + 1) * P], qkT[n][:, s], start=True, stop=True)
            t = k.p(t)
            ms = k.V(v.tensor_tensor, sT[n][:, :], bank[2][:, :], k.c("ret_mask"), ALU.mult, after=[t])
            yield
            k.wait(nc.tensor, ms, kwm, *kept.get(n - 1, []))
            for h in range(RH):
                s = slice(h * P, (h + 1) * P)
                val = qkvg[:, ds(i, 1), 2 * BANK + h * P:2 * BANK + (h + 1) * P].squeeze(1)
                nc.tensor.matmul(bank[3][:, s], sT[n][:, s], val, start=True, stop=False)
                nc.tensor.matmul(bank[3][:, s], qkT[n][:, s], state[:, s], start=False, stop=True)
                t = nc.tensor.matmul(bank[0][:, s], kw[n][:, s], val, start=True, stop=True)
            t = k.p(t)
            for h in range(RH):
                s = slice(h * P, (h + 1) * P)
                m = k.V(v.scalar_tensor_tensor, state[:, s], state[:, s], float(gamma[h] ** RC), bank[0][:, s], ALU.mult, ALU.add,
                        after=[t] if h == 0 else [], chain=h == 0)
            kept[n] = [m]
            yield
            o3 = o[n][:, :].rearrange("p (h d) -> p h d", h=RH)
            m = k.V(v.tensor_tensor, o3, bank[3][:, :].rearrange("p (h d) -> p h d", h=RH), wide(k.c("ret_out"), 2, DH), ALU.mult)
            yield
            m = yield from heads_norm(k, o3, sq[n][:, :].rearrange("p (h d) -> p h d", h=RH), ss[n][:, :], None,
                                      sg[n][:, :].rearrange("p (h d) -> p h d", h=RH), DH, m, gm)
            t = transposes(k, bank[1], o[n][:, :], after=[m])
            yield
            k.A(mixT[:, 0:2, ds(i * P, P)], bank[1][:, 0:2 * P].rearrange("p (h t) -> p h t", h=2), ACT.Copy, after=[t])
            k.A(mixT[:, 2:4, ds(i * P, P)], bank[1][:, 2 * P:].rearrange("p (h t) -> p h t", h=2), ACT.Copy)

        with k.rounds(NT // 2, v=34, a=10, g=6, p=10) as r:
            interleave(*(tile(r, n, r.i * 2 + n) for n in range(2)))
    k.meet()


def channels(k, xT, w, col0, n_chunks, use, bank0=0, **per):
    nc = k.nc
    with ExitStack() as c:
        wbuf = [c.enter_context(k.area([P, NK, P], F32)) for _ in range(2)]
        with k.rounds(n_chunks // 2, s0=1, s1=1, **per) as r:
            for s in range(2):
                loaded = load_columns(k, s, wbuf[s][:, :, :], w, r.i * 2 * P + (col0 + s * P), P, after=[r.last(k.p)])
                k.wait(nc.tensor, loaded, r.last(k.v), r.last(k.a))
                banks = [k.bank[bank0 + 2 * s], k.bank[bank0 + 2 * s + 1]]
                for h in range(2):
                    for f in range(NK):
                        t = nc.tensor.matmul(banks[h][:, :], wbuf[s][:, f, :], xT[:, f, h * BANK:(h + 1) * BANK],
                                             start=f == 0, stop=f == NK - 1)
                use(r, r.i * 2 + s, s, banks, k.p(t))


def delta(k, hT, mixT):
    nc, io = k.nc, k.io
    v, g = nc.vector, nc.gpsimd
    hd = lambda ap: ap.rearrange("p (h d) -> p h d", d=DH)
    with ExitStack() as c:
        sb = lambda *s: c.enter_context(k.area(list(s), F32))
        dtok = sb(P, NT, 3 * BANK)
        z = sb(P, NT, BANK)
        ab = sb(P, NT, 2 * RH)

        def keep_z(chunk, m, bank, mark):
            k.A(z[:, m, :], bank[:, :], ACT.Silu, after=[mark])
        project(k, hT, io["w_in"], 7 * BANK, 1, keep_z, a=NT)

        with ExitStack() as c2:
            tail = c2.enter_context(k.area([P, NK, 2 * RH], F32))
            loaded = load_columns(k, 0, tail[:, :, :], io["w_in"], 8 * BANK, 2 * RH)
            k.wait(nc.tensor, loaded)
            for m in range(NT):
                for f in range(NK):
                    t = nc.tensor.matmul(k.bank[0][:, m * 8:m * 8 + 8], hT[:, f, m * P:(m + 1) * P], tail[:, f, :],
                                         start=f == 0, stop=f == NK - 1)
            t = k.p(t)
            k.V(v.tensor_copy, ab[:, :, :], k.bank[0][:, 0:NT * 8].rearrange("p (m e) -> p m e", m=NT), after=[t])
            k.meet()

        with ExitStack() as c2:
            sb2 = lambda *s: c2.enter_context(k.area(list(s), F32))
            cw = sb2(P, 12, 4)
            raw = [sb2(P, T + 3) for _ in range(2)]
            conv = [sb2(P, T) for _ in range(2)]
            m = k.slot[2](nc.sync.dma_start(cw[:, :, :], io["conv"]))
            for s in range(2):
                k.V(v.memset, raw[s][:, 0:3], 0.0, after=[m])
            k.wait(nc.scalar, *k.now(k.v))

            def use(r, j, s, banks, mark):
                m = k.A(raw[s][:, 3:3 + BANK], banks[0][:, :], ACT.Copy, after=[mark, r.last(k.v)])
                m = k.A(raw[s][:, 3 + BANK:], banks[1][:, :], ACT.Copy)
                w4 = cw[:, ds(j, 1), :].squeeze(1)
                m = k.V(v.tensor_scalar, conv[s][:, :], raw[s][:, 0:T], w4[:, 0:1], None, ALU.mult, after=[m, r.last(k.p)])
                for tap in range(1, 4):
                    m = k.V(v.scalar_tensor_tensor, conv[s][:, :], raw[s][:, tap:tap + T], w4[:, tap:tap + 1], conv[s][:, :],
                            ALU.mult, ALU.add, after=[m])
                m = k.A(conv[s][:, :], conv[s][:, :], ACT.Silu, after=[m])
                for h in range(2):
                    t = transposes(k, k.bank[4 + 2 * s + h], conv[s][:, h * BANK:(h + 1) * BANK], after=[m])
                    dst = dtok[:, 4 * h:4 * h + 4, ds(j * P, P)]
                    src = k.bank[4 + 2 * s + h][:, :].rearrange("p (m d) -> p m d", d=P)
                    if h:
                        k.V(v.tensor_copy, dst, src, after=[t])
                    else:
                        k.A(dst, src, ACT.Copy, after=[t])
            channels(k, hT, io["w_in"], 4 * BANK, 12, use, p=6, v=10, a=8)
            k.meet()

        beta, gl, gcum, egc, etail = (sb(P, NT, RH) for _ in range(5))
        gtot = sb(P, 2, NT, RH)
        u = [sb(P, NT, RH) for _ in range(3)]
        alog, dtb, dnw = sb(P, RH), sb(P, RH), sb(P, DH)
        k.slot[0](nc.sync.dma_start(alog[:, :], spread(io["a_log"], RH)))
        k.slot[0](nc.sync.dma_start(dtb[:, :], spread(io["dt_bias"], RH)))
        m = k.slot[0](nc.sync.dma_start(dnw[:, :], spread(io["dn_norm_w"], DH)))
        mb = k.A(beta[:, :, :], ab[:, :, RH:], ACT.Sigmoid, after=k.now(k.v))
        mx = k.V(v.tensor_tensor, u[0][:, :, :], ab[:, :, 0:RH], wide(dtb[:, :], 1, NT), ALU.add, after=[m])
        me = k.A(alog[:, :], alog[:, :], ACT.Exp, after=[m])
        m = k.A(u[1][:, :, :], u[0][:, :, :], ACT.Abs, after=[mx])
        m = k.A(u[1][:, :, :], u[1][:, :, :], ACT.Exp, scale=-1.0, after=[m])
        m = k.A(u[1][:, :, :], u[1][:, :, :], ACT.Ln, bias=1.0, after=[m])
        m = k.V(v.scalar_tensor_tensor, u[0][:, :, :], u[0][:, :, :], 0.0, u[1][:, :, :], ALU.max, ALU.add, after=[m])
        m = k.V(v.scalar_tensor_tensor, gl[:, :, :], u[0][:, :, :], -1.0, wide(alog[:, :], 1, NT), ALU.mult, ALU.mult, after=[m, me])
        k.wait(nc.tensor, m)
        glf = gl[:, :, :].rearrange("p m h -> p (m h)")
        for n, table in enumerate(("upto", "chunk", "half0", "half1")):
            t = nc.tensor.matmul(k.bank[0][:, n * 32:n * 32 + 32], k.c(table), glf, start=True, stop=True)
        t = k.p(t)
        part = lambda n: k.bank[0][:, n * 32:n * 32 + 32].rearrange("p (m h) -> p m h", h=RH)
        m = k.V(v.tensor_copy, gcum[:, :, :], part(0), after=[t])
        k.A(egc[:, :, :], gcum[:, :, :], ACT.Exp, after=[m])
        m = k.V(v.tensor_tensor, u[2][:, :, :], part(1), gcum[:, :, :], ALU.subtract, after=[m])
        k.A(etail[:, :, :], u[2][:, :, :], ACT.Exp, after=[m])
        k.A(gtot[:, 0], part(2), ACT.Exp)
        k.A(gtot[:, 1], part(3), ACT.Exp)

        def buffers(wide_ones, narrow_ones):
            z = dict(zip(("qk", "t1"), wide_ones))
            z.update(zip(("kb", "kbg", "vb", "kt", "gb", "qT", "kT", "kbT", "qgT", "eg", "dec", "B", "at"), narrow_ones))
            z.update(U=z["gb"], X=z["qT"], Y=z["kbT"], BM=z["kT"], nw=z["eg"], vn=z["kb"], o=z["t1"][:, 0:BANK], sq=z["t1"][:, BANK:])
            z.update(ss=sb(P, RH), ss8=sb(P, 2 * RH))
            return z
        first_set = buffers([sb(P, 2 * BANK)[:, :] for _ in range(2)], [sb(P, BANK)[:, :] for _ in range(13)])
        halves = [hT[:, f, h * BANK:(h + 1) * BANK] for f in range(2, NK) for h in range(2)]
        second_set = buffers([hT[:, f, :] for f in range(2)], halves + [sb(P, BANK)[:, :]])
        state = sb(P, BANK)
        k.V(v.memset, state[:, :], 0.0)
        k.meet()
        col = lambda ap, i: ap[:, ds(i, 1), :].squeeze(1)
        kept = {}

        def tile(r, n, i):
            bank = k.bank[4 * n:4 * n + 4]
            b = (first_set, second_set)[n]
            qk, t1, kb, kbg, vb, kt, gb = (b[x] for x in ("qk", "t1", "kb", "kbg", "vb", "kt", "gb"))
            qT, kT, kbT, qgT, eg, dec, B, at = (b[x] for x in ("qT", "kT", "kbT", "qgT", "eg", "dec", "B", "at"))
            BM, U, X, Y, nw, vn = (b[x] for x in ("BM", "U", "X", "Y", "nw", "vn"))
            o, sq, ss, ss8 = (b[x] for x in ("o", "sq", "ss", "ss8"))
            row = dtok[:, ds(i, 1), :].squeeze(1)
            bi, gi = col(beta, i), col(gcum, i)
            m = k.A(t1[:, :], row[:, 0:2 * BANK], ACT.Square, after=[r.last(k.v), r.last(k.p)])
            yield
            m = k.V(v.tensor_reduce, ss8[:, :], hd(t1[:, :]), AX.X, ALU.add, after=[m])
            yield
            m = rstd(k, ss8[:, :], ss8[:, :], 1, m)
            yield
            m = k.V(v.tensor_tensor, ss8[:, :], ss8[:, :], k.c("qk_scale"), ALU.mult, after=[m])
            mq = k.V(v.tensor_tensor, hd(qk[:, :]), hd(row[:, 0:2 * BANK]), wide(ss8[:, :], 2, DH), ALU.mult,
                     after=[m, r.last(k.p), r.last(k.g)])
            mkb = k.V(v.tensor_tensor, hd(kb[:, :]), hd(qk[:, BANK:]), wide(bi, 2, DH), ALU.mult, after=[mq])
            yield
            mg = k.G(g.tensor_tensor, hd(gb[:, :]), wide(k.c("ones"), 1, RH), wide(col(gl, i), 2, P), ALU.mult, after=[r.last(k.p)])
            mvb = k.G(g.tensor_tensor, hd(vb[:, :]), hd(row[:, 2 * BANK:]), wide(bi, 2, DH), ALU.mult)
            mkt = k.G(g.tensor_tensor, hd(kt[:, :]), hd(qk[:, BANK:]), wide(col(etail, i), 2, DH), ALU.mult, after=[mq])
            mkg = k.G(g.tensor_tensor, hd(kbg[:, :]), hd(kb[:, :]), wide(col(egc, i), 2, DH), ALU.mult, after=[mkb])
            k.wait(nc.tensor, mg, r.last(k.v), r.last(k.a))
            for h in range(RH):
                t = nc.tensor.matmul(bank[3][:, h * P:(h + 1) * P], gb[:, h * P:(h + 1) * P], k.c("upto"), start=True, stop=True)
            t = k.p(t)
            yield
            me = k.A(eg[:, :], bank[3][:, :], ACT.Exp, after=[t, mq])
            m = k.V(v.tensor_tensor, hd(dec[:, :]), hd(bank[3][:, :]), wide(gi, 2, P), ALU.subtract, after=[t, me])
            m = k.V(v.tensor_scalar, dec[:, :], dec[:, :], 0.0, None, ALU.min, after=[m])
            mdec = m
            yield
            m = k.A(dec[:, :], dec[:, :], ACT.Exp, after=[m])
            yield
            md = k.G(g.tensor_tensor, hd(dec[:, :]), hd(dec[:, :]), wide(k.c("upto"), 1, RH), ALU.mult, after=[m])
            ta = transposes(k, bank[0], qk[:, 0:BANK], after=[mq])
            tb = transposes(k, bank[1], qk[:, BANK:])
            tc = transposes(k, bank[2], kb[:, :], after=[mkb])
            yield
            ea = k.A(qT[:, :], bank[0][:, :], ACT.Copy, after=[ta])
            eb = k.A(kT[:, :], bank[1][:, :], ACT.Copy, after=[tb])
            ec = k.A(kbT[:, :], bank[2][:, :], ACT.Copy, after=[tc])
            mqg = k.V(v.tensor_tensor, qgT[:, :], bank[0][:, :], eg[:, :], ALU.mult, after=[ta, me, ea])
            yield
            k.wait(nc.tensor, ea, eb, ec, mdec)
            for h in range(RH):
                s = slice(h * P, (h + 1) * P)
                nc.tensor.matmul(bank[3][:, s], kT[:, s], kbT[:, s], start=True, stop=True)
                t = nc.tensor.matmul(bank[2][:, s], kT[:, s], qT[:, s], start=True, stop=True)
            t = k.p(t)
            yield
            mB = k.V(v.tensor_tensor, B[:, :], bank[3][:, :], dec[:, :], ALU.mult, after=[t, md])
            mat = k.V(v.tensor_tensor, at[:, :], bank[2][:, :], dec[:, :], ALU.mult)
            mm = k.V(v.tensor_tensor, hd(BM[:, :]), hd(B[:, :]), wide(k.c("level1"), 1, RH), ALU.mult, after=[mB])
            mu = k.V(v.scalar_tensor_tensor, hd(U[:, :]), hd(BM[:, :]), -1.0, wide(k.c("ident"), 1, RH), ALU.mult, ALU.add, after=[mm])
            t = transposes(k, bank[1], BM[:, :], after=[mm, eb])
            yield
            mx = k.V(v.scalar_tensor_tensor, hd(X[:, :]), hd(bank[1][:, :]), -1.0, wide(k.c("ident"), 1, RH), ALU.mult, ALU.add, after=[t])
            for b in LEVELS[1:]:
                last = b == LEVELS[-1]
                mm = k.V(v.tensor_tensor, hd(BM[:, :]), hd(B[:, :]), wide(k.c(f"level{b}"), 1, RH), ALU.mult)
                yield
                k.wait(nc.tensor, mm, mx, mu, mat)
                for h in range(RH):
                    s = slice(h * P, (h + 1) * P)
                    t = nc.tensor.matmul(bank[2][:, s], BM[:, s], X[:, s], start=True, stop=True)
                t = k.p(t)
                yield
                my = k.A(Y[:, :], bank[2][:, :], ACT.Copy, after=[t])
                k.wait(nc.tensor, my)
                for h in range(RH):
                    s = slice(h * P, (h + 1) * P)
                    if not last:
                        nc.tensor.matmul(bank[1][:, s], U[:, s], Y[:, s], start=True, stop=True)
                    t = nc.tensor.matmul(bank[3][:, s], Y[:, s], U[:, s], start=True, stop=True)
                t = k.p(t)
                yield
                mu = k.V(v.tensor_tensor, U[:, :], U[:, :], bank[3][:, :], ALU.subtract, after=[t])
                if not last:
                    mx = k.V(v.tensor_tensor, X[:, :], X[:, :], bank[1][:, :], ALU.subtract)
            yield
            k.wait(nc.tensor, mu, mkg, mvb, mkt)
            for h in range(RH):
                s = slice(h * P, (h + 1) * P)
                t = nc.tensor.matmul(bank[2][:, s], kbg[:, s], U[:, s], start=True, stop=True)
            t = k.p(t)
            yield
            mw = k.A(nw[:, :], bank[2][:, :], ACT.Copy, scale=-1.0, after=[t])
            yield
            while n and not kept:
                yield
            k.wait(nc.tensor, mw, mqg, mat, *(kept["state"] if n else []))
            for q in range(2):
                rows = slice(q * DC, (q + 1) * DC)
                for h in range(RH):
                    s = slice(h * P, (h + 1) * P)
                    cs = slice(h * P + q * DC, h * P + (q + 1) * DC)
                    nc.tensor.matmul(bank[0][rows, s], U[:, cs], vb[:, s], start=True, stop=False)
                    t = nc.tensor.matmul(bank[0][rows, s], nw[:, cs], state[:, s], start=False, stop=True)
                t = k.p(t)
                yield
                mv = k.A(vn[rows, :], bank[0][rows, :], ACT.Copy, after=[t])
                yield
                k.wait(nc.tensor, mv)
                for h in range(RH):
                    s = slice(h * P, (h + 1) * P)
                    cs = slice(h * P + q * DC, h * P + (q + 1) * DC)
                    t = nc.tensor.matmul(bank[1 + q][:, s], kt[rows, s], vn[rows, s], start=True, stop=True)
                t = k.p(t)
                for h in range(RH):
                    s = slice(h * P, (h + 1) * P)
                    cs = slice(h * P + q * DC, h * P + (q + 1) * DC)
                    nc.tensor.matmul(bank[3][rows, s], qgT[:, cs], state[:, s], start=True, stop=False)
                    to = nc.tensor.matmul(bank[3][rows, s], at[rows, cs], vn[rows, s], start=False, stop=True)
                to = k.p(to)
                yield
                for h in range(RH):
                    s = slice(h * P, (h + 1) * P)
                    ms = k.V(v.scalar_tensor_tensor, state[:, s], state[:, s], gtot[:, q, ds(i, 1), h:h + 1].squeeze(1),
                             bank[1 + q][:, s], ALU.mult, ALU.add, after=[t, to] if h == 0 else [], chain=h == 0)
                yield
                k.wait(nc.tensor, ms)
            if not n:
                kept["state"] = [ms]
            m = k.V(v.tensor_copy, o[:, :], bank[3][:, :], after=[to])
            yield
            m = yield from heads_norm(k, hd(o[:, :]), hd(sq[:, :]), ss[:, :], dnw[:, :], hd(col(z, i)), DH, m, to)
            t = transposes(k, bank[0], o[:, :], after=[m])
            yield
            k.A(mixT[:, 4:6, ds(i * P, P)], bank[0][:, 0:2 * P].rearrange("p (h t) -> p h t", h=2), ACT.Copy, after=[t])
            k.A(mixT[:, 6:8, ds(i * P, P)], bank[0][:, 2 * P:].rearrange("p (h t) -> p h t", h=2), ACT.Copy)

        with k.rounds(NT // 2, v=88, a=36, g=10, p=48) as r:
            interleave(*(tile(r, n, r.i * 2 + n) for n in range(2)))
    k.meet()


def residual(k, mixT, w, x, gate):
    nc = k.nc
    with ExitStack() as c:
        tmp = [c.enter_context(k.area([P, BANK], F32)) for _ in range(2)]

        pending = {0: [], 1: []}

        def add(chunk, m, bank, mark):
            dst = x[:, m, chunk * BANK:(chunk + 1) * BANK]
            if gate is None:
                k.V(nc.vector.tensor_tensor, dst, dst, bank[:, :], ALU.add, after=[mark])
                return
            t = tmp[m % 2]
            a = k.V(nc.vector.tensor_tensor, t[:, :], bank[:, :], gate[:, chunk * BANK:(chunk + 1) * BANK], ALU.mult,
                    after=[mark] + pending[m % 2])
            pending[m % 2] = [k.G(nc.gpsimd.tensor_tensor, dst, dst, t[:, :], ALU.add, after=[a])]
        project(k, mixT, w, 0, 2, add)


def route(k, h2T, gates, where, tokens, experts):
    nc, io = k.nc, k.io
    v = nc.vector
    NL = GROUPS + NE
    with ExitStack() as c:
        sb = lambda *s, dt=F32: c.enter_context(k.area(list(s), dt))
        wr, br = sb(P, NK, NL), sb(P, NL)
        lg, eq = sb(P, NT, NL), sb(P, NT, NE)
        gp, top, ix, ixf = sb(P, NT, 8), sb(P, NT, 8), sb(P, NT, 8, dt=U32), sb(P, NT, 8)
        sel = sb(P, NT, PER_GROUP)
        hot = sb(P, 2, NT, NE)
        both = sb(P, NT, NE)
        a1, a2, a3 = sb(P, NT), sb(P, NT), sb(P, NT)
        k.slot[0](nc.sync.dma_start(wr[:, :, 0:GROUPS], io["w_group"].rearrange("(k p) c -> p k c", p=P)))
        k.slot[0](nc.sync.dma_start(wr[:, :, GROUPS:], io["w_expert"].rearrange("(k p) c -> p k c", p=P)))
        k.slot[0](nc.sync.dma_start(br[:, 0:GROUPS], spread(io["b_group"], GROUPS)))
        loaded = k.slot[0](nc.sync.dma_start(br[:, GROUPS:], spread(io["b_expert"], NE)))
        k.wait(nc.tensor, loaded)
        for m in range(NT):
            for f in range(NK):
                t = nc.tensor.matmul(k.bank[0][:, m * NL:(m + 1) * NL], h2T[:, f, m * P:(m + 1) * P], wr[:, f, :],
                                     start=f == 0, stop=f == NK - 1)
        t = k.p(t)
        m = k.V(v.tensor_tensor, lg[:, :, :], k.bank[0][:, 0:NT * NL].rearrange("p (m e) -> p m e", m=NT),
                wide(br[:, :], 1, NT), ALU.add, after=[t, loaded])
        m1 = k.V(v.memset, gp[:, :, :], NEG)
        m = k.V(v.tensor_copy, gp[:, :, 0:GROUPS], lg[:, :, 0:GROUPS], after=[m, m1])
        for n in range(NT):
            mt = k.V(v.max, top[:, n, :], gp[:, n, :], after=[m])
            mi = k.V(v.max_index, ix[:, n, :], top[:, n, :], gp[:, n, :], after=[mt])
        m = k.V(v.tensor_copy, ixf[:, :, 0:1], ix[:, :, 0:1], after=[mi])
        m2 = k.V(v.tensor_tensor, gp[:, :, 0:GROUPS], gp[:, :, 0:GROUPS], top[:, :, 0:1].broadcast_to([P, NT, GROUPS]), ALU.subtract, after=[mi])
        m2 = k.A(gp[:, :, 0:GROUPS], gp[:, :, 0:GROUPS], ACT.Exp, after=[m2])
        mz = k.V(v.tensor_reduce, a1[:, :], gp[:, :, 0:GROUPS], AX.X, ALU.add, after=[m2])
        me = k.V(v.tensor_tensor, eq[:, :, 0:GROUPS], wide(k.c("row")[:, 0:GROUPS], 1, NT), ixf[:, :, 0:1].broadcast_to([P, NT, GROUPS]), ALU.is_equal, after=[m])
        for n in range(GROUPS):
            src = lg[:, :, GROUPS + n * PER_GROUP:GROUPS + (n + 1) * PER_GROUP]
            pick = eq[:, :, n:n + 1].broadcast_to([P, NT, PER_GROUP])
            if n == 0:
                ms = k.V(v.tensor_tensor, sel[:, :, :], src, pick, ALU.mult, after=[me])
            else:
                mp = k.V(v.tensor_tensor, both[:, :, 0:PER_GROUP], src, pick, ALU.mult, after=[ms])
                ms = k.V(v.tensor_tensor, sel[:, :, :], sel[:, :, :], both[:, :, 0:PER_GROUP], ALU.add, after=[mp])
        base = k.V(v.tensor_scalar, a2[:, :], ixf[:, :, 0:1].squeeze(2), float(PER_GROUP), None, ALU.mult, after=[ms])
        for n in range(NT):
            mt = k.V(v.max, top[:, n, :], sel[:, n, :], after=[ms, base])
            mi = k.V(v.max_index, ix[:, n, :], top[:, n, :], sel[:, n, :], after=[mt])
        m = k.V(v.tensor_copy, ixf[:, :, 0:2], ix[:, :, 0:2], after=[mi])
        m = k.V(v.tensor_tensor, ixf[:, :, 0:2], ixf[:, :, 0:2], wide(a2[:, :], 2, 2), ALU.add, after=[m])
        md = k.V(v.tensor_tensor, a2[:, :], top[:, :, 1:2].squeeze(2), top[:, :, 0:1].squeeze(2), ALU.subtract, after=[m])
        md = k.A(a2[:, :], a2[:, :], ACT.Exp, after=[md])
        ms = k.V(v.scalar_tensor_tensor, a3[:, :], a2[:, :], 1.0, a1[:, :], ALU.add, ALU.mult, after=[md, mz])
        ms = k.V(v.reciprocal, gates[:, :, 0:1].squeeze(2), a3[:, :], after=[ms])
        k.V(v.tensor_tensor, gates[:, :, 1:2].squeeze(2), gates[:, :, 0:1].squeeze(2), a2[:, :], ALU.mult, after=[ms])
        for j in range(2):
            mh = k.V(v.tensor_tensor, hot[:, j], wide(k.c("row")[:, 0:NE], 1, NT), ixf[:, :, j:j + 1].broadcast_to([P, NT, NE]), ALU.is_equal, after=[m])
        m = k.V(v.tensor_tensor, both[:, :, :], hot[:, 0], hot[:, 1], ALU.add, after=[mh])
        k.wait(nc.tensor, m)
        for n in range(NT):
            for q in range(n + 1):
                t = nc.tensor.matmul(k.bank[1][:, n * NE:(n + 1) * NE], k.c("before" if q == n else "ones"), both[:, q, :],
                                     start=q == 0, stop=q == n)
        for q in range(NT):
            t = nc.tensor.matmul(k.bank[2][:, 0:NE], k.c("ones"), both[:, q, :], start=q == 0, stop=q == NT - 1)
        t = k.p(t)
        cnt, full = sb(P, NE, NT), sb(P, NE)
        upto = [sb(P, NE + 16) for _ in range(2)]
        first = sb(P, NE)
        m = k.V(v.tensor_tensor, cnt[:, :, :], k.bank[2][:, 0:NE].unsqueeze(2).broadcast_to([P, NE, NT]), wide(k.c("steps"), 1, NE), ALU.is_gt, after=[t])
        m = k.V(v.tensor_reduce, full[:, :], cnt[:, :, :], AX.X, ALU.add, after=[m])
        m = k.V(v.memset, upto[0][:, 0:16], 0.0)
        m = k.V(v.memset, upto[1][:, 0:16], 0.0)
        m = k.V(v.tensor_copy, upto[0][:, 16:], full[:, :], after=[m])
        for n, d in enumerate((1, 2, 4, 8, 16)):
            src, dst = upto[n % 2], upto[(n + 1) % 2]
            m = k.V(v.tensor_tensor, dst[:, 16:], src[:, 16:], src[:, 16 - d:16 - d + NE], ALU.add, after=[m])
        total = dst[:, 16:]
        m = k.V(v.tensor_tensor, first[:, :], total, full[:, :], ALU.subtract, after=[m])
        blk = sb(P, BLOCKS, NE)
        ef = sb(P, BLOCKS)
        m1 = k.V(v.tensor_tensor, blk[:, :, :], wide(total, 1, BLOCKS), k.c("row")[:, 0:BLOCKS].unsqueeze(2).broadcast_to([P, BLOCKS, NE]), ALU.is_le, after=[m])
        m1 = k.V(v.tensor_reduce, ef[:, :], blk[:, :, :], AX.X, ALU.add, after=[m1])
        m1 = k.V(v.tensor_scalar, ef[:, :], ef[:, :], float(NE - 1), None, ALU.min, after=[m1])
        k.V(v.tensor_copy, experts[:, 0:BLOCKS], ef[:, :], after=[m1])
        k.V(v.tensor_copy, experts[:, BLOCKS:], total[:, NE - 1:NE])
        rank, div, w2 = sb(P, NT), sb(P, NT), sb(P, NT, NE)
        row_of, blk_of = sb(P, NT, 2), sb(P, NT, 2)
        hp, hb = [sb(P, P) for _ in range(2)], [sb(P, BLOCKS) for _ in range(2)]
        pos = sb(P, NT, 2)
        ranks = k.bank[1][:, 0:NT * NE].rearrange("p (m e) -> p m e", m=NT)
        for j in range(2):
            m = k.V(v.tensor_tensor, w2[:, :, :], ranks, hot[:, j], ALU.mult, after=[m])
            mr = k.V(v.tensor_reduce, rank[:, :], w2[:, :, :], AX.X, ALU.add, after=[m])
            m = k.V(v.tensor_tensor, w2[:, :, :], wide(first[:, :], 1, NT), hot[:, j], ALU.mult, after=[mr])
            m = k.V(v.tensor_reduce, a1[:, :], w2[:, :, :], AX.X, ALU.add, after=[m])
            m = k.V(v.tensor_tensor, w2[:, :, 0:NT - 1], wide(rank[:, :], 2, NT - 1), wide(k.c("steps")[:, 1:NT], 1, NT), ALU.is_ge, after=[m])
            m = k.V(v.tensor_reduce, div[:, :], w2[:, :, 0:NT - 1], AX.X, ALU.add, after=[m])
            m = k.V(v.scalar_tensor_tensor, row_of[:, :, j:j + 1].squeeze(2), div[:, :], -float(P), rank[:, :], ALU.mult, ALU.add, after=[m])
            m = k.V(v.tensor_tensor, blk_of[:, :, j:j + 1].squeeze(2), div[:, :], a1[:, :], ALU.add, after=[m])
        m = k.V(v.scalar_tensor_tensor, pos[:, :, :], blk_of[:, :, :], float(P), row_of[:, :, :], ALU.mult, ALU.add, after=[m])
        k.V(v.tensor_copy, where[:, :, :], pos[:, :, :], after=[m])
        t = None
        for n in range(NT):
            for j in range(2):
                free = [t] if t is not None else []
                m1 = k.V(v.tensor_scalar, hp[j][:, :], k.c("row"), row_of[:, n, j:j + 1], None, ALU.is_equal, after=[m] + free)
                m2 = k.V(v.tensor_scalar, hb[j][:, :], k.c("row")[:, 0:BLOCKS], blk_of[:, n, j:j + 1], k.c("token")[:, n:n + 1],
                         ALU.is_equal, ALU.mult)
                k.wait(nc.tensor, m1, m2)
                t = k.p(nc.tensor.matmul(k.bank[3][:, 0:BLOCKS], hp[j][:, :], hb[j][:, :], start=n + j == 0, stop=n + j == NT))
        k.V(v.tensor_copy, tokens[:, 0:BLOCKS], k.bank[3][:, 0:BLOCKS], after=[t])
        k.V(v.memset, tokens[:, BLOCKS:], 0)
    k.meet()


def experts_pass(k, scale, shift, tokens, experts, xn, ys):
    nc, io = k.nc, k.io
    v, pe, sy, gp = nc.vector, nc.tensor, nc.sync, nc.gpsimd
    with ExitStack() as c:
        sb = lambda *s, dt=F32: c.enter_context(k.area(list(s), dt))
        w1 = [sb(P, NK, DE) for _ in range(2)]
        w3 = [sb(P, NK, DE) for _ in range(2)]
        w2 = [sb(P, DE // P, D) for _ in range(2)]
        rows = [sb(P, D) for _ in range(2)]
        idx = [sb(P, 1, dt=U32) for _ in range(2)]
        xsT = [sb(P, NK, P) for _ in range(2)]
        act, hid, hidT = (sb(P, DE) for _ in range(3))
        y = [sb(P, D) for _ in range(2)]

        PE_STEPS, ACT_STEPS, VEC_STEPS = 6, 7, 6

        def gather(at, s, after):
            m = k.G(gp.tensor_copy, idx[s][:, :], tokens[:, ds(at, 1)], after=after)
            k.wait(gp, m)
            k.settled(gp)
            return k.soft[s](gp.indirect_dma_start(out=rows[s][:, :], out_offset=None, in_=xn[:, :],
                                                   in_offset=bass.IndirectOffsetOnAxis(ap=idx[s][:, 0:1], axis=0)))

        def turn(s, half):
            return transposes(k, k.bank[half], rows[s][:, half * BANK:(half + 1) * BANK])

        def rows_out(s, half, t, before):
            for q in range(4):
                f = half * 4 + q
                src = k.bank[half][:, q * P:(q + 1) * P]
                if half:
                    m = k.V(v.tensor_scalar, xsT[s][:, f, :], src, scale[:, f:f + 1], shift[:, f:f + 1], ALU.mult, ALU.add,
                            after=[t] + before)
                else:
                    m = k.A(xsT[s][:, f, :], src, ACT.Identity, scale=scale[:, f:f + 1], bias=shift[:, f:f + 1], after=[t] + before)
            return m

        used_t = pe.value_load(experts[0:1, BLOCKS:BLOCKS + 1], min_val=0, max_val=BLOCKS)
        used_s = sy.value_load(experts[0:1, BLOCKS:BLOCKS + 1], min_val=0, max_val=BLOCKS)
        got = gather(0, 0, [])
        k.wait(pe, got)
        for half in range(2):
            rows_out(0, half, turn(0, half), [])
        k.wait(pe, *k.now(k.v, k.a))
        k.wait(gp, *k.now(k.p))
        with k.rounds(BLOCKS // 2, s0=2, s1=2, s2=1, s3=1, s4=1, s5=1, q0=1, q1=1, g=2,
                      v=2 * VEC_STEPS, a=2 * ACT_STEPS, p=2 * PE_STEPS) as r:
            for s in range(2):
                at = r.i * 2 + s
                n = 1 - s
                there = used_s > at
                e = sy.value_load(experts[0:1, ds(at, 1)], min_val=0, max_val=NE - 1)
                for m in (r.step(k.p, PE_STEPS * s + 2), *k.now(k.slot[s], k.slot[2 + s])):
                    k.wait(sy, m)
                    k.settled(sy)
                k.slot[s](sy.dma_start(w1[s][:, :, :], io["w1"][ds(e, 1)].squeeze(0).rearrange("(k p) f -> p k f", p=P),
                                       cond=there, bounds_check="skip_entire_dma"))
                up = k.slot[s](sy.dma_start(w3[s][:, :, :], io["w3"][ds(e, 1)].squeeze(0).rearrange("(k p) f -> p k f", p=P),
                                            cond=there, bounds_check="skip_entire_dma"))
                k.wait(sy, r.step(k.p, PE_STEPS * s + 6))
                k.settled(sy)
                down = k.slot[2 + s](sy.dma_start(w2[s][:, :, :], io["w2"][ds(e, 1)].squeeze(0).rearrange("(k p) f -> p k f", p=P),
                                                  cond=there, bounds_check="skip_entire_dma"))
                got = gather(at + 1, n, [r.step(k.p, PE_STEPS * s + 5)])
                with k.only(pe, used_t > at, k.p, PE_STEPS, after=[got]):
                    if s:
                        k.wait(pe, up, rowed[0], rowed[1])
                    else:
                        k.wait(pe, up, r.step(k.a, ACT_STEPS + 5), r.step(k.v, VEC_STEPS + 5))
                    ts = []
                    for j, w in enumerate((w1[s], w3[s])):
                        for f in range(NK):
                            t = pe.matmul(k.bank[2 + j][:, :], xsT[s][:, f, :], w[:, f, :], start=f == 0, stop=f == NK - 1)
                        ts.append(k.p(t))
                    k.wait(pe, got)
                    t0 = turn(n, 0)
                    k.wait(pe, Mark(k.v, k.v.count + 1, r))
                    th = transposes(k, k.bank[4], hid[:, :])
                    t1 = turn(n, 1)
                    k.wait(pe, Mark(k.a, k.a.count + 6, r), down)
                    for h in range(2):
                        for f in range(DE // P):
                            t = pe.matmul(k.bank[5 + h][:, :], hidT[:, f * P:(f + 1) * P], w2[s][:, f, h * BANK:(h + 1) * BANK],
                                          start=f == 0, stop=f == DE // P - 1)
                    td = k.p(t)
                ma = k.A(act[:, :], k.bank[2][:, :], ACT.Silu, after=[ts[0], Mark(k.v, k.v.count - 5, r)])
                k.V(v.tensor_tensor, hid[:, :], act[:, :], k.bank[3][:, :], ALU.mult, after=[ma, ts[1]])
                rowed = [rows_out(n, 0, t0, [ts[1]]), rows_out(n, 1, t1, [ts[1]])]
                k.A(hidT[:, :], k.bank[4][:, :], ACT.Copy, after=[th])
                m1 = k.A(y[s][:, 0:BANK], k.bank[5][:, :], ACT.Copy, after=[td, r.last(k.slot[4 + s])])
                m2 = k.V(v.tensor_copy, y[s][:, BANK:], k.bank[6][:, :], after=[td, r.last(k.slot[4 + s])])
                k.wait(nc.scalar, m1, m2)
                k.slot[4 + s](nc.scalar.dma_start(ys[ds(at * P, P), :], y[s][:, :]))
    k.meet()


def combine(k, x, gates, where, ys, gate2, norm_w):
    nc = k.nc
    v = nc.vector
    with ExitStack() as c:
        sb = lambda *s, dt=F32: c.enter_context(k.area(list(s), dt))
        y = [[sb(P, D) for _ in range(2)] for _ in range(2)]
        idx = [[sb(P, 1, dt=U32) for _ in range(2)] for _ in range(2)]
        sq, ss = sb(P, D), sb(P, 2)
        with k.rounds(NT // 2, q0=2, q1=2, v=18, a=4) as r:
            for s in range(2):
                n = r.i * 2 + s
                xt = x[:, ds(n, 1), :].squeeze(1)
                for j in range(2):
                    mi = k.V(v.tensor_copy, idx[s][j][:, :], where[:, ds(n, 1), j:j + 1].squeeze(1), after=[r.last(k.soft[s])])
                    k.wait(nc.gpsimd, mi)
                    k.settled(nc.gpsimd)
                    got = k.soft[s](nc.gpsimd.indirect_dma_start(
                        out=y[s][j][:, :], out_offset=None, in_=ys[:, :],
                        in_offset=bass.IndirectOffsetOnAxis(ap=idx[s][j][:, 0:1], axis=0)))
                gt = gates[:, ds(n, 1), :].squeeze(1)
                m = k.V(v.tensor_scalar, y[s][0][:, :], y[s][0][:, :], gt[:, 0:1], None, ALU.mult, after=[got])
                m = k.V(v.scalar_tensor_tensor, y[s][0][:, :], y[s][1][:, :], gt[:, 1:2], y[s][0][:, :], ALU.mult, ALU.add, after=[m])
                m = k.V(v.tensor_tensor, y[s][0][:, :], y[s][0][:, :], gate2[:, :], ALU.mult, after=[m])
                mx = k.V(v.tensor_tensor, xt, xt, y[s][0][:, :], ALU.add, after=[m])
                m = k.A(sq[:, :], xt, ACT.Square, accum_out=ss[:, 0:1], after=[mx])
                m = rstd(k, ss[:, 1:2], ss[:, 0:1], D, m)
                k.V(v.scalar_tensor_tensor, xt, xt, ss[:, 1:2], norm_w[:, :], ALU.mult, ALU.mult, after=[m])
    k.meet()


def neighbourhood(k, nT, mixT, scratch):
    nc, io = k.nc, k.io
    v = nc.vector
    pairs = NAH // 2
    dr_w = (2 * KH - 1) * W
    with ExitStack() as c:
        sb = lambda *s: c.enter_context(k.area(list(s), F32))
        qkT = sb(P, 2 * pairs, T)
        val = sb(P, ROWS, BANK)

        def keep(r, j, s, banks, mark):
            m = k.A(qkT[:, ds(j, 1), 0:BANK].squeeze(1), banks[0][:, :], ACT.Copy, after=[mark])
            k.V(v.tensor_copy, qkT[:, ds(j, 1), BANK:].squeeze(1), banks[1][:, :], after=[mark])
        channels(k, nT, io["w_in_2"], 0, 2 * pairs, keep, p=2, v=2, a=2)
        k.meet()

        def keep_v(chunk, m, bank, mark):
            k.A(val[:, 2 * m, :], bank[:, :], ACT.Copy, after=[mark])
        project(k, nT, io["w_in_2"], 2 * BANK, 1, keep_v, a=NT)
        vv = val[:, :, :].rearrange("p (m t) c -> p m t c", t=2)
        for lo, hi, src in ((0, W, vv[W:P, 0:NT, 0, :]), (W, P, vv[0:W, 1:NT, 0, :])):
            n = NT if lo == 0 else NT - 1
            m = k.slot[0](nc.sync.dma_start(vv[lo:hi, 0:n, 1, :], src))
        bias = sb(P, pairs, dr_w)
        RW = 2 * W - 1
        k.slot[1](nc.sync.dma_start(scratch, wide(io["rpb"], 2, W)))
        k.wait(nc.sync, *k.now(k.slot[1]))
        for h in range(NAH):
            src = bass.AP(scratch.tensor, scratch.offset + h * (2 * KH - 1) * W * RW + W - 1, [[RW - 1, W], [W * RW, 2 * KH - 1], [1, W]])
            dst = bias[(h % 2) * W:(h % 2 + 1) * W, h // 2, :].rearrange("p (r c) -> p r c", c=W)
            m = k.slot[0](nc.sync.dma_start(dst, src))
        q2, ob = [sb(P, P) for _ in range(pairs)], [sb(P, P) for _ in range(pairs)]
        sc, pT = [sb(P, KH * W) for _ in range(pairs)], [sb(P, KH * W) for _ in range(pairs)]
        st = [sb(P, 4) for _ in range(pairs)]
        for p in range(pairs):
            k.V(v.memset, q2[p][:, :], 0.0, after=[m])
            b3 = bias[:, p, :].rearrange("p (r c) -> p r c", c=W)
            k.V(v.tensor_tensor, b3, b3, wide(k.c("window"), 1, 2 * KH - 1), ALU.add)
        k.meet()

        def pair(r, p, i, lo, dr):
            one, two = k.bank[2 * p], k.bank[2 * p + 1]
            k.A(q2[p][0:W, 0:W], qkT[0:W, p, ds(i * W, W)], ACT.Copy, scale=NAD ** -0.5, after=[r.step(k.p, p + 1)])
            m = k.A(q2[p][W:P, W:P], qkT[W:P, p, ds(i * W, W)], ACT.Copy, scale=NAD ** -0.5)
            k.wait(nc.tensor, m)
            t = k.p(nc.tensor.matmul(one[:, :], q2[p][:, :], qkT[:, pairs + p, ds(lo * W, KH * W)], start=True, stop=True))
            yield
            m = k.V(v.tensor_tensor, sc[p][:, :], one[:, :], bias[:, p, ds(dr * W, KH * W)], ALU.add, after=[t, r.last(k.p)])
            yield
            m = k.V(v.tensor_reduce, st[p][:, 0:1], sc[p][:, :], AX.X, ALU.max, after=[m])
            yield
            m = k.V(v.tensor_scalar, st[p][:, 1:2], st[p][:, 0:1], -1.0, None, ALU.mult, after=[m])
            m = k.A(sc[p][:, :], sc[p][:, :], ACT.Exp, bias=st[p][:, 1:2], accum_out=st[p][:, 2:3], after=[m])
            yield
            mr = k.V(v.reciprocal, st[p][:, 3:4], st[p][:, 2:3], after=[m])
            t = transposes(k, two, sc[p][:, :], after=[m])
            yield
            m = k.V(v.tensor_copy, pT[p][:, :], two[:, :], after=[t])
            yield
            k.wait(nc.tensor, m)
            for q in range(4):
                t = nc.tensor.matmul(one[:, 0:P], pT[p][:, q * P:(q + 1) * P],
                                     val[:, ds(lo + 2 * q, 1), p * P:(p + 1) * P].squeeze(1), start=q == 0, stop=q == 3)
            t = k.p(t)
            yield
            m = k.A(ob[p][:, :], one[:, 0:P], ACT.Copy, scale=st[p][:, 3:4], after=[t, mr])
            yield
            k.wait(nc.tensor, m)
            t = k.p(nc.tensor.transpose(two[:, 0:P], ob[p][:, :], k.c("ident")))
            yield
            k.A(mixT[0:W, p, ds(i * W, W)], two[0:W, 0:W], ACT.Copy, after=[t])
            k.A(mixT[W:P, p, ds(i * W, W)], two[W:P, W:P], ACT.Copy)

        with k.rounds(ROWS, p=4 * pairs, v=5 * pairs, a=6 * pairs) as r:
            lo = window_start(k, r.i)
            dr = k.nc.snap(lo - r.i + (KH - 1), min_val=0, max_val=KH - 1)
            interleave(*(pair(r, p, r.i, lo, dr) for p in range(pairs)))
    k.meet()


def window_start(k, i):
    lo = (i - KH // 2) * (i >= KH // 2) - (i - (ROWS - KH // 2)) * (i >= ROWS - KH // 2)
    return k.nc.snap(lo, min_val=0, max_val=ROWS - KH)


def log_sigmoid(k, out, x, t, m):
    v = k.nc.vector
    m = k.A(t, x, ACT.Abs, after=[m])
    m = k.A(t, t, ACT.Exp, scale=-1.0, after=[m])
    m = k.A(t, t, ACT.Ln, bias=1.0, after=[m])
    m = k.V(v.scalar_tensor_tensor, out, x, 0.0, t, ALU.min, ALU.subtract, after=[m])
    return k.V(v.tensor_scalar, out, out, 1.0 / 16.0, None, ALU.mult, after=[m])


def gla(k, nT, mixT):
    nc, io = k.nc, k.io
    v, g = nc.vector, nc.gpsimd
    KW2 = RH * DK
    RANK = 16
    hd = lambda ap, d=DH: ap.rearrange("p (h d) -> p h d", d=d)
    with ExitStack() as c:
        sb = lambda *s: c.enter_context(k.area(list(s), F32))
        qkvr = sb(P, NT, 3 * BANK)

        def keep(chunk, m, bank, mark):
            if chunk == 2:
                k.A(qkvr[:, m, 2 * BANK:], bank[:, :], ACT.Silu, after=[mark])
            else:
                k.V(v.tensor_copy, qkvr[:, m, chunk * BANK:(chunk + 1) * BANK], bank[:, :], after=[mark])
        project(k, nT, io["w_in_2"], 3 * BANK, 3, keep)
        oacc = sb(P, NT, BANK)
        la = [sb(P, NT, KW2) for _ in range(2)]
        ng = sb(P, DV)
        with ExitStack() as c2:
            sb2 = lambda *s: c2.enter_context(k.area(list(s), F32))
            wz, zT, gu, gbias = sb2(P, NK, 2 * RANK), [sb2(RANK, T) for _ in range(2)], sb2(RANK, 2, KW2), sb2(P, 2, KW2)
            x, t = [sb2(P, KW2) for _ in range(2)], [sb2(P, KW2) for _ in range(2)]
            load_columns(k, 0, wz[:, :, :], io["w_in_2"], 6 * BANK, 2 * RANK)
            for n, way in enumerate(("fwd", "bwd")):
                k.slot[0](nc.sync.dma_start(gu[:, n, :], io[f"gate_up_{way}"]))
                k.slot[0](nc.sync.dma_start(gbias[:, n, :], spread(io[f"gate_bias_{way}"], KW2)))
            loaded = k.slot[0](nc.sync.dma_start(ng[:, :], spread(io["gla_norm_g"], DV)))
            k.wait(nc.tensor, loaded)
            for n in range(2):
                for h in range(2):
                    b = k.bank[2 * n + h]
                    for f in range(NK):
                        tt = nc.tensor.matmul(b[0:RANK, :], wz[:, f, n * RANK:(n + 1) * RANK], nT[:, f, h * BANK:(h + 1) * BANK],
                                              start=f == 0, stop=f == NK - 1)
                    m = k.V(v.tensor_copy, zT[n][:, h * BANK:(h + 1) * BANK], b[0:RANK, :], after=[k.p(tt)])
            k.wait(nc.tensor, m)
            k.wait(nc.vector, loaded)
            last = {}
            for m in range(NT):
                for n in range(2):
                    b = k.bank[4 + 2 * n + m % 2]
                    k.wait(nc.tensor, *last.get((n, m % 2), []))
                    tt = k.p(nc.tensor.matmul(b[:, 0:KW2], zT[n][:, m * P:(m + 1) * P], gu[:, n, :], start=True, stop=True))
                    mm = k.V(v.tensor_tensor, x[n][:, :], b[:, 0:KW2], gbias[:, n, :], ALU.add, after=[tt] + last.get((n, (m + 1) % 2), []))
                    last[(n, m % 2)] = [log_sigmoid(k, la[n][:, m, :], x[n][:, :], t[n][:, :], mm)]
            k.meet()

        two_of = lambda make: [make() for _ in range(2)]
        lt, eb, enb, ek, qd, ki, kt = (two_of(lambda: sb(P, KW2)) for _ in range(7))
        vt, qkT, AT, o, sq = (two_of(lambda: sb(P, BANK)) for _ in range(5))
        ss, dec, state = two_of(lambda: sb(P, RH)), two_of(lambda: sb(P, 2, 2)), two_of(lambda: sb(P, 2, DV))

        def turn(r, back, i, finish):
            sums, mask = ("after", "behind") if back else ("upto", "upto")
            n = int(back)
            bank = k.bank[4 * n:4 * n + 4]
            row = qkvr[:, ds(i, 1), :].squeeze(1)
            ml = k.V(v.tensor_copy, lt[n][:, :], la[n][:, ds(i, 1), :].squeeze(1), after=[r.last(k.p)])
            mv = k.A(vt[n][:, :], row[:, BANK:2 * BANK], ACT.Copy, after=[r.last(k.p)])
            k.wait(nc.tensor, ml, mv, r.last(k.v), r.last(k.a))
            nc.tensor.matmul(bank[0][:, 0:KW2], k.c(sums), lt[n][:, :], start=True, stop=True)
            nc.tensor.matmul(bank[0][:, KW2:], k.c("chunk"), lt[n][:, :], start=True, stop=True)
            for p in range(2):
                t = nc.tensor.matmul(bank[3][:, 2 * p:2 * p + 2], lt[n][:, p * P:(p + 1) * P], k.c("halves"), start=True, stop=True)
            t = k.p(t)
            yield
            me = k.A(eb[n][:, :], bank[0][:, 0:KW2], ACT.Exp, after=[t, r.last(k.v)])
            mn = k.A(enb[n][:, :], bank[0][:, 0:KW2], ACT.Exp, scale=-1.0, after=[r.last(k.g)])
            md = k.A(dec[n][:, :, :], bank[3][:, 0:4].rearrange("p (a b) -> p a b", b=2), ACT.Exp)
            mb = k.V(v.tensor_copy, ek[n][:, :], bank[0][:, 0:KW2], after=[t, r.last(k.g), mn])
            m = k.V(v.tensor_tensor, ek[n][:, :], bank[0][:, KW2:], ek[n][:, :], ALU.subtract, after=[mb])
            yield
            mk = k.A(ek[n][:, :], ek[n][:, :], ACT.Exp, after=[m])
            mq = k.V(v.scalar_tensor_tensor, qd[n][:, :], row[:, 0:KW2], DK ** -0.5, eb[n][:, :], ALU.mult, ALU.mult, after=[me])
            mi = k.V(v.tensor_tensor, ki[n][:, :], row[:, KW2:BANK], enb[n][:, :], ALU.mult, after=[mn])
            mt = k.G(g.tensor_tensor, kt[n][:, :], row[:, KW2:BANK], ek[n][:, :], ALU.mult, after=[mk, r.last(k.p)])
            yield
            k.wait(nc.tensor, mq, mi, m)
            for p in range(2):
                nc.tensor.transpose(bank[0][:, p * P:(p + 1) * P], qd[n][:, p * P:(p + 1) * P], k.c("ident"))
                t = nc.tensor.transpose(bank[0][:, (2 + p) * P:(3 + p) * P], ki[n][:, p * P:(p + 1) * P], k.c("ident"))
            t = k.p(t)
            m = k.V(v.tensor_copy, qkT[n][:, :], bank[0][:, :], after=[t])
            yield
            k.wait(nc.tensor, m)
            for u in range(2):
                ch = slice(u * DK, (u + 1) * DK)
                for p in range(2):
                    t = nc.tensor.matmul(bank[1 + u][:, p * P:(p + 1) * P], qkT[n][ch, (2 + p) * P:(3 + p) * P], qkT[n][ch, p * P:(p + 1) * P],
                                         start=True, stop=True)
                t = k.p(t)
                ma = k.V(v.tensor_tensor, AT[n][:, :].rearrange("p (a u d) -> p a u d", a=2, u=2)[:, :, u, :],
                         hd(bank[1 + u][:, 0:2 * P]), wide(k.c(mask), 1, 2), ALU.mult, after=[t])
            k.wait(nc.tensor, mt, md)
            tc = {}
            for q in range(2):
                rows = slice(q * DC, (q + 1) * DC)
                for p in range(2):
                    t = nc.tensor.matmul(bank[3 * q][:, p * 2 * DV:(p + 1) * 2 * DV], kt[n][rows, p * P:(p + 1) * P],
                                         vt[n][rows, p * 2 * DV:(p + 1) * 2 * DV], start=True, stop=True)
                tc[q] = k.p(t)
            yield
            k.wait(nc.tensor, ma)
            ob = bank[1:3]
            for h in range(RH):
                nc.tensor.matmul(ob[h % 2][:, h // 2 * DV:(h // 2 + 1) * DV], AT[n][:, h * P:(h + 1) * P], vt[n][:, h * DV:(h + 1) * DV], start=h < 2, stop=False,
                                 skip_group_check=True)
            for q in ((1, 0) if back else (0, 1)):
                rows = slice(q * DC, (q + 1) * DC)
                k.settled(nc.tensor)
                for h in range(RH):
                    p, u = h // 2, h % 2
                    ch = slice(u * DK, (u + 1) * DK)
                    t = nc.tensor.matmul(ob[u][rows, p * DV:(p + 1) * DV], qkT[n][ch, p * P + q * DC:p * P + (q + 1) * DC], state[n][ch, p, :],
                                         start=False, stop=True, skip_group_check=True)
                t = k.p(t)
                yield
                for h in range(RH):
                    p, u = h // 2, h % 2
                    ch = slice(u * DK, (u + 1) * DK)
                    m = k.V(v.scalar_tensor_tensor, state[n][ch, p, :], state[n][ch, p, :], dec[n][ch, p, q:q + 1],
                            bank[3 * q][ch, h * DV:(h + 1) * DV], ALU.mult, ALU.add, after=[t, tc[q], md], chain=h == 0)
                yield
                k.wait(nc.tensor, m)
            acc = oacc[:, ds(i, 1), :].squeeze(1)
            two = lambda ap, u: ap.rearrange("p (a u d) -> p a u d", a=2, u=2)[:, :, u, :]
            for u in range(2):
                src = hd(ob[u][:, 0:2 * DV])
                if not finish:
                    m = k.V(v.tensor_copy, two(acc, u), src, after=[t])
                else:
                    m = k.V(v.tensor_tensor, two(o[n][:, :], u), src, two(acc, u), ALU.add, after=[t])
            if finish:
                yield
                m = yield from heads_norm(k, hd(o[n][:, :]), hd(sq[n][:, :]), ss[n][:, :], ng[:, :], hd(row[:, 2 * BANK:]), DV, m, t)
                t = transposes(k, bank[0], o[n][:, :], after=[m])
                yield
                k.A(mixT[:, 4:6, ds(i * P, P)], bank[0][:, 0:2 * P].rearrange("p (h t) -> p h t", h=2), ACT.Copy, after=[t])
                k.A(mixT[:, 6:8, ds(i * P, P)], bank[0][:, 2 * P:].rearrange("p (h t) -> p h t", h=2), ACT.Copy)

        for n in range(2):
            zero = k.V(v.memset, state[n][:, :, :], 0.0)
        k.wait(nc.tensor, zero)
        for finish in (False, True):
            with k.rounds(NT // 2, p=18 if finish else 16, v=50 if finish else 36, a=16 if finish else 10, g=2) as r:
                first = r.i + (NT // 2 if finish else 0)
                final = nc.snap((NT // 2 - 1 if finish else NT - 1) - r.i, min_val=0, max_val=NT - 1)
                interleave(turn(r, False, first, finish), turn(r, True, final, finish))
            k.meet()


def mlp_up(k, nT, uT):
    nc = k.nc

    def use(r, j, s, banks, mark):
        for h in range(2):
            dst = uT[:, ds(j, 1), h * BANK:(h + 1) * BANK].squeeze(1)
            m = k.A(dst, banks[h][:, :], ACT.Relu, after=[mark])
            k.V(nc.vector.tensor_tensor, dst, dst, banks[h][:, :], ALU.mult, after=[m])
    channels(k, nT, k.io["w_ff1"], 0, NF, use, p=2, v=4, a=4)
    k.meet()


def mlp_down(k, uT, x_dram, out_dram):
    nc = k.nc
    v = nc.vector
    with ExitStack() as c:
        sb = lambda *s: c.enter_context(k.area(list(s), F32))
        w = [sb(P, NF // 2, P) for _ in range(2)]
        yT = sb(P, T)
        xc = sb(P, NT, P)
        with k.rounds(NK, s0=1, s1=1, s2=1, q4=1, p=4, a=1, v=3) as r:
            cols = ds(r.i * P, P)
            t = None
            k.wait(nc.sync, r.last(k.soft[4]))
            mx = k.slot[2](nc.sync.dma_start(xc[:, :, :], x_dram[:, cols].rearrange("(m p) c -> p m c", p=P)))
            for s in range(2):
                k.wait(nc.sync, r.step(k.p, s + 1))
                rows = k.io["w_ff2"][s * (DFF // 2):(s + 1) * (DFF // 2), cols]
                loaded = k.slot[s](nc.sync.dma_start(w[s][:, :, :], rows.rearrange("(f p) c -> p f c", p=P)))
                k.wait(nc.tensor, loaded, *([r.last(k.v), r.last(k.a)] if s == 0 else []))
                for f in range(NF // 2):
                    for h in range(2):
                        ff = s * (NF // 2) + f
                        t = nc.tensor.matmul(k.bank[h][:, :], w[s][:, f, :], uT[:, ff, h * BANK:(h + 1) * BANK],
                                             start=ff == 0, stop=ff == NF - 1)
                t = k.p(t)
            ma = k.A(yT[:, 0:BANK], k.bank[0][:, :], ACT.Copy, after=[t])
            mb = k.V(v.tensor_copy, yT[:, BANK:], k.bank[1][:, :], after=[t])
            for h in range(2):
                t = transposes(k, k.bank[2 + h], yT[:, h * BANK:(h + 1) * BANK], after=[(ma, mb)[h]])
                part = xc[:, 4 * h:4 * h + 4, :]
                m = k.V(v.tensor_tensor, part, part, k.bank[2 + h][:, :].rearrange("p (m c) -> p m c", c=P), ALU.add, after=[t, mx])
            k.wait(nc.gpsimd, m)
            k.soft[4](nc.gpsimd.dma_start(out_dram[:, cols].rearrange("(m p) c -> p m c", p=P), xc[:, :, :]))
    k.meet()


def final_norm(k, x, norm_w, out):
    nc = k.nc
    v = nc.vector
    with ExitStack() as c:
        sq = c.enter_context(k.area([P, D], F32))
        ss = c.enter_context(k.area([P, 2 * NT], F32))
        for n in range(NT):
            s0, s1 = ss[:, 2 * n:2 * n + 1], ss[:, 2 * n + 1:2 * n + 2]
            m = k.A(sq[:, :], x[:, n, :], ACT.Square, accum_out=s0)
            m = rstd(k, s1, s0, D, m)
            m = k.V(v.scalar_tensor_tensor, x[:, n, :], x[:, n, :], s1, norm_w[:, :], ALU.mult, ALU.mult, after=[m])
            k.wait(nc.sync, m)
            k.store(nc.sync.dma_start(out[0, n * P:(n + 1) * P, :], x[:, n, :]))


def load_rows(k, x, dram):
    return k.slot[8](k.nc.sync.dma_start(x[:, :, :], dram.rearrange("(m p) c -> p m c", p=P)))


def build(nc, io, out, tap=None):
    with ExitStack() as ctx:
        k = Program(nc, ctx, io)
        tap = tap or (lambda *a: None)
        sb = lambda *s, dt=F32: ctx.enter_context(k.area(list(s), dt))
        k.bank = [ctx.enter_context(nc.psum_tensor(f"bank{n}", [P, BANK], F32)) for n in range(8)]
        table = shape_constants()
        width = sum(a.shape[1] for a in table.values())
        consts = sb(P, width)
        k.slot[0](nc.sync.dma_start(consts[:, :], io["constants"]))
        at, where_const = 0, {}
        for name, a in table.items():
            where_const[name] = consts[:, at:at + a.shape[1]]
            at += a.shape[1]
        k.c = lambda name: where_const[name]

        xn_rows = nc.dram_tensor("xn_rows", [T, D], F32, kind="Internal").ap()
        y_rows = nc.dram_tensor("y_rows", [BLOCKS * P, D], F32, kind="Internal").ap()
        x_rows = [nc.dram_tensor(f"x_rows{n}", [T, D], F32, kind="Internal").ap() for n in range(4)]

        rpb_rows = nc.dram_tensor("rpb_rows", [NAH, 2 * KH - 1, W, 2 * W - 1], F32, kind="Internal").ap()

        cols = sb(P, 4, NK)
        k.slot[1](nc.sync.dma_start(cols[:, :, :], io["norm_columns"]))
        k.meet()
        mod = sb(P, 6 * NK)
        affine = sb(P, 4, NK)
        gate1, gate2 = sb(P, D), sb(P, D)
        gates = sb(P, NT, 2)
        where, tokens = sb(P, NT, 2, dt=U32), sb(P, BLOCKS + 1, dt=U32)
        experts = sb(P, BLOCKS + 1, dt=I32)
        hT = sb(P, NK, T)

        def with_x(source, *steps):
            with k.area([P, NT, D], F32) as x:
                loaded = load_rows(k, x, source)
                k.wait(nc.vector, loaded)
                k.wait(nc.scalar, loaded)
                for step in steps:
                    step(x)
                k.meet()

        def to(dram):
            def step(x):
                k.wait(nc.sync, *k.now(k.v, k.g))
                k.store(nc.sync.dma_start(dram.rearrange("(m p) c -> p m c", p=P), x[:, :, :]))
            return step

        modulation(k, mod, (gate1, gate2))
        for n, j in ((0, 0), (1, 3)):
            k.V(nc.vector.scalar_tensor_tensor, affine[:, 2 * n, :], mod[:, (j + 1) * NK:(j + 2) * NK], 1.0, cols[:, n, :], ALU.add, ALU.mult)
            k.V(nc.vector.tensor_copy, affine[:, 2 * n + 1, :], mod[:, j * NK:(j + 1) * NK])
        k.meet()
        with_x(io["x"], lambda x: norm_transpose(k, x, hT, affine[:, 0, :], affine[:, 1, :]))
        tap("hT", hT)
        with k.area([P, NK, T], F32) as mixT:
            with k.area([P, NT, DH // 2], F32) as cos, k.area([P, NT, DH // 2], F32) as sin:
                rotary_tables(k, cos, sin)
                tap("cos", cos)
                tap("sin", sin)
                retention(k, hT, mixT, cos, sin)
            delta(k, hT, mixT)
            tap("mixT", mixT)
            with_x(io["x"], lambda x: residual(k, mixT, io["w_out"], x, gate1), to(x_rows[0]),
                   lambda x: norm_transpose(k, x, hT, affine[:, 2, :], affine[:, 3, :], xn_dram=xn_rows))
        route(k, hT, gates, where, tokens, experts)
        for name, value in (("gates", gates), ("where", where), ("tokens", tokens), ("experts", experts)):
            tap(name, value)
        experts_pass(k, affine[:, 2, :], affine[:, 3, :], tokens, experts, xn_rows, y_rows)
        with k.area([P, D], F32) as norm_w:
            k.slot[2](nc.sync.dma_start(norm_w[:, :], spread(io["final_norm_w"], D)))
            k.meet()
            with_x(x_rows[0], lambda x: combine(k, x, gates, where, y_rows, gate2, norm_w), to(x_rows[1]), lambda x: tap("x3", x),
                   lambda x: norm_transpose(k, x, hT, cols[:, 2, :], None))
        with k.area([P, NK, T], F32) as mixT:
            neighbourhood(k, hT, mixT, rpb_rows)
            gla(k, hT, mixT)
            tap("mixT2", mixT)
            with_x(x_rows[1], lambda x: residual(k, mixT, io["w_out_2"], x, None), to(x_rows[2]),
                   lambda x: norm_transpose(k, x, hT, cols[:, 3, :], None))
        with k.area([P, NF, T], F32) as uT:
            mlp_up(k, hT, uT)
            mlp_down(k, uT, x_rows[2], x_rows[3])
        with k.area([P, D], F32) as norm_w:
            k.slot[2](nc.sync.dma_start(norm_w[:, :], spread(io["ln_final_g_2"], D)))
            k.meet()
            with_x(x_rows[3], lambda x: final_norm(k, x, norm_w, out))


def arrays_of(inputs):
    a = {n: np.ascontiguousarray(v) for n, v in inputs.items()}
    by_feature = lambda v: v.reshape(NK, P).T
    vec = lambda n: a[n].reshape(-1)
    io = {n: a[n][0] for n in ("x", "w_ada", "w_in", "w_out", "w_group", "w_expert", "w1", "w3", "w2",
                               "w_in_2", "w_out_2", "w_ff1_2", "w_ff2_2")}
    io["w_ff1"], io["w_ff2"] = io.pop("w_ff1_2"), io.pop("w_ff2_2")
    io["b_ada"] = a["b_ada"].reshape(1, -1)
    io["cT"] = by_feature(a["c"].reshape(-1))
    io["positions"] = a["positions"].reshape(NT, P).T
    io["norm_columns"] = np.stack([by_feature(a[n].reshape(-1)) for n in ("norm1_w", "norm2_w", "ln_mix_g_2", "ln_ff_g_2")], 1)
    io["conv"] = a["conv_w"][0].reshape(4, 12, P).transpose(2, 1, 0)
    for n, src in (("a_log", "a_log"), ("dt_bias", "dt_bias"), ("dn_norm_w", "dn_norm_w"), ("b_group", "b_group"),
                   ("b_expert", "b_expert"), ("final_norm_w", "final_norm_w"), ("ln_final_g_2", "ln_final_g_2"),
                   ("gla_norm_g", "gla_norm_g_2"), ("gate_bias_fwd", "gla_gate_bias_fwd_2"), ("gate_bias_bwd", "gla_gate_bias_bwd_2")):
        io[n] = vec(src)
    io["gate_up_fwd"], io["gate_up_bwd"] = a["gla_gate_up_fwd_2"][0], a["gla_gate_up_bwd_2"][0]
    rpb = np.zeros((NAH, 2 * KH - 1, 2 * W - 1), np.float32)
    rpb[:, :, W - KW:W - KW + 2 * KW - 1] = a["na_rpb_2"][0]
    io["rpb"] = rpb
    io["constants"] = np.concatenate(list(shape_constants().values()), 1)
    return {n: np.ascontiguousarray(v) for n, v in io.items()}


def kernel(**inputs):
    import concourse.bacc as bacc
    from concourse.bass_utils import run_bass_kernel_spmd as run

    arrays = arrays_of({n: np.asarray(v) for n, v in inputs.items()})
    nc = bacc.Bacc("TRN2", target_bir_lowering=False, num_devices=1)
    io = {n: nc.dram_tensor(f"in_{n}", a.shape, mybir.dt.from_np(a.dtype), kind="ExternalInput").ap() for n, a in arrays.items()}
    out = nc.dram_tensor("out", [1, T, D], F32, kind="ExternalOutput").ap()
    build(nc, io, out)
    result = run(nc, [{f"in_{n}": a for n, a in arrays.items()}], core_ids=[0])
    return result.results[0]["out"]
```

```python
from contextlib import ExitStack, contextmanager

import numpy as np

import concourse.bass as bass
from concourse import mybir

F32 = mybir.dt.float32
I32 = mybir.dt.int32
U32 = mybir.dt.uint32
ALU = mybir.AluOpType
ACT = mybir.ActivationFunctionType
AX = mybir.AxisListType
ds = bass.ds

P = 128
T = 1024
D = 1024
NT = T // P
NK = D // P
BANK = 512
NEG = -1.0e30
EPS = 1e-6

RH = 4
DH = 128
RC = 128
DC = 64
GROUPS, PER_GROUP = 4, 8
NE = GROUPS * PER_GROUP
DE = D // 2
BLOCKS = 2 * T // P + NE
ROWS, W = 16, 64
KH, KW = 8, 16
NAH, NAD = 8, 64
DK, DV = 64, 128
DFF = 4 * D
NF = DFF // P
IN1 = 8 * 512 + 8
IN2 = 3 * 512 + 2 * 256 + 2 * 512 + 32

LEVELS = (1, 2, 4, 8, 16, 32)


def shape_constants():
    i = np.arange(P)
    j = i[:, None]
    same = (i[None, :] // DC) == (j // DC)
    gamma = 1.0 - 2.0 ** (-5.0 - np.arange(RH))
    c = {}
    c["ident"] = np.eye(P)
    c["ones"] = np.ones((P, P))
    c["upto"] = same & (j <= i[None, :])
    c["after"] = same & (j >= i[None, :])
    c["behind"] = same & (j > i[None, :])
    c["chunk"] = same
    c["before"] = j < i[None, :]
    for b in LEVELS:
        c[f"level{b}"] = (i[None, :] // (2 * b) == j // (2 * b)) & (i[None, :] % (2 * b) >= b) & (j % (2 * b) < b)
    c["ret_mask"] = np.concatenate([np.where(i[None, :] >= j, g ** -(j + 1.0), 0.0) * DH ** -0.5 for g in gamma], 1)
    c["ret_out"] = np.stack([g ** (i + 1.0) for g in gamma], 1)
    c["ret_key"] = np.stack([g ** (RC - 1.0 - i) * DH ** -0.5 for g in gamma], 1)
    c["halves"] = np.stack([i < DC, i >= DC], 1)
    c["half0"] = np.repeat((i < DC)[:, None], P, 1)
    c["half1"] = np.repeat((i >= DC)[:, None], P, 1)
    c["row"] = np.repeat(i[None, :], P, 0)
    c["token"] = j + P * np.arange(NT)[None, :]
    c["steps"] = np.repeat(P * np.arange(NT)[None, :], P, 0)
    c["inv_freq"] = np.repeat((np.float32(10000.0) ** (-np.arange(0, DH, 2, dtype=np.float32) / np.float32(DH)))[None, :], P, 0)
    q = i % W
    start = np.clip(q - KW // 2, 0, W - KW)[:, None]
    k = np.arange(W)[None, :]
    c["window"] = np.where((k >= start) & (k < start + KW), 0.0, NEG)
    c["qk_scale"] = np.repeat(np.array([DH ** -0.5] * RH + [1.0] * RH)[None, :], P, 0)
    return {n: np.asarray(v, np.float32).reshape(P, -1) for n, v in c.items()}


class Line:

    def __init__(self, k, name, step=1, credit=0, engine=None):
        self.k, self.step, self.count, self.engine = k, step, credit, engine
        self.sem = k.ctx.enter_context(k.nc.semaphore(name))
        self.name = name
        k.lines.append(self)

    def __call__(self, instruction):
        instruction.then_inc(self.sem, self.step)
        self.count += self.step
        loop = self.k.loop
        assert loop is None or self in loop.per, f"{self.name} is not among the loop's lines"
        return Mark(self, self.count, loop)


class Mark:

    def __init__(self, line, at, loop, ago=0):
        self.line, self.at, self.loop, self.ago = line, at, loop, ago

    def before(self, rounds):
        return Mark(self.line, self.at, self.loop, self.ago + rounds)

    def order(self):
        back = self.ago * self.loop.per[self.line] * self.line.step if self.loop else 0
        return (self.at - back) if self.loop is None or not self.loop.over else self.value()

    def value(self):
        if self.loop is None:
            return self.at
        per = self.loop.per[self.line] * self.line.step
        if self.loop.over:
            return self.at + (self.loop.n - 1) * per
        return self.loop.i * per + (self.at - self.ago * per)


class Rounds:

    def __init__(self, k, n, per):
        self.k, self.n, self.per, self.over = k, n, dict(per), False

    def __enter__(self):
        assert self.k.loop is None
        self.k.loop = self
        self.base = {line: line.count for line in self.per}
        self.fori = self.k.nc.Fori(0, self.n)
        self.i = self.fori.__enter__()
        return self

    def last(self, line, ago=1):
        return Mark(line, self.base[line] + self.per[line] * line.step, self, ago)

    def step(self, line, nth, ago=1):
        return Mark(line, self.base[line] + nth * line.step, self, ago)

    def __exit__(self, *failed):
        self.fori.__exit__(*failed)
        if failed[0] is None:
            made = {line: (line.count - self.base[line]) // line.step for line in self.per}
            assert made == self.per, "steps a round: " + ", ".join(f"{x.name} {n}" for x, n in made.items())
            for line, per in self.per.items():
                line.count = self.base[line] + self.n * per * line.step
            self.over = True
            self.k.loop = None


class Program:
    CREDIT = 256

    def __init__(self, nc, ctx, io, tap=None):
        self.nc, self.ctx, self.io, self.lines, self.loop, self.areas = nc, ctx, io, [], None, 0
        self.tap = tap
        self.v = Line(self, "vector_steps", credit=self.CREDIT, engine=nc.vector)
        self.a = Line(self, "scalar_steps", credit=self.CREDIT, engine=nc.scalar)
        self.p = Line(self, "tensor_steps", credit=self.CREDIT, engine=nc.tensor)
        self.g = Line(self, "gpsimd_steps", credit=self.CREDIT, engine=nc.gpsimd)
        self.slot = [Line(self, f"load_slot{n}", step=16, credit=self.CREDIT, engine=nc.sync) for n in range(10)]
        self.store = Line(self, "stores", step=16, credit=self.CREDIT, engine=nc.sync)
        for line in self.lines:
            line.engine.sem_inc(line.sem, self.CREDIT)
        self.soft = [Line(self, f"soft_slot{n}", step=16) for n in range(5)]
        self.passed = ctx.enter_context(nc.semaphore("waits_passed"))

    def area(self, shape, dtype=F32):
        self.areas += 1
        return self.nc.sbuf_tensor(f"area{self.areas}", list(shape), dtype)

    def wait(self, engine, *marks):
        latest = {}
        for m in marks:
            if m.line not in latest or m.order() > latest[m.line].order():
                latest[m.line] = m
        for m in latest.values():
            engine.wait_ge(m.line.sem, m.value())

    @contextmanager
    def only(self, engine, cond, line, steps, after=()):
        before = self.now(line)
        with engine.If(cond):
            yield
        assert line.count == before[0].at + steps * line.step
        with engine.Else():
            self.wait(engine, *before, *after)
            engine.sem_inc(line.sem, steps * line.step)

    def settled(self, engine):
        engine.sem_inc(self.passed, 1)

    def now(self, *lines):
        return [Mark(x, x.count, self.loop) for x in lines]

    def meet(self):
        assert self.loop is None
        for engine in (self.nc.sync, self.nc.vector, self.nc.scalar, self.nc.tensor, self.nc.gpsimd):
            for line in self.lines:
                if line.count:
                    engine.wait_ge(line.sem, line.count)

    def rounds(self, n, **per):
        return Rounds(self, n, {self.named(k): c for k, c in per.items() if c})

    def named(self, k):
        lines = {"v": self.v, "a": self.a, "p": self.p, "g": self.g, "store": self.store}
        lines.update({f"s{n}": x for n, x in enumerate(self.slot)})
        lines.update({f"q{n}": x for n, x in enumerate(self.soft)})
        return lines[k]

    def take(self, line, after, chain):
        own = self.now(line) if chain else [m for m in after if m.line is line]
        self.wait(line.engine, *own, *[m for m in after if m.line is not line])

    def V(self, instruction, *args, after=(), chain=True, **kw):
        self.take(self.v, after, chain)
        return self.v(instruction(*args, **kw))

    def A(self, out, in_, func, after=(), chain=True, **kw):
        self.take(self.a, after, chain)
        return self.a(self.nc.scalar.activation(out, in_, func, **kw))

    def G(self, instruction, *args, after=(), **kw):
        self.take(self.g, after, True)
        return self.g(instruction(*args, **kw))


def wide(ap, axis, n):
    shape = list(ap.shape)
    shape.insert(axis, n)
    return ap.unsqueeze(axis).broadcast_to(shape)


def interleave(*streams):
    streams = list(streams)
    while streams:
        streams = [x for x in streams if next(x, x) is not x]


def spread(dram, n, parts=P):
    return bass.AP(dram.tensor, dram.offset, [[0, parts], [1, n]])


def rstd(k, out, total, n, m, eps=EPS):
    v = k.nc.vector
    m = k.V(v.tensor_scalar, out, total, 1.0 / n, eps, ALU.mult, ALU.add, after=[m])
    m = k.V(v.reciprocal, out, out, after=[m])
    return k.A(out, out, ACT.Sqrt, after=[m])


def norm_transpose(k, x, xT, scale, shift, xn_dram=None):
    nc = k.nc
    with ExitStack() as c:
        two_of = lambda n: [c.enter_context(k.area([P, n], F32)) for _ in range(2)]
        sq, xn, ss = two_of(D), two_of(D), two_of(2)
        store = xn_dram is not None

        def tile(r, n, i):
            xi = x[:, ds(i, 1), :].squeeze(1)
            m = k.A(sq[n][:, :], xi, ACT.Square, accum_out=ss[n][:, 0:1], after=[r.last(k.v)])
            yield
            m = rstd(k, ss[n][:, 1:2], ss[n][:, 0:1], D, m)
            yield
            before = [r.last(k.p)] + ([r.last(k.slot[4 + n])] if store else [])
            m = k.V(nc.vector.tensor_scalar, xn[n][:, :], xi, ss[n][:, 1:2], None, ALU.mult, after=[m] + before)
            if store:
                k.wait(nc.sync, m)
                k.slot[4 + n](nc.sync.dma_start(xn_dram[ds(i * P, P), :], xn[n][:, :]))
            ts = []
            for half in range(2):
                ts.append(transposes(k, k.bank[2 * n + half], xn[n][:, half * BANK:(half + 1) * BANK],
                                     after=[m, r.last(k.v), r.last(k.a)]))
            yield
            for half in range(2):
                for q in range(4):
                    f = half * 4 + q
                    dst = xT[:, f, ds(i * P, P)]
                    src = k.bank[2 * n + half][:, q * P:(q + 1) * P]
                    if half == 0:
                        k.A(dst, src, ACT.Identity, scale=scale[:, f:f + 1],
                            bias=shift[:, f:f + 1] if shift is not None else 0.0, after=[ts[0]], chain=q == 0)
                    elif shift is not None:
                        k.V(nc.vector.tensor_scalar, dst, src, scale[:, f:f + 1], shift[:, f:f + 1],
                            ALU.mult, ALU.add, after=[ts[1]], chain=q == 0)
                    else:
                        k.V(nc.vector.tensor_scalar, dst, src, scale[:, f:f + 1], None, ALU.mult, after=[ts[1]], chain=q == 0)

        with k.rounds(NT // 2, a=2 * (2 + NK // 2), v=2 * (3 + NK // 2), p=4, s4=store, s5=store) as r:
            interleave(*(tile(r, n, r.i * 2 + n) for n in range(2)))
    k.meet()


def load_columns(k, slot, wbuf, w, col, n, after=()):
    k.wait(k.nc.sync, *after)
    return k.slot[slot](k.nc.sync.dma_start(wbuf, w[:, ds(col, n)].rearrange("(k p) c -> p k c", p=P)))


def project(k, xT, w, col0, chunks, evacuate, v=0, a=0, g=0):
    nc = k.nc
    with ExitStack() as c:
        wbuf = [c.enter_context(k.area([P, NK, BANK], F32)) for _ in range(2)]

        def chunk(s, at, before, used):
            loaded = load_columns(k, s, wbuf[s][:, :, :], w, at * BANK + col0, BANK, after=used)
            for m in range(NT):
                k.wait(nc.tensor, *before(m))
                if m == 0:
                    k.wait(nc.tensor, loaded)
                for f in range(NK):
                    t = nc.tensor.matmul(k.bank[m][:, :], xT[:, f, m * P:(m + 1) * P], wbuf[s][:, f, :],
                                         start=f == 0, stop=f == NK - 1)
                evacuate(at, m, k.bank[m], k.p(t))

        if chunks % 2 == 0 and chunks > 2:
            with k.rounds(chunks // 2, p=2 * NT, v=2 * v, a=2 * a, g=2 * g, s0=1, s1=1) as r:
                chunk(0, r.i * 2, lambda m: [r.last(k.v), r.last(k.a)], [r.step(k.p, NT)])
                made = k.now(k.v, k.a)
                chunk(1, r.i * 2 + 1, lambda m: made, [r.last(k.p)])
        else:
            for n in range(chunks):
                made = k.now(k.v, k.a)
                chunk(n % 2, n, lambda m: made, k.now(k.p) if n > 1 else [])
    k.meet()


def modulation(k, mod, gates):
    nc, io = k.nc, k.io
    third = 2 * D
    with ExitStack() as c:
        acc = c.enter_context(k.area([P, 6 * D], F32))
        wa = [c.enter_context(k.area([P, third], F32)) for _ in range(6)]
        cT = c.enter_context(k.area([P, NK], F32))
        zero = k.V(nc.vector.memset, acc[:, :], 0.0)
        k.wait(nc.sync, zero)
        bias = k.slot[6](nc.sync.dma_start(acc[0:1, :], io["b_ada"]))
        cl = k.slot[7](nc.sync.dma_start(cT[:, :], io["cT"]))
        silu = k.A(cT[:, :], cT[:, :], ACT.Silu, after=[cl])
        k.wait(nc.vector, bias, silu)
        with k.rounds(NK // 2, v=6, s0=1, s1=1, s2=1, s3=1, s4=1, s5=1) as r:
            for h in range(2):
                for j in range(3):
                    s = 3 * h + j
                    k.wait(nc.sync, r.step(k.v, s + 1))
                    m = k.slot[s](nc.sync.dma_start(wa[s][:, :], io["w_ada"][ds((r.i * 2 + h) * P, P), j * third:(j + 1) * third]))
                    part = acc[:, j * third:(j + 1) * third]
                    k.V(nc.vector.scalar_tensor_tensor, part, wa[s][:, :], cT[:, ds(r.i * 2 + h, 1)], part, ALU.mult, ALU.add,
                        after=[m, r.step(k.v, s - 2, ago=0) if h else r.step(k.v, s + 4)])
        done = k.now(k.v)
        k.wait(nc.tensor, *done)
        columns = [j for j in range(6 * NK) if j // NK not in (2, 5)]
        for j in columns:
            t = nc.tensor.matmul(k.bank[0][:, j:j + 1], acc[:, j * P:(j + 1) * P], k.c("ones")[:, 0:1], start=True, stop=True)
        t = k.p(t)
        for j in (0, 3):
            part = slice(j * NK, (j + 2) * NK)
            k.V(nc.vector.tensor_copy, mod[:, part], k.bank[0][:, part], after=[t])
        for n, (gate, at) in enumerate(((gates[0], 2), (gates[1], 5))):
            for h in range(2):
                b = 1 + 2 * n + h
                t = k.p(nc.tensor.matmul(k.bank[b][:, :], k.c("ones"), acc[:, at * D + h * BANK:at * D + (h + 1) * BANK],
                                         start=True, stop=True))
                k.V(nc.vector.tensor_copy, gate[:, h * BANK:(h + 1) * BANK], k.bank[b][:, :], after=[t])
    k.meet()


def rotary_tables(k, cos, sin):
    nc, io = k.nc, k.io
    v = nc.vector
    two_pi = 2.0 * np.pi
    parts, rest = [], two_pi
    for bits in (6, 17):
        parts.append(np.floor(rest * 2.0 ** bits) / 2.0 ** bits)
        rest -= parts[-1]
    parts.append(rest)
    magic = 1.5 * 2.0 ** 23
    with ExitStack() as c:
        pos = c.enter_context(k.area([P, NT], I32))
        posf = c.enter_context(k.area([P, NT], F32))
        ang = c.enter_context(k.area([P, NT, DH // 2], F32))
        cnt = c.enter_context(k.area([P, NT, DH // 2], F32))
        red = c.enter_context(k.area([P, NT, DH // 2], F32))
        m = k.slot[0](nc.sync.dma_start(pos[:, :], io["positions"]))
        m = k.V(v.tensor_copy, posf[:, :], pos[:, :], after=[m])
        m = k.V(v.tensor_tensor, ang[:, :, :], wide(posf[:, :], 2, DH // 2), wide(k.c("inv_freq"), 1, NT), ALU.mult, after=[m])
        for out, turn in ((sin, 0.0), (cos, 0.25)):
            m = k.V(v.tensor_scalar, cnt[:, :, :], ang[:, :, :], 1.0 / two_pi, turn, ALU.mult, ALU.add, after=[m])
            m = k.V(v.tensor_scalar, cnt[:, :, :], cnt[:, :, :], magic, -magic, ALU.add, ALU.add, after=[m])
            src = ang
            for part in parts:
                m = k.V(v.scalar_tensor_tensor, red[:, :, :], cnt[:, :, :], -float(part), src[:, :, :], ALU.mult, ALU.add, after=[m])
                src = red
            m = k.V(v.tensor_scalar, red[:, :, :], red[:, :, :], turn * two_pi, np.pi, ALU.add, ALU.min, after=[m])
            m = k.V(v.tensor_scalar, red[:, :, :], red[:, :, :], -np.pi, None, ALU.max, after=[m])
            m = k.A(out[:, :, :], red[:, :, :], ACT.Sin, after=[m])
    k.meet()


def heads_norm(k, o, sq, ss, weight, gate, n, m, gate_mark):
    v = k.nc.vector
    h = o.shape[1]
    m = k.V(v.tensor_tensor, sq, o, o, ALU.mult, after=[m])
    yield
    m = k.V(v.tensor_reduce, ss, sq, AX.X, ALU.add, after=[m])
    yield
    m = rstd(k, ss, ss, n, m)
    yield
    m = k.V(v.tensor_tensor, o, o, wide(ss, 2, n), ALU.mult, after=[m])
    if weight is not None:
        yield
        m = k.V(v.tensor_tensor, o, o, wide(weight, 1, h), ALU.mult, after=[m])
    yield
    return k.V(v.tensor_tensor, o, o, gate, ALU.mult, after=[m, gate_mark])


def transposes(k, bank, src, n=4, after=()):
    nc = k.nc
    k.wait(nc.tensor, *after)
    for h in range(n):
        t = nc.tensor.transpose(bank[:, h * P:(h + 1) * P], src[:, h * P:(h + 1) * P], k.c("ident"))
    return k.p(t)


def retention(k, hT, mixT, cos, sin, meanwhile):
    nc, io = k.nc, k.io
    v = nc.vector
    with ExitStack() as c:
        sb = lambda *s: c.enter_context(k.area(list(s), F32))
        qkvg = sb(P, NT, 4 * BANK)

        def evacuate(chunk, m, bank, mark):
            dst = qkvg[:, m, ds(chunk * BANK, BANK)]
            if m % 2:
                k.V(v.tensor_copy, dst, bank[:, :], after=[mark])
            else:
                k.A(dst, bank[:, :], ACT.Copy, after=[mark])
        project(k, hT, io["w_in"], 0, 4, evacuate, v=4, a=4)
        meanwhile()

        two_of = lambda n: [sb(P, n) for _ in range(2)]
        qk, qkT, t1 = two_of(2 * BANK), two_of(2 * BANK), two_of(2 * BANK)
        kw, sT, o, sq, sg = (two_of(BANK) for _ in range(5))
        ss, state = two_of(RH), sb(P, BANK)
        zero = k.V(v.memset, state[:, :], 0.0)
        k.wait(nc.tensor, zero)
        k.wait(nc.gpsimd, zero)
        gamma = [1.0 - 2.0 ** (-5.0 - h) for h in range(RH)]
        kept = {}

        def tile(r, n, i):
            bank = k.bank[4 * n:4 * n + 4]
            row = qkvg[:, ds(i, 1), :].squeeze(1)
            x = row[:, 0:2 * BANK].rearrange("p (h t d) -> p h t d", h=2 * RH, t=2)
            x1, x2 = x[:, :, 0, :], x[:, :, 1, :]
            y = qk[n][:, :].rearrange("p (h t d) -> p h t d", h=2 * RH, t=2)
            t4 = t1[n][:, :].rearrange("p (t h d) -> p t h d", t=2, h=2 * RH)
            co = wide(cos[:, ds(i, 1), :].squeeze(1), 1, 2 * RH)
            si = wide(sin[:, ds(i, 1), :].squeeze(1), 1, 2 * RH)
            m1 = k.V(v.tensor_tensor, t4[:, 0], x2, si, ALU.mult)
            m = k.V(v.tensor_tensor, y[:, :, 0, :], x1, co, ALU.mult, after=[r.last(k.p)])
            first = k.V(v.tensor_tensor, y[:, :, 0, :], y[:, :, 0, :], t4[:, 0], ALU.subtract, after=[m, m1])
            m1 = k.G(nc.gpsimd.tensor_tensor, t4[:, 1], x1, si, ALU.mult)
            m = k.G(nc.gpsimd.tensor_tensor, y[:, :, 1, :], x2, co, ALU.mult, after=[r.last(k.p), r.last(k.v)])
            second = k.G(nc.gpsimd.tensor_tensor, y[:, :, 1, :], y[:, :, 1, :], t4[:, 1], ALU.add, after=[m, m1])
            gm = k.A(sg[n][:, :], row[:, 3 * BANK:], ACT.Silu, after=[r.last(k.v)])
            yield
            kwm = k.V(v.tensor_tensor, kw[n][:, :].rearrange("p (h d) -> p h d", h=RH),
                      qk[n][:, BANK:].rearrange("p (h d) -> p h d", h=RH), wide(k.c("ret_key"), 2, DH), ALU.mult, after=[first, second])
            ta = transposes(k, bank[0], qk[n][:, 0:BANK], after=[first, second, r.last(k.v), r.last(k.a)])
            tb = transposes(k, bank[1], qk[n][:, BANK:])
            ea = k.A(qkT[n][:, 0:BANK], bank[0][:, :], ACT.Copy, after=[ta])
            eb = k.V(v.tensor_copy, qkT[n][:, BANK:], bank[1][:, :], after=[tb])
            yield
            k.wait(nc.tensor, ea, eb)
            for h in range(RH):
                s = slice(h * P, (h + 1) * P)
                t = nc.tensor.matmul(bank[2][:, s], qkT[n][:, BANK + h * P:BANK + (h + 1) * P], qkT[n][:, s], start=True, stop=True)
            t = k.p(t)
            ms = k.V(v.tensor_tensor, sT[n][:, :], bank[2][:, :], k.c("ret_mask"), ALU.mult, after=[t])
            yield
            k.wait(nc.tensor, ms, kwm, *kept.get(n - 1, []))
            for h in range(RH):
                s = slice(h * P, (h + 1) * P)
                val = qkvg[:, ds(i, 1), 2 * BANK + h * P:2 * BANK + (h + 1) * P].squeeze(1)
                nc.tensor.matmul(bank[3][:, s], sT[n][:, s], val, start=True, stop=False)
                nc.tensor.matmul(bank[3][:, s], qkT[n][:, s], state[:, s], start=False, stop=True)
                t = nc.tensor.matmul(bank[0][:, s], kw[n][:, s], val, start=True, stop=True)
            t = k.p(t)
            for h in range(RH):
                s = slice(h * P, (h + 1) * P)
                m = k.V(v.scalar_tensor_tensor, state[:, s], state[:, s], float(gamma[h] ** RC), bank[0][:, s], ALU.mult, ALU.add,
                        after=[t] if h == 0 else [], chain=h == 0)
            kept[n] = [m]
            yield
            o3 = o[n][:, :].rearrange("p (h d) -> p h d", h=RH)
            m = k.V(v.tensor_tensor, o3, bank[3][:, :].rearrange("p (h d) -> p h d", h=RH), wide(k.c("ret_out"), 2, DH), ALU.mult)
            yield
            m = yield from heads_norm(k, o3, sq[n][:, :].rearrange("p (h d) -> p h d", h=RH), ss[n][:, :], None,
                                      sg[n][:, :].rearrange("p (h d) -> p h d", h=RH), DH, m, gm)
            t = transposes(k, bank[1], o[n][:, :], after=[m])
            yield
            k.A(mixT[:, 0:2, ds(i * P, P)], bank[1][:, 0:2 * P].rearrange("p (h t) -> p h t", h=2), ACT.Copy, after=[t])
            k.A(mixT[:, 2:4, ds(i * P, P)], bank[1][:, 2 * P:].rearrange("p (h t) -> p h t", h=2), ACT.Copy)

        with k.rounds(NT // 2, v=34, a=10, g=6, p=10) as r:
            interleave(*(tile(r, n, r.i * 2 + n) for n in range(2)))
    k.meet()


def channels(k, xT, w, col0, n_chunks, use, unroll=2, p=0, v=0, a=0):
    nc = k.nc
    with ExitStack() as c:
        wbuf = [c.enter_context(k.area([P, NK, P], F32)) for _ in range(2)]
        with k.rounds(n_chunks // unroll, s0=unroll // 2, s1=unroll // 2, p=p, v=v, a=a) as r:
            free = {}
            later = None
            for n in range(unroll):
                s = n % 2
                if n < 2 and unroll == 2:
                    read, evacuated = [r.step(k.p, (n + 1) * p // 2)], [r.step(k.v, (n + 1) * v // 2), r.step(k.a, (n + 1) * a // 2)]
                elif n < 2:
                    read, evacuated = [r.last(k.p)], [r.last(k.v), r.last(k.a)]
                else:
                    read, evacuated = free[s]
                loaded = load_columns(k, s, wbuf[s][:, :, :], w, r.i * unroll * P + (col0 + n * P), P, after=read)
                k.wait(nc.tensor, loaded, *evacuated)
                banks = [k.bank[2 * s], k.bank[2 * s + 1]]
                for h in range(2):
                    for f in range(NK):
                        t = nc.tensor.matmul(banks[h][:, :], wbuf[s][:, f, :], xT[:, f, h * BANK:(h + 1) * BANK],
                                             start=f == 0, stop=f == NK - 1)
                t = k.p(t)
                if later:
                    later()
                later = use(r, r.i * unroll + n, s, banks, t)
                free[s] = [t], k.now(k.v, k.a)
            if later:
                later()


def delta(k, hT, mixT):
    nc, io = k.nc, k.io
    v, g = nc.vector, nc.gpsimd
    hd = lambda ap: ap.rearrange("p (h d) -> p h d", d=DH)
    with ExitStack() as c:
        sb = lambda *s: c.enter_context(k.area(list(s), F32))
        dtok = sb(P, NT, 3 * BANK)
        z = sb(P, NT, BANK)
        ab = sb(P, NT, 2 * RH)

        def keep_z(chunk, m, bank, mark):
            k.A(z[:, m, :], bank[:, :], ACT.Silu, after=[mark])
        project(k, hT, io["w_in"], 7 * BANK, 1, keep_z, a=NT)

        with ExitStack() as c2:
            tail = c2.enter_context(k.area([P, NK, 2 * RH], F32))
            loaded = load_columns(k, 0, tail[:, :, :], io["w_in"], 8 * BANK, 2 * RH)
            k.wait(nc.tensor, loaded)
            for m in range(NT):
                for f in range(NK):
                    t = nc.tensor.matmul(k.bank[0][:, m * 8:m * 8 + 8], hT[:, f, m * P:(m + 1) * P], tail[:, f, :],
                                         start=f == 0, stop=f == NK - 1)
            t = k.p(t)
            k.V(v.tensor_copy, ab[:, :, :], k.bank[0][:, 0:NT * 8].rearrange("p (m e) -> p m e", m=NT), after=[t])
            k.meet()

        with ExitStack() as c2:
            sb2 = lambda *s: c2.enter_context(k.area(list(s), F32))
            cw = sb2(P, 12, 4)
            raw = [sb2(P, T + 3) for _ in range(2)]
            conv = [sb2(P, T) for _ in range(2)]
            m = k.slot[2](nc.sync.dma_start(cw[:, :, :], io["conv"]))
            for s in range(2):
                k.V(v.memset, raw[s][:, 0:3], 0.0, after=[m])
            k.wait(nc.scalar, *k.now(k.v))

            turned = {}

            def use(r, j, s, banks, mark):
                m = k.A(raw[s][:, 3:3 + BANK], banks[0][:, :], ACT.Copy, after=[mark] + (k.now(k.v) if turned else [r.last(k.v)]))
                m = k.A(raw[s][:, 3 + BANK:], banks[1][:, :], ACT.Copy)
                w4 = cw[:, ds(j, 1), :].squeeze(1)
                m = k.V(v.tensor_scalar, conv[s][:, :], raw[s][:, 0:T], w4[:, 0:1], None, ALU.mult, after=[m, r.last(k.p)] + turned.get(s, []))
                for tap in range(1, 4):
                    m = k.V(v.scalar_tensor_tensor, conv[s][:, :], raw[s][:, tap:tap + T], w4[:, tap:tap + 1], conv[s][:, :],
                            ALU.mult, ALU.add, after=[m])
                m = k.A(conv[s][:, :], conv[s][:, :], ACT.Silu, after=[m])

                def turn():
                    for h in range(2):
                        t = transposes(k, k.bank[4 + 2 * s + h], conv[s][:, h * BANK:(h + 1) * BANK], after=[m])
                        dst = dtok[:, 4 * h:4 * h + 4, ds(j * P, P)]
                        src = k.bank[4 + 2 * s + h][:, :].rearrange("p (m d) -> p m d", d=P)
                        if h:
                            k.V(v.tensor_copy, dst, src, after=[t])
                        else:
                            k.A(dst, src, ACT.Copy, after=[t])
                        turned[s] = [t]
                return turn
            channels(k, hT, io["w_in"], 4 * BANK, 12, use, unroll=4, p=12, v=20, a=16)
            k.meet()

        beta, gl, gcum, egc, etail = (sb(P, NT, RH) for _ in range(5))
        gtot = sb(P, 2, NT, RH)
        u = [sb(P, NT, RH) for _ in range(3)]
        alog, dtb, dnw = sb(P, RH), sb(P, RH), sb(P, DH)
        k.slot[0](nc.sync.dma_start(alog[:, :], spread(io["a_log"], RH)))
        k.slot[0](nc.sync.dma_start(dtb[:, :], spread(io["dt_bias"], RH)))
        m = k.slot[0](nc.sync.dma_start(dnw[:, :], spread(io["dn_norm_w"], DH)))
        mb = k.A(beta[:, :, :], ab[:, :, RH:], ACT.Sigmoid, after=k.now(k.v))
        mx = k.V(v.tensor_tensor, u[0][:, :, :], ab[:, :, 0:RH], wide(dtb[:, :], 1, NT), ALU.add, after=[m])
        me = k.A(alog[:, :], alog[:, :], ACT.Exp, after=[m])
        m = k.A(u[1][:, :, :], u[0][:, :, :], ACT.Abs, after=[mx])
        m = k.A(u[1][:, :, :], u[1][:, :, :], ACT.Exp, scale=-1.0, after=[m])
        m = k.A(u[1][:, :, :], u[1][:, :, :], ACT.Ln, bias=1.0, after=[m])
        m = k.V(v.scalar_tensor_tensor, u[0][:, :, :], u[0][:, :, :], 0.0, u[1][:, :, :], ALU.max, ALU.add, after=[m])
        m = k.V(v.scalar_tensor_tensor, gl[:, :, :], u[0][:, :, :], -1.0, wide(alog[:, :], 1, NT), ALU.mult, ALU.mult, after=[m, me])
        k.wait(nc.tensor, m)
        glf = gl[:, :, :].rearrange("p m h -> p (m h)")
        for n, table in enumerate(("upto", "chunk", "half0", "half1")):
            t = nc.tensor.matmul(k.bank[0][:, n * 32:n * 32 + 32], k.c(table), glf, start=True, stop=True)
        t = k.p(t)
        part = lambda n: k.bank[0][:, n * 32:n * 32 + 32].rearrange("p (m h) -> p m h", h=RH)
        m = k.V(v.tensor_copy, gcum[:, :, :], part(0), after=[t])
        k.A(egc[:, :, :], gcum[:, :, :], ACT.Exp, after=[m])
        m = k.V(v.tensor_tensor, u[2][:, :, :], part(1), gcum[:, :, :], ALU.subtract, after=[m])
        k.A(etail[:, :, :], u[2][:, :, :], ACT.Exp, after=[m])
        k.A(gtot[:, 0], part(2), ACT.Exp)
        k.A(gtot[:, 1], part(3), ACT.Exp)

        def buffers(wide_ones, narrow_ones):
            z = dict(zip(("qk", "t1"), wide_ones))
            z.update(zip(("kb", "kbg", "vb", "kt", "gb", "qT", "kT", "kbT", "qgT", "eg", "dec", "B", "at"), narrow_ones))
            z.update(U=z["gb"], X=z["qT"], Y=z["kbT"], BM=z["kT"], nw=z["eg"], vn=z["kb"], o=z["t1"][:, 0:BANK], sq=z["t1"][:, BANK:])
            z.update(ss=sb(P, RH), ss8=sb(P, 2 * RH))
            return z
        first_set = buffers([sb(P, 2 * BANK)[:, :] for _ in range(2)], [sb(P, BANK)[:, :] for _ in range(13)])
        halves = [hT[:, f, h * BANK:(h + 1) * BANK] for f in range(2, NK) for h in range(2)]
        second_set = buffers([hT[:, f, :] for f in range(2)], halves + [sb(P, BANK)[:, :]])
        state = sb(P, BANK)
        k.V(v.memset, state[:, :], 0.0)
        k.meet()
        col = lambda ap, i: ap[:, ds(i, 1), :].squeeze(1)
        kept = {}

        def tile(r, n, i):
            for _ in range(n * 8):
                yield
            bank = k.bank[4 * n:4 * n + 4]
            b = (first_set, second_set)[n]
            qk, t1, kb, kbg, vb, kt, gb = (b[x] for x in ("qk", "t1", "kb", "kbg", "vb", "kt", "gb"))
            qT, kT, kbT, qgT, eg, dec, B, at = (b[x] for x in ("qT", "kT", "kbT", "qgT", "eg", "dec", "B", "at"))
            BM, U, X, Y, nw, vn = (b[x] for x in ("BM", "U", "X", "Y", "nw", "vn"))
            o, sq, ss, ss8 = (b[x] for x in ("o", "sq", "ss", "ss8"))
            row = dtok[:, ds(i, 1), :].squeeze(1)
            bi, gi = col(beta, i), col(gcum, i)
            m = k.A(t1[:, :], row[:, 0:2 * BANK], ACT.Square, after=[r.last(k.v), r.last(k.p)])
            yield
            m = k.V(v.tensor_reduce, ss8[:, :], hd(t1[:, :]), AX.X, ALU.add, after=[m])
            yield
            m = rstd(k, ss8[:, :], ss8[:, :], 1, m)
            yield
            m = k.V(v.tensor_tensor, ss8[:, :], ss8[:, :], k.c("qk_scale"), ALU.mult, after=[m])
            mq = k.V(v.tensor_tensor, hd(qk[:, :]), hd(row[:, 0:2 * BANK]), wide(ss8[:, :], 2, DH), ALU.mult,
                     after=[m, r.last(k.p), r.last(k.g)])
            mkb = k.V(v.tensor_tensor, hd(kb[:, :]), hd(qk[:, BANK:]), wide(bi, 2, DH), ALU.mult, after=[mq])
            yield
            mg = k.G(g.tensor_tensor, hd(gb[:, :]), wide(k.c("ones"), 1, RH), wide(col(gl, i), 2, P), ALU.mult, after=[r.last(k.p)])
            mvb = k.G(g.tensor_tensor, hd(vb[:, :]), hd(row[:, 2 * BANK:]), wide(bi, 2, DH), ALU.mult)
            mkt = k.G(g.tensor_tensor, hd(kt[:, :]), hd(qk[:, BANK:]), wide(col(etail, i), 2, DH), ALU.mult, after=[mq])
            mkg = k.G(g.tensor_tensor, hd(kbg[:, :]), hd(kb[:, :]), wide(col(egc, i), 2, DH), ALU.mult, after=[mkb])
            k.wait(nc.tensor, mg, r.last(k.v), r.last(k.a))
            for h in range(RH):
                t = nc.tensor.matmul(bank[3][:, h * P:(h + 1) * P], gb[:, h * P:(h + 1) * P], k.c("upto"), start=True, stop=True)
            t = k.p(t)
            yield
            me = k.A(eg[:, :], bank[3][:, :], ACT.Exp, after=[t, mq])
            m = k.V(v.tensor_tensor, hd(dec[:, :]), hd(bank[3][:, :]), wide(gi, 2, P), ALU.subtract, after=[t, me])
            m = k.V(v.tensor_scalar, dec[:, :], dec[:, :], 0.0, None, ALU.min, after=[m])
            mdec = m
            yield
            m = k.A(dec[:, :], dec[:, :], ACT.Exp, after=[m])
            yield
            md = k.G(g.tensor_tensor, hd(dec[:, :]), hd(dec[:, :]), wide(k.c("upto"), 1, RH), ALU.mult, after=[m])
            ta = transposes(k, bank[0], qk[:, 0:BANK], after=[mq])
            tb = transposes(k, bank[1], qk[:, BANK:])
            tc = transposes(k, bank[2], kb[:, :], after=[mkb])
            yield
            ea = k.A(qT[:, :], bank[0][:, :], ACT.Copy, after=[ta])
            eb = k.A(kT[:, :], bank[1][:, :], ACT.Copy, after=[tb])
            ec = k.A(kbT[:, :], bank[2][:, :], ACT.Copy, after=[tc])
            mqg = k.V(v.tensor_tensor, qgT[:, :], bank[0][:, :], eg[:, :], ALU.mult, after=[ta, me, ea])
            yield
            k.wait(nc.tensor, ea, eb, ec, mdec)
            for h in range(RH):
                s = slice(h * P, (h + 1) * P)
                nc.tensor.matmul(bank[3][:, s], kT[:, s], kbT[:, s], start=True, stop=True)
                t = nc.tensor.matmul(bank[2][:, s], kT[:, s], qT[:, s], start=True, stop=True)
            t = k.p(t)
            yield
            mB = k.V(v.tensor_tensor, B[:, :], bank[3][:, :], dec[:, :], ALU.mult, after=[t, md])
            mat = k.V(v.tensor_tensor, at[:, :], bank[2][:, :], dec[:, :], ALU.mult)
            mm = k.V(v.tensor_tensor, hd(BM[:, :]), hd(B[:, :]), wide(k.c("level1"), 1, RH), ALU.mult, after=[mB])
            mu = k.V(v.scalar_tensor_tensor, hd(U[:, :]), hd(BM[:, :]), -1.0, wide(k.c("ident"), 1, RH), ALU.mult, ALU.add, after=[mm])
            t = transposes(k, bank[1], BM[:, :], after=[mm, eb])
            yield
            mx = k.V(v.scalar_tensor_tensor, hd(X[:, :]), hd(bank[1][:, :]), -1.0, wide(k.c("ident"), 1, RH), ALU.mult, ALU.add, after=[t])
            for b in LEVELS[1:]:
                last = b == LEVELS[-1]
                mm = k.V(v.tensor_tensor, hd(BM[:, :]), hd(B[:, :]), wide(k.c(f"level{b}"), 1, RH), ALU.mult)
                yield
                k.wait(nc.tensor, mm, mx, mu, mat)
                for h in range(RH):
                    s = slice(h * P, (h + 1) * P)
                    t = nc.tensor.matmul(bank[2][:, s], BM[:, s], X[:, s], start=True, stop=True)
                t = k.p(t)
                yield
                my = k.A(Y[:, :], bank[2][:, :], ACT.Copy, after=[t])
                k.wait(nc.tensor, my)
                for h in range(RH):
                    s = slice(h * P, (h + 1) * P)
                    if not last:
                        nc.tensor.matmul(bank[1][:, s], U[:, s], Y[:, s], start=True, stop=True)
                    t = nc.tensor.matmul(bank[3][:, s], Y[:, s], U[:, s], start=True, stop=True)
                t = k.p(t)
                yield
                mu = k.V(v.tensor_tensor, U[:, :], U[:, :], bank[3][:, :], ALU.subtract, after=[t])
                if not last:
                    mx = k.V(v.tensor_tensor, X[:, :], X[:, :], bank[1][:, :], ALU.subtract)
            yield
            k.wait(nc.tensor, mu, mkg, mvb, mkt)
            for h in range(RH):
                s = slice(h * P, (h + 1) * P)
                t = nc.tensor.matmul(bank[2][:, s], kbg[:, s], U[:, s], start=True, stop=True)
            t = k.p(t)
            yield
            mw = k.A(nw[:, :], bank[2][:, :], ACT.Copy, scale=-1.0, after=[t])
            yield
            while n and not kept:
                yield
            k.wait(nc.tensor, mw, mqg, mat, *(kept["state"] if n else []))
            for q in range(2):
                rows = slice(q * DC, (q + 1) * DC)
                for h in range(RH):
                    s = slice(h * P, (h + 1) * P)
                    cs = slice(h * P + q * DC, h * P + (q + 1) * DC)
                    nc.tensor.matmul(bank[0][rows, s], U[:, cs], vb[:, s], start=True, stop=False)
                    t = nc.tensor.matmul(bank[0][rows, s], nw[:, cs], state[:, s], start=False, stop=True)
                t = k.p(t)
                yield
                mv = k.A(vn[rows, :], bank[0][rows, :], ACT.Copy, after=[t])
                yield
                k.wait(nc.tensor, mv)
                for h in range(RH):
                    s = slice(h * P, (h + 1) * P)
                    cs = slice(h * P + q * DC, h * P + (q + 1) * DC)
                    t = nc.tensor.matmul(bank[1 + q][:, s], kt[rows, s], vn[rows, s], start=True, stop=True)
                t = k.p(t)
                for h in range(RH):
                    s = slice(h * P, (h + 1) * P)
                    cs = slice(h * P + q * DC, h * P + (q + 1) * DC)
                    nc.tensor.matmul(bank[3][rows, s], qgT[:, cs], state[:, s], start=True, stop=False)
                    to = nc.tensor.matmul(bank[3][rows, s], at[rows, cs], vn[rows, s], start=False, stop=True)
                to = k.p(to)
                yield
                for h in range(RH):
                    s = slice(h * P, (h + 1) * P)
                    ms = k.V(v.scalar_tensor_tensor, state[:, s], state[:, s], gtot[:, q, ds(i, 1), h:h + 1].squeeze(1),
                             bank[1 + q][:, s], ALU.mult, ALU.add, after=[t, to] if h == 0 else [], chain=h == 0)
                yield
                k.wait(nc.tensor, ms)
            if not n:
                kept["state"] = [ms]
            m = k.V(v.tensor_copy, o[:, :], bank[3][:, :], after=[to])
            yield
            m = yield from heads_norm(k, hd(o[:, :]), hd(sq[:, :]), ss[:, :], dnw[:, :], hd(col(z, i)), DH, m, to)
            t = transposes(k, bank[0], o[:, :], after=[m])
            yield
            k.A(mixT[:, 4:6, ds(i * P, P)], bank[0][:, 0:2 * P].rearrange("p (h t) -> p h t", h=2), ACT.Copy, after=[t])
            k.A(mixT[:, 6:8, ds(i * P, P)], bank[0][:, 2 * P:].rearrange("p (h t) -> p h t", h=2), ACT.Copy)

        with k.rounds(NT // 2, v=88, a=36, g=10, p=48) as r:
            interleave(*(tile(r, n, r.i * 2 + n) for n in range(2)))
    k.meet()


def residual(k, mixT, w, x, gate):
    nc = k.nc
    with ExitStack() as c:
        tmp = [c.enter_context(k.area([P, BANK], F32)) for _ in range(2)]

        pending = {0: [], 1: []}

        def add(chunk, m, bank, mark):
            dst = x[:, m, chunk * BANK:(chunk + 1) * BANK]
            if gate is None:
                k.V(nc.vector.tensor_tensor, dst, dst, bank[:, :], ALU.add, after=[mark])
                return
            t = tmp[m % 2]
            a = k.V(nc.vector.tensor_tensor, t[:, :], bank[:, :], gate[:, chunk * BANK:(chunk + 1) * BANK], ALU.mult,
                    after=[mark] + pending[m % 2])
            pending[m % 2] = [k.G(nc.gpsimd.tensor_tensor, dst, dst, t[:, :], ALU.add, after=[a])]
        project(k, mixT, w, 0, 2, add)


def route(k, h2T, gates, where, tokens, experts):
    nc, io = k.nc, k.io
    v = nc.vector
    NL = GROUPS + NE
    with ExitStack() as c:
        sb = lambda *s, dt=F32: c.enter_context(k.area(list(s), dt))
        wr, br = sb(P, NK, NL), sb(P, NL)
        lg, eq = sb(P, NT, NL), sb(P, NT, NE)
        gp, top, ix, ixf = sb(P, NT, 8), sb(P, NT, 8), sb(P, NT, 8, dt=U32), sb(P, NT, 8)
        sel = sb(P, NT, PER_GROUP)
        hot = sb(P, 2, NT, NE)
        both = sb(P, NT, NE)
        a1, a2, a3 = sb(P, NT), sb(P, NT), sb(P, NT)
        k.slot[0](nc.sync.dma_start(wr[:, :, 0:GROUPS], io["w_group"].rearrange("(k p) c -> p k c", p=P)))
        k.slot[0](nc.sync.dma_start(wr[:, :, GROUPS:], io["w_expert"].rearrange("(k p) c -> p k c", p=P)))
        k.slot[0](nc.sync.dma_start(br[:, 0:GROUPS], spread(io["b_group"], GROUPS)))
        loaded = k.slot[0](nc.sync.dma_start(br[:, GROUPS:], spread(io["b_expert"], NE)))
        k.wait(nc.tensor, loaded)
        for m in range(NT):
            for f in range(NK):
                t = nc.tensor.matmul(k.bank[0][:, m * NL:(m + 1) * NL], h2T[:, f, m * P:(m + 1) * P], wr[:, f, :],
                                     start=f == 0, stop=f == NK - 1)
        t = k.p(t)
        m = k.V(v.tensor_tensor, lg[:, :, :], k.bank[0][:, 0:NT * NL].rearrange("p (m e) -> p m e", m=NT),
                wide(br[:, :], 1, NT), ALU.add, after=[t, loaded])
        m1 = k.V(v.memset, gp[:, :, :], NEG)
        m = k.V(v.tensor_copy, gp[:, :, 0:GROUPS], lg[:, :, 0:GROUPS], after=[m, m1])
        mt = [k.V(v.max, top[:, n, :], gp[:, n, :], after=[m], chain=False) for n in range(NT)]
        for n in range(NT):
            mi = k.V(v.max_index, ix[:, n, :], top[:, n, :], gp[:, n, :], after=[mt[n]], chain=False)
        m = k.V(v.tensor_copy, ixf[:, :, 0:1], ix[:, :, 0:1], after=[mi])
        m2 = k.V(v.tensor_tensor, gp[:, :, 0:GROUPS], gp[:, :, 0:GROUPS], top[:, :, 0:1].broadcast_to([P, NT, GROUPS]), ALU.subtract, after=[mi])
        m2 = k.A(gp[:, :, 0:GROUPS], gp[:, :, 0:GROUPS], ACT.Exp, after=[m2])
        mz = k.V(v.tensor_reduce, a1[:, :], gp[:, :, 0:GROUPS], AX.X, ALU.add, after=[m2])
        me = k.V(v.tensor_tensor, eq[:, :, 0:GROUPS], wide(k.c("row")[:, 0:GROUPS], 1, NT), ixf[:, :, 0:1].broadcast_to([P, NT, GROUPS]), ALU.is_equal, after=[m])
        for n in range(GROUPS):
            src = lg[:, :, GROUPS + n * PER_GROUP:GROUPS + (n + 1) * PER_GROUP]
            pick = eq[:, :, n:n + 1].broadcast_to([P, NT, PER_GROUP])
            if n == 0:
                ms = k.V(v.tensor_tensor, sel[:, :, :], src, pick, ALU.mult, after=[me])
            else:
                mp = k.V(v.tensor_tensor, both[:, :, 0:PER_GROUP], src, pick, ALU.mult, after=[ms])
                ms = k.V(v.tensor_tensor, sel[:, :, :], sel[:, :, :], both[:, :, 0:PER_GROUP], ALU.add, after=[mp])
        base = k.V(v.tensor_scalar, a2[:, :], ixf[:, :, 0:1].squeeze(2), float(PER_GROUP), None, ALU.mult, after=[ms])
        mt = [k.V(v.max, top[:, n, :], sel[:, n, :], after=[ms, base], chain=False) for n in range(NT)]
        for n in range(NT):
            mi = k.V(v.max_index, ix[:, n, :], top[:, n, :], sel[:, n, :], after=[mt[n]], chain=False)
        m = k.V(v.tensor_copy, ixf[:, :, 0:2], ix[:, :, 0:2], after=[mi])
        m = k.V(v.tensor_tensor, ixf[:, :, 0:2], ixf[:, :, 0:2], wide(a2[:, :], 2, 2), ALU.add, after=[m])
        md = k.V(v.tensor_tensor, a2[:, :], top[:, :, 1:2].squeeze(2), top[:, :, 0:1].squeeze(2), ALU.subtract, after=[m])
        md = k.A(a2[:, :], a2[:, :], ACT.Exp, after=[md])
        ms = k.V(v.scalar_tensor_tensor, a3[:, :], a2[:, :], 1.0, a1[:, :], ALU.add, ALU.mult, after=[md, mz])
        ms = k.V(v.reciprocal, gates[:, :, 0:1].squeeze(2), a3[:, :], after=[ms])
        k.V(v.tensor_tensor, gates[:, :, 1:2].squeeze(2), gates[:, :, 0:1].squeeze(2), a2[:, :], ALU.mult, after=[ms])
        for j in range(2):
            mh = k.V(v.tensor_tensor, hot[:, j], wide(k.c("row")[:, 0:NE], 1, NT), ixf[:, :, j:j + 1].broadcast_to([P, NT, NE]), ALU.is_equal, after=[m])
        m = k.V(v.tensor_tensor, both[:, :, :], hot[:, 0], hot[:, 1], ALU.add, after=[mh])
        earlier = sb(P, NT + 1, NE)
        me = k.V(v.memset, earlier[:, 0, :], 0.0)
        for n in range(NT):
            m = k.V(v.tensor_tensor, earlier[:, n + 1, :], earlier[:, n, :], both[:, n, :], ALU.add, after=[m, me])
        k.wait(nc.tensor, m)
        t = nc.tensor.matmul(k.bank[1][:, 0:NT * NE], k.c("before"), both[:, :, :].rearrange("p m e -> p (m e)"), start=True, stop=False)
        t = nc.tensor.matmul(k.bank[1][:, 0:NT * NE], k.c("ones"), earlier[:, 0:NT, :].rearrange("p m e -> p (m e)"), start=False, stop=True)
        t = nc.tensor.matmul(k.bank[2][:, 0:NE], k.c("ones"), earlier[:, NT, :], start=True, stop=True)
        t = k.p(t)
        cnt, full = sb(P, NE, NT), sb(P, NE)
        upto = [sb(P, NE + 16) for _ in range(2)]
        first = sb(P, NE)
        m = k.V(v.tensor_tensor, cnt[:, :, :], k.bank[2][:, 0:NE].unsqueeze(2).broadcast_to([P, NE, NT]), wide(k.c("steps"), 1, NE), ALU.is_gt, after=[t])
        m = k.V(v.tensor_reduce, full[:, :], cnt[:, :, :], AX.X, ALU.add, after=[m])
        m = k.V(v.memset, upto[0][:, 0:16], 0.0)
        m = k.V(v.memset, upto[1][:, 0:16], 0.0)
        m = k.V(v.tensor_copy, upto[0][:, 16:], full[:, :], after=[m])
        for n, d in enumerate((1, 2, 4, 8, 16)):
            src, dst = upto[n % 2], upto[(n + 1) % 2]
            m = k.V(v.tensor_tensor, dst[:, 16:], src[:, 16:], src[:, 16 - d:16 - d + NE], ALU.add, after=[m])
        total = dst[:, 16:]
        m = k.V(v.tensor_tensor, first[:, :], total, full[:, :], ALU.subtract, after=[m])
        blk = sb(P, BLOCKS, NE)
        ef = sb(P, BLOCKS)
        m1 = k.V(v.tensor_tensor, blk[:, :, :], wide(total, 1, BLOCKS), k.c("row")[:, 0:BLOCKS].unsqueeze(2).broadcast_to([P, BLOCKS, NE]), ALU.is_le, after=[m])
        m1 = k.V(v.tensor_reduce, ef[:, :], blk[:, :, :], AX.X, ALU.add, after=[m1])
        m1 = k.V(v.tensor_scalar, ef[:, :], ef[:, :], float(NE - 1), None, ALU.min, after=[m1])
        k.V(v.tensor_copy, experts[:, 0:BLOCKS], ef[:, :], after=[m1])
        k.V(v.tensor_copy, experts[:, BLOCKS:], total[:, NE - 1:NE])
        rank, div, w2 = sb(P, NT), sb(P, NT), sb(P, NT, NE)
        row_of, blk_of = sb(P, NT, 2), sb(P, NT, 2)
        hp, hb = [sb(P, P) for _ in range(2)], [sb(P, BLOCKS) for _ in range(2)]
        pos = sb(P, NT, 2)
        ranks = k.bank[1][:, 0:NT * NE].rearrange("p (m e) -> p m e", m=NT)
        for j in range(2):
            m = k.V(v.tensor_tensor, w2[:, :, :], ranks, hot[:, j], ALU.mult, after=[m])
            mr = k.V(v.tensor_reduce, rank[:, :], w2[:, :, :], AX.X, ALU.add, after=[m])
            m = k.V(v.tensor_tensor, w2[:, :, :], wide(first[:, :], 1, NT), hot[:, j], ALU.mult, after=[mr])
            m = k.V(v.tensor_reduce, a1[:, :], w2[:, :, :], AX.X, ALU.add, after=[m])
            m = k.V(v.tensor_tensor, w2[:, :, 0:NT - 1], wide(rank[:, :], 2, NT - 1), wide(k.c("steps")[:, 1:NT], 1, NT), ALU.is_ge, after=[m])
            m = k.V(v.tensor_reduce, div[:, :], w2[:, :, 0:NT - 1], AX.X, ALU.add, after=[m])
            m = k.V(v.scalar_tensor_tensor, row_of[:, :, j:j + 1].squeeze(2), div[:, :], -float(P), rank[:, :], ALU.mult, ALU.add, after=[m])
            m = k.V(v.tensor_tensor, blk_of[:, :, j:j + 1].squeeze(2), div[:, :], a1[:, :], ALU.add, after=[m])
        m = k.V(v.scalar_tensor_tensor, pos[:, :, :], blk_of[:, :, :], float(P), row_of[:, :, :], ALU.mult, ALU.add, after=[m])
        k.V(v.tensor_copy, where[:, :, :], pos[:, :, :], after=[m])
        read = {}
        for n in range(NT):
            for j in range(2):
                free = read.get(j, [])
                m1 = k.V(v.tensor_scalar, hp[j][:, :], k.c("row"), row_of[:, n, j:j + 1], None, ALU.is_equal, after=[m] + free)
                m2 = k.V(v.tensor_scalar, hb[j][:, :], k.c("row")[:, 0:BLOCKS], blk_of[:, n, j:j + 1], k.c("token")[:, n:n + 1],
                         ALU.is_equal, ALU.mult)
                k.wait(nc.tensor, m1, m2)
                t = k.p(nc.tensor.matmul(k.bank[3][:, 0:BLOCKS], hp[j][:, :], hb[j][:, :], start=n + j == 0, stop=n + j == NT))
                read[j] = [t]
        k.V(v.tensor_copy, tokens[:, 0:BLOCKS], k.bank[3][:, 0:BLOCKS], after=[t])
        k.V(v.memset, tokens[:, BLOCKS:], 0)
    k.meet()


def experts_pass(k, scale, shift, tokens, experts, xn, ys):
    nc, io = k.nc, k.io
    v, pe, sy, gp = nc.vector, nc.tensor, nc.sync, nc.gpsimd
    with ExitStack() as c:
        sb = lambda *s, dt=F32: c.enter_context(k.area(list(s), dt))
        w1 = [sb(P, NK, DE) for _ in range(2)]
        w3 = [sb(P, NK, DE) for _ in range(2)]
        w2 = [sb(P, DE // P, D) for _ in range(2)]
        rows = [sb(P, D) for _ in range(2)]
        idx = [sb(P, 1, dt=U32) for _ in range(2)]
        xsT = [sb(P, NK, P) for _ in range(2)]
        act, hid, hidT = (sb(P, DE) for _ in range(3))
        y = [sb(P, D) for _ in range(2)]

        PE_STEPS, ACT_STEPS, VEC_STEPS = 6, 7, 6

        def gather(at, s, after):
            m = k.G(gp.tensor_copy, idx[s][:, :], tokens[:, ds(at, 1)], after=after)
            k.wait(gp, m)
            k.settled(gp)
            return k.soft[s](gp.indirect_dma_start(out=rows[s][:, :], out_offset=None, in_=xn[:, :],
                                                   in_offset=bass.IndirectOffsetOnAxis(ap=idx[s][:, 0:1], axis=0)))

        def turn(s, half):
            return transposes(k, k.bank[half], rows[s][:, half * BANK:(half + 1) * BANK])

        def rows_out(s, half, t, before):
            for q in range(4):
                f = half * 4 + q
                src = k.bank[half][:, q * P:(q + 1) * P]
                if half:
                    m = k.V(v.tensor_scalar, xsT[s][:, f, :], src, scale[:, f:f + 1], shift[:, f:f + 1], ALU.mult, ALU.add,
                            after=[t] + before)
                else:
                    m = k.A(xsT[s][:, f, :], src, ACT.Identity, scale=scale[:, f:f + 1], bias=shift[:, f:f + 1], after=[t] + before)
            return m

        used_t, used_s, used_v, used_a = (engine.value_load(experts[0:1, BLOCKS:BLOCKS + 1], min_val=0, max_val=BLOCKS)
                                          for engine in (pe, sy, v, nc.scalar))
        got = gather(0, 0, [])
        k.wait(pe, got)
        for half in range(2):
            rows_out(0, half, turn(0, half), [])
        k.wait(pe, *k.now(k.v, k.a))
        k.wait(gp, *k.now(k.p))
        with k.rounds(BLOCKS // 2, s0=2, s1=2, s2=1, s3=1, s4=1, s5=1, q0=1, q1=1, g=2,
                      v=2 * VEC_STEPS, a=2 * ACT_STEPS, p=2 * PE_STEPS) as r:
            for s in range(2):
                at = r.i * 2 + s
                n = 1 - s
                there = used_s > at
                e = sy.value_load(experts[0:1, ds(at, 1)], min_val=0, max_val=NE - 1)
                for m in (r.step(k.p, PE_STEPS * s + 2), *k.now(k.slot[s], k.slot[2 + s])):
                    k.wait(sy, m)
                    k.settled(sy)
                k.slot[s](sy.dma_start(w1[s][:, :, :], io["w1"][ds(e, 1)].squeeze(0).rearrange("(k p) f -> p k f", p=P),
                                       cond=there, bounds_check="skip_entire_dma"))
                up = k.slot[s](sy.dma_start(w3[s][:, :, :], io["w3"][ds(e, 1)].squeeze(0).rearrange("(k p) f -> p k f", p=P),
                                            cond=there, bounds_check="skip_entire_dma"))
                k.wait(sy, r.step(k.p, PE_STEPS * s + 6))
                k.settled(sy)
                down = k.slot[2 + s](sy.dma_start(w2[s][:, :, :], io["w2"][ds(e, 1)].squeeze(0).rearrange("(k p) f -> p k f", p=P),
                                                  cond=there, bounds_check="skip_entire_dma"))
                got = gather(at + 1, n, [r.step(k.p, PE_STEPS * s + 5)])
                by = lambda line: {n + 1: Mark(line, line.count + n + 1, r) for n in range(PE_STEPS + 1)}
                tensor, scalar, vector = by(k.p), by(k.a), by(k.v)
                with k.only(pe, used_t > at, k.p, PE_STEPS, after=[got]):
                    if s:
                        k.wait(pe, up, *rowed)
                    else:
                        k.wait(pe, up, r.step(k.a, ACT_STEPS + 6), r.step(k.v, VEC_STEPS + 5))
                    for j, w in enumerate((w1[s], w3[s])):
                        for f in range(NK):
                            t = pe.matmul(k.bank[2 + j][:, :], xsT[s][:, f, :], w[:, f, :], start=f == 0, stop=f == NK - 1)
                        k.p(t)
                    k.wait(pe, got)
                    turn(n, 0)
                    k.wait(pe, vector[1])
                    transposes(k, k.bank[4], hid[:, :])
                    turn(n, 1)
                    k.wait(pe, scalar[2], down)
                    for h in range(2):
                        for f in range(DE // P):
                            t = pe.matmul(k.bank[5 + h][:, :], hidT[:, f * P:(f + 1) * P], w2[s][:, f, h * BANK:(h + 1) * BANK],
                                          start=f == 0, stop=f == DE // P - 1)
                    k.p(t)
                rowed = [scalar[6], vector[5]]
                with k.only(nc.scalar, used_a > at, k.a, ACT_STEPS, after=[r.last(k.slot[4 + s])]):
                    k.A(act[:, :], k.bank[2][:, :], ACT.Silu, after=[tensor[1], vector[1].before(1) if not s else last_product])
                    k.A(hidT[:, :], k.bank[4][:, :], ACT.Copy, after=[tensor[4]])
                    rows_out(n, 0, tensor[3], [tensor[2]])
                    k.A(y[s][:, 0:BANK], k.bank[5][:, :], ACT.Copy, after=[tensor[6], r.last(k.slot[4 + s])])
                with k.only(v, used_v > at, k.v, VEC_STEPS):
                    k.V(v.tensor_tensor, hid[:, :], act[:, :], k.bank[3][:, :], ALU.mult, after=[scalar[1], tensor[2]])
                    rows_out(n, 1, tensor[5], [])
                    k.V(v.tensor_copy, y[s][:, BANK:], k.bank[6][:, :], after=[tensor[6], r.last(k.slot[4 + s])])
                last_product = vector[1]
                k.wait(nc.scalar, scalar[7], vector[6])
                k.slot[4 + s](nc.scalar.dma_start(ys[ds(at * P, P), :], y[s][:, :]))
    k.meet()


def combine(k, x, gates, where, ys, gate2, norm_w):
    nc = k.nc
    v = nc.vector
    with ExitStack() as c:
        sb = lambda *s, dt=F32: c.enter_context(k.area(list(s), dt))
        SETS = 4
        y = [[sb(P, D) for _ in range(2)] for _ in range(SETS)]
        idx = [[sb(P, 1, dt=U32) for _ in range(2)] for _ in range(SETS)]
        sq, ss = [sb(P, D) for _ in range(2)], [sb(P, 2) for _ in range(SETS)]

        def tile(r, s, n):
            xt = x[:, ds(n, 1), :].squeeze(1)
            for j in range(2):
                mi = k.V(v.tensor_copy, idx[s][j][:, :], where[:, ds(n, 1), j:j + 1].squeeze(1))
                k.wait(nc.gpsimd, mi)
                k.settled(nc.gpsimd)
                got = k.soft[s](nc.gpsimd.indirect_dma_start(
                    out=y[s][j][:, :], out_offset=None, in_=ys[:, :],
                    in_offset=bass.IndirectOffsetOnAxis(ap=idx[s][j][:, 0:1], axis=0)))
            yield
            gt = gates[:, ds(n, 1), :].squeeze(1)
            m = k.V(v.tensor_scalar, y[s][0][:, :], y[s][0][:, :], gt[:, 0:1], None, ALU.mult, after=[got])
            m = k.V(v.scalar_tensor_tensor, y[s][0][:, :], y[s][1][:, :], gt[:, 1:2], y[s][0][:, :], ALU.mult, ALU.add, after=[m])
            m = k.V(v.tensor_tensor, y[s][0][:, :], y[s][0][:, :], gate2[:, :], ALU.mult, after=[m])
            mx = k.V(v.tensor_tensor, xt, xt, y[s][0][:, :], ALU.add, after=[m])
            m = k.A(sq[s % 2][:, :], xt, ACT.Square, accum_out=ss[s][:, 0:1], after=[mx])
            yield
            m = rstd(k, ss[s][:, 1:2], ss[s][:, 0:1], D, m)
            yield
            k.V(v.scalar_tensor_tensor, xt, xt, ss[s][:, 1:2], norm_w[:, :], ALU.mult, ALU.mult, after=[m])

        with k.rounds(NT // SETS, q0=2, q1=2, q2=2, q3=2, v=9 * SETS, a=2 * SETS) as r:
            interleave(*(tile(r, n, r.i * SETS + n) for n in range(SETS)))
    k.meet()


def neighbourhood(k, nT, mixT, scratch):
    nc, io = k.nc, k.io
    v = nc.vector
    pairs = NAH // 2
    dr_w = (2 * KH - 1) * W
    with ExitStack() as c:
        sb = lambda *s: c.enter_context(k.area(list(s), F32))
        qkT = sb(P, 2 * pairs, T)
        val = sb(P, ROWS, BANK)
        bias = sb(P, pairs, dr_w)
        RW = 2 * W - 1
        k.wait(nc.sync, *k.now(k.slot[9]))
        for h in range(NAH):
            src = bass.AP(scratch.tensor, scratch.offset + h * (2 * KH - 1) * W * RW + W - 1, [[RW - 1, W], [W * RW, 2 * KH - 1], [1, W]])
            dst = bias[(h % 2) * W:(h % 2 + 1) * W, h // 2, :].rearrange("p (r c) -> p r c", c=W)
            biased = k.slot[9](nc.sync.dma_start(dst, src))

        def keep(r, j, s, banks, mark):
            m = k.A(qkT[:, ds(j, 1), 0:BANK].squeeze(1), banks[0][:, :], ACT.Copy, after=[mark])
            k.V(v.tensor_copy, qkT[:, ds(j, 1), BANK:].squeeze(1), banks[1][:, :], after=[mark])
        channels(k, nT, io["w_in_2"], 0, 2 * pairs, keep, p=2, v=2, a=2)
        k.meet()

        def keep_v(chunk, m, bank, mark):
            k.A(val[:, 2 * m, :], bank[:, :], ACT.Copy, after=[mark])
        project(k, nT, io["w_in_2"], 2 * BANK, 1, keep_v, a=NT)
        vv = val[:, :, :].rearrange("p (m t) c -> p m t c", t=2)
        for lo, hi, src in ((0, W, vv[W:P, 0:NT, 0, :]), (W, P, vv[0:W, 1:NT, 0, :])):
            n = NT if lo == 0 else NT - 1
            m = k.slot[0](nc.sync.dma_start(vv[lo:hi, 0:n, 1, :], src))
        SETS = 2 * pairs
        q2, ob = [sb(P, P) for _ in range(SETS)], [sb(P, P) for _ in range(SETS)]
        sc, pT = [sb(P, KH * W) for _ in range(SETS)], [sb(P, KH * W) for _ in range(SETS)]
        st = [sb(P, 4) for _ in range(SETS)]
        for n in range(SETS):
            k.V(v.memset, q2[n][:, :], 0.0, after=[m, biased])
        for p in range(pairs):
            b3 = bias[:, p, :].rearrange("p (r c) -> p r c", c=W)
            k.V(v.tensor_tensor, b3, b3, wide(k.c("window"), 1, 2 * KH - 1), ALU.add)
        k.meet()

        def pair(r, n, i, lo, dr):
            p = n % pairs
            bank = k.bank[n]
            k.A(q2[n][0:W, 0:W], qkT[0:W, p, ds(i * W, W)], ACT.Copy, scale=NAD ** -0.5, after=[r.step(k.p, n + 1)], chain=False)
            m = k.A(q2[n][W:P, W:P], qkT[W:P, p, ds(i * W, W)], ACT.Copy, scale=NAD ** -0.5, chain=False)
            k.wait(nc.tensor, m)
            t = k.p(nc.tensor.matmul(bank[:, :], q2[n][:, :], qkT[:, pairs + p, ds(lo * W, KH * W)], start=True, stop=True))
            yield
            m = k.V(v.tensor_tensor, sc[n][:, :], bank[:, :], bias[:, p, ds(dr * W, KH * W)], ALU.add, after=[t, r.step(k.p, SETS + n + 1)])
            m = k.V(v.tensor_reduce, st[n][:, 0:1], sc[n][:, :], AX.X, ALU.max, after=[m])
            m = k.V(v.tensor_scalar, st[n][:, 1:2], st[n][:, 0:1], -1.0, None, ALU.mult, after=[m])
            m = k.A(sc[n][:, :], sc[n][:, :], ACT.Exp, bias=st[n][:, 1:2], accum_out=st[n][:, 2:3], after=[m])
            yield
            t = transposes(k, bank, sc[n][:, :], after=[m])
            yield
            mr = k.V(v.reciprocal, st[n][:, 3:4], st[n][:, 2:3], after=[m])
            m = k.V(v.tensor_copy, pT[n][:, :], bank[:, :], after=[t])
            yield
            k.wait(nc.tensor, m)
            for q in range(4):
                t = nc.tensor.matmul(bank[:, 0:P], pT[n][:, q * P:(q + 1) * P],
                                     val[:, ds(lo + 2 * q, 1), p * P:(p + 1) * P].squeeze(1), start=q == 0, stop=q == 3)
            t = k.p(t)
            yield
            m = k.A(ob[n][:, :], bank[:, 0:P], ACT.Copy, scale=st[n][:, 3:4], after=[t, mr])
            yield
            k.wait(nc.tensor, m)
            t = k.p(nc.tensor.transpose(bank[:, 0:P], ob[n][:, :], k.c("ident")))
            yield
            k.A(mixT[0:W, p, ds(i * W, W)], bank[0:W, 0:W], ACT.Copy, after=[t], chain=False)
            k.A(mixT[W:P, p, ds(i * W, W)], bank[W:P, W:P], ACT.Copy, chain=False)

        with k.rounds(ROWS // 2, p=4 * SETS, v=5 * SETS, a=6 * SETS) as r:
            streams = []
            for row in range(2):
                i = k.nc.snap(r.i * 2 + row, min_val=0, max_val=ROWS - 1)
                lo = window_start(k, i)
                dr = k.nc.snap(lo - i + (KH - 1), min_val=0, max_val=KH - 1)
                streams += [pair(r, row * pairs + p, i, lo, dr) for p in range(pairs)]
            interleave(*streams)
    k.meet()


def window_start(k, i):
    lo = (i - KH // 2) * (i >= KH // 2) - (i - (ROWS - KH // 2)) * (i >= ROWS - KH // 2)
    return k.nc.snap(lo, min_val=0, max_val=ROWS - KH)


def log_sigmoid(k, out, x, t, m):
    v = k.nc.vector
    m = k.A(t, x, ACT.Abs, after=[m])
    m = k.A(t, t, ACT.Exp, scale=-1.0, after=[m])
    m = k.A(t, t, ACT.Ln, bias=1.0, after=[m])
    m = k.V(v.scalar_tensor_tensor, out, x, 0.0, t, ALU.min, ALU.subtract, after=[m])
    return k.V(v.tensor_scalar, out, out, 1.0 / 16.0, None, ALU.mult, after=[m])


def gla(k, nT, mixT):
    nc, io = k.nc, k.io
    v, g = nc.vector, nc.gpsimd
    KW2 = RH * DK
    RANK = 16
    hd = lambda ap, d=DH: ap.rearrange("p (h d) -> p h d", d=d)
    with ExitStack() as c:
        sb = lambda *s: c.enter_context(k.area(list(s), F32))
        qkvr = sb(P, NT, 3 * BANK)

        def keep(chunk, m, bank, mark):
            if chunk == 2:
                k.A(qkvr[:, m, 2 * BANK:], bank[:, :], ACT.Silu, after=[mark])
            else:
                k.V(v.tensor_copy, qkvr[:, m, chunk * BANK:(chunk + 1) * BANK], bank[:, :], after=[mark])
        project(k, nT, io["w_in_2"], 3 * BANK, 3, keep)
        oacc = sb(P, NT, BANK)
        la = [sb(P, NT, KW2) for _ in range(2)]
        ng = sb(P, DV)
        with ExitStack() as c2:
            sb2 = lambda *s: c2.enter_context(k.area(list(s), F32))
            wz, zT, gu, gbias = sb2(P, NK, 2 * RANK), [sb2(RANK, T) for _ in range(2)], sb2(RANK, 2, KW2), sb2(P, 2, KW2)
            load_columns(k, 0, wz[:, :, :], io["w_in_2"], 6 * BANK, 2 * RANK)
            for n, way in enumerate(("fwd", "bwd")):
                k.slot[0](nc.sync.dma_start(gu[:, n, :], io[f"gate_up_{way}"]))
                k.slot[0](nc.sync.dma_start(gbias[:, n, :], spread(io[f"gate_bias_{way}"], KW2)))
            loaded = k.slot[0](nc.sync.dma_start(ng[:, :], spread(io["gla_norm_g"], DV)))
            k.wait(nc.tensor, loaded)
            for n in range(2):
                for h in range(2):
                    b = k.bank[2 * n + h]
                    for f in range(NK):
                        tt = nc.tensor.matmul(b[0:RANK, :], wz[:, f, n * RANK:(n + 1) * RANK], nT[:, f, h * BANK:(h + 1) * BANK],
                                              start=f == 0, stop=f == NK - 1)
                    m = k.V(v.tensor_copy, zT[n][:, h * BANK:(h + 1) * BANK], b[0:RANK, :], after=[k.p(tt)])
            k.wait(nc.tensor, m)
            k.wait(nc.vector, loaded)
            second = oacc[:, :, :].rearrange("p m (n d) -> p n m d", n=2)
            z_read = k.now(k.v)
            for n in range(2):
                for m in range(NT):
                    b = k.bank[(4 * n + m // 2 + 4) % 8]
                    if m == 0:
                        k.wait(nc.tensor, *z_read)
                    tt = nc.tensor.matmul(b[:, m % 2 * KW2:(m % 2 + 1) * KW2], zT[n][:, m * P:(m + 1) * P], gu[:, n, :], start=True, stop=True)
                    if m % 2:
                        mm = k.V(v.tensor_tensor, la[n][:, m - 1:m + 1, :], b[:, :].rearrange("p (m d) -> p m d", d=KW2),
                                 wide(gbias[:, n, :], 1, 2), ALU.add, after=[k.p(tt)])
                log_sigmoid(k, la[n][:, :, :], la[n][:, :, :], second[:, n], mm)
            k.meet()

        two_of = lambda make: [make() for _ in range(2)]
        lt, eb, enb, ek, qd, ki, kt = (two_of(lambda: sb(P, KW2)) for _ in range(7))
        vt, qkT, AT, o, sq = (two_of(lambda: sb(P, BANK)) for _ in range(5))
        ss, dec, state = two_of(lambda: sb(P, RH)), two_of(lambda: sb(P, 2, 2)), two_of(lambda: sb(P, 2, DV))

        def turn(r, back, i, finish):
            sums, mask = ("after", "behind") if back else ("upto", "upto")
            n = int(back)
            for _ in range(n * 2):
                yield
            bank = k.bank[4 * n:4 * n + 4]
            row = qkvr[:, ds(i, 1), :].squeeze(1)
            ml = k.V(v.tensor_copy, lt[n][:, :], la[n][:, ds(i, 1), :].squeeze(1), after=[r.last(k.p)])
            mv = k.A(vt[n][:, :], row[:, BANK:2 * BANK], ACT.Copy, after=[r.last(k.p)])
            k.wait(nc.tensor, ml, mv, r.last(k.v), r.last(k.a))
            nc.tensor.matmul(bank[0][:, 0:KW2], k.c(sums), lt[n][:, :], start=True, stop=True)
            nc.tensor.matmul(bank[0][:, KW2:], k.c("chunk"), lt[n][:, :], start=True, stop=True)
            for p in range(2):
                t = nc.tensor.matmul(bank[3][:, 2 * p:2 * p + 2], lt[n][:, p * P:(p + 1) * P], k.c("halves"), start=True, stop=True)
            t = k.p(t)
            yield
            me = k.A(eb[n][:, :], bank[0][:, 0:KW2], ACT.Exp, after=[t, r.last(k.v)])
            mn = k.A(enb[n][:, :], bank[0][:, 0:KW2], ACT.Exp, scale=-1.0, after=[r.last(k.g)])
            md = k.A(dec[n][:, :, :], bank[3][:, 0:4].rearrange("p (a b) -> p a b", b=2), ACT.Exp)
            mb = k.V(v.tensor_copy, ek[n][:, :], bank[0][:, 0:KW2], after=[t, r.last(k.g), mn])
            m = k.V(v.tensor_tensor, ek[n][:, :], bank[0][:, KW2:], ek[n][:, :], ALU.subtract, after=[mb])
            yield
            mk = k.A(ek[n][:, :], ek[n][:, :], ACT.Exp, after=[m])
            mq = k.V(v.scalar_tensor_tensor, qd[n][:, :], row[:, 0:KW2], DK ** -0.5, eb[n][:, :], ALU.mult, ALU.mult, after=[me])
            mi = k.V(v.tensor_tensor, ki[n][:, :], row[:, KW2:BANK], enb[n][:, :], ALU.mult, after=[mn])
            mt = k.G(g.tensor_tensor, kt[n][:, :], row[:, KW2:BANK], ek[n][:, :], ALU.mult, after=[mk, r.last(k.p)])
            yield
            k.wait(nc.tensor, mq, mi, m)
            for p in range(2):
                nc.tensor.transpose(bank[0][:, p * P:(p + 1) * P], qd[n][:, p * P:(p + 1) * P], k.c("ident"))
                t = nc.tensor.transpose(bank[0][:, (2 + p) * P:(3 + p) * P], ki[n][:, p * P:(p + 1) * P], k.c("ident"))
            t = k.p(t)
            m = k.V(v.tensor_copy, qkT[n][:, :], bank[0][:, :], after=[t])
            yield
            k.wait(nc.tensor, m)
            for u in range(2):
                ch = slice(u * DK, (u + 1) * DK)
                for p in range(2):
                    t = nc.tensor.matmul(bank[1 + u][:, p * P:(p + 1) * P], qkT[n][ch, (2 + p) * P:(3 + p) * P], qkT[n][ch, p * P:(p + 1) * P],
                                         start=True, stop=True)
                t = k.p(t)
                ma = k.V(v.tensor_tensor, AT[n][:, :].rearrange("p (a u d) -> p a u d", a=2, u=2)[:, :, u, :],
                         hd(bank[1 + u][:, 0:2 * P]), wide(k.c(mask), 1, 2), ALU.mult, after=[t])
            k.wait(nc.tensor, mt, md)
            tc = {}
            for q in range(2):
                rows = slice(q * DC, (q + 1) * DC)
                for p in range(2):
                    t = nc.tensor.matmul(bank[3 * q][:, p * 2 * DV:(p + 1) * 2 * DV], kt[n][rows, p * P:(p + 1) * P],
                                         vt[n][rows, p * 2 * DV:(p + 1) * 2 * DV], start=True, stop=True)
                tc[q] = k.p(t)
            yield
            k.wait(nc.tensor, ma)
            ob = bank[1:3]
            for h in range(RH):
                nc.tensor.matmul(ob[h % 2][:, h // 2 * DV:(h // 2 + 1) * DV], AT[n][:, h * P:(h + 1) * P], vt[n][:, h * DV:(h + 1) * DV], start=h < 2, stop=False,
                                 skip_group_check=True)
            for q in ((1, 0) if back else (0, 1)):
                rows = slice(q * DC, (q + 1) * DC)
                k.settled(nc.tensor)
                for h in range(RH):
                    p, u = h // 2, h % 2
                    ch = slice(u * DK, (u + 1) * DK)
                    t = nc.tensor.matmul(ob[u][rows, p * DV:(p + 1) * DV], qkT[n][ch, p * P + q * DC:p * P + (q + 1) * DC], state[n][ch, p, :],
                                         start=False, stop=True, skip_group_check=True)
                t = k.p(t)
                yield
                for h in range(RH):
                    p, u = h // 2, h % 2
                    ch = slice(u * DK, (u + 1) * DK)
                    m = k.V(v.scalar_tensor_tensor, state[n][ch, p, :], state[n][ch, p, :], dec[n][ch, p, q:q + 1],
                            bank[3 * q][ch, h * DV:(h + 1) * DV], ALU.mult, ALU.add, after=[t, tc[q], md], chain=h == 0)
                yield
                k.wait(nc.tensor, m)
            acc = oacc[:, ds(i, 1), :].squeeze(1)
            two = lambda ap, u: ap.rearrange("p (a u d) -> p a u d", a=2, u=2)[:, :, u, :]
            for u in range(2):
                src = hd(ob[u][:, 0:2 * DV])
                if not finish:
                    m = k.V(v.tensor_copy, two(acc, u), src, after=[t])
                else:
                    m = k.V(v.tensor_tensor, two(o[n][:, :], u), src, two(acc, u), ALU.add, after=[t])
            if finish:
                yield
                m = yield from heads_norm(k, hd(o[n][:, :]), hd(sq[n][:, :]), ss[n][:, :], ng[:, :], hd(row[:, 2 * BANK:]), DV, m, t)
                t = transposes(k, bank[0], o[n][:, :], after=[m])
                yield
                k.A(mixT[:, 4:6, ds(i * P, P)], bank[0][:, 0:2 * P].rearrange("p (h t) -> p h t", h=2), ACT.Copy, after=[t])
                k.A(mixT[:, 6:8, ds(i * P, P)], bank[0][:, 2 * P:].rearrange("p (h t) -> p h t", h=2), ACT.Copy)

        for n in range(2):
            zero = k.V(v.memset, state[n][:, :, :], 0.0)
        k.wait(nc.tensor, zero)
        for finish in (False, True):
            with k.rounds(NT // 2, p=18 if finish else 16, v=50 if finish else 36, a=16 if finish else 10, g=2) as r:
                first = r.i + (NT // 2 if finish else 0)
                final = nc.snap((NT // 2 - 1 if finish else NT - 1) - r.i, min_val=0, max_val=NT - 1)
                interleave(turn(r, False, first, finish), turn(r, True, final, finish))
            k.meet()


def mlp_up(k, nT, uT):
    nc = k.nc

    def use(r, j, s, banks, mark):
        for h in range(2):
            dst = uT[:, ds(j, 1), h * BANK:(h + 1) * BANK].squeeze(1)
            m = k.A(dst, banks[h][:, :], ACT.Relu, after=[mark])
            k.V(nc.vector.tensor_tensor, dst, dst, banks[h][:, :], ALU.mult, after=[m])
    channels(k, nT, k.io["w_ff1"], 0, NF, use, p=2, v=4, a=4)
    k.meet()


def mlp_down(k, uT, hT, x_dram, out_dram):
    nc = k.nc
    v = nc.vector
    with ExitStack() as c:
        sb = lambda *s: c.enter_context(k.area(list(s), F32))
        w = [hT[:, 2 * n:2 * n + 2, :].rearrange("p k (g c) -> p (k g) c", c=P) for n in range(4)]
        yT, xc = [sb(P, T) for _ in range(2)], [sb(P, NT, P) for _ in range(2)]
        with k.rounds(NK // 2, s0=1, s1=1, s2=1, s3=1, s4=1, s5=1, s6=1, s7=1, p=8, a=2, v=6) as r:
            evacuated, mx, ms = {}, {}, {}
            for n in range(2):
                cols = ds(r.i * 2 * P + n * P, P)
                for s in range(2):
                    b = 2 * n + s
                    k.wait(nc.sync, r.step(k.p, b + 1))
                    rows = k.io["w_ff2"][s * (DFF // 2):(s + 1) * (DFF // 2), cols]
                    loaded = k.slot[b](nc.sync.dma_start(w[b], rows.rearrange("(f p) c -> p f c", p=P)))
                    k.wait(nc.tensor, loaded, *([r.step(k.v, n + 1), r.step(k.a, n + 1)] if s == 0 else []))
                    for f in range(NF // 2):
                        for h in range(2):
                            ff = s * (NF // 2) + f
                            t = nc.tensor.matmul(k.bank[4 * n + h][:, :], w[b][:, f, :], uT[:, ff, h * BANK:(h + 1) * BANK],
                                                 start=ff == 0, stop=ff == NF - 1)
                    t = k.p(t)
                evacuated[n] = (k.A(yT[n][:, 0:BANK], k.bank[4 * n][:, :], ACT.Copy, after=[t, r.last(k.p)]),
                                k.V(v.tensor_copy, yT[n][:, BANK:], k.bank[4 * n + 1][:, :], after=[t, r.last(k.p)]))
            for n in range(2):
                k.wait(nc.sync, r.last(k.slot[6 + n]))
                mx[n] = k.slot[4 + n](nc.sync.dma_start(xc[n][:, :, :], x_dram[:, ds(r.i * 2 * P + n * P, P)].rearrange("(m p) c -> p m c", p=P)))
            for n in range(2):
                for h in range(2):
                    t = transposes(k, k.bank[4 * n + 2 + h], yT[n][:, h * BANK:(h + 1) * BANK], after=[evacuated[n][h], r.last(k.v)])
                    part = xc[n][:, 4 * h:4 * h + 4, :]
                    ms[n] = k.V(v.tensor_tensor, part, part, k.bank[4 * n + 2 + h][:, :].rearrange("p (m c) -> p m c", c=P), ALU.add,
                                after=[t, mx[n]])
            for n in range(2):
                k.wait(nc.scalar, ms[n])
                k.slot[6 + n](nc.scalar.dma_start(out_dram[:, ds(r.i * 2 * P + n * P, P)].rearrange("(m p) c -> p m c", p=P), xc[n][:, :, :]))
    k.meet()


def final_norm(k, x, norm_w, out):
    nc = k.nc
    v = nc.vector
    with ExitStack() as c:
        sq = c.enter_context(k.area([P, D], F32))
        ss = c.enter_context(k.area([P, 2 * NT], F32))
        for n in range(NT):
            s0, s1 = ss[:, 2 * n:2 * n + 1], ss[:, 2 * n + 1:2 * n + 2]
            m = k.A(sq[:, :], x[:, n, :], ACT.Square, accum_out=s0)
            m = rstd(k, s1, s0, D, m)
            m = k.V(v.scalar_tensor_tensor, x[:, n, :], x[:, n, :], s1, norm_w[:, :], ALU.mult, ALU.mult, after=[m])
            k.wait(nc.sync, m)
            k.store(nc.sync.dma_start(out[0, n * P:(n + 1) * P, :], x[:, n, :]))


def load_rows(k, x, dram):
    return k.slot[8](k.nc.sync.dma_start(x[:, :, :], dram.rearrange("(m p) c -> p m c", p=P)))


def build(nc, io, out, tap=None):
    with ExitStack() as ctx:
        k = Program(nc, ctx, io)
        tap = tap or (lambda *a: None)
        sb = lambda *s, dt=F32: ctx.enter_context(k.area(list(s), dt))
        k.bank = [ctx.enter_context(nc.psum_tensor(f"bank{n}", [P, BANK], F32)) for n in range(8)]
        table = shape_constants()
        width = sum(a.shape[1] for a in table.values())
        consts = sb(P, width)
        k.slot[0](nc.sync.dma_start(consts[:, :], io["constants"]))
        at, where_const = 0, {}
        for name, a in table.items():
            where_const[name] = consts[:, at:at + a.shape[1]]
            at += a.shape[1]
        k.c = lambda name: where_const[name]

        xn_rows = nc.dram_tensor("xn_rows", [T, D], F32, kind="Internal").ap()
        y_rows = nc.dram_tensor("y_rows", [BLOCKS * P, D], F32, kind="Internal").ap()
        x_rows = [nc.dram_tensor(f"x_rows{n}", [T, D], F32, kind="Internal").ap() for n in range(4)]

        rpb_rows = nc.dram_tensor("rpb_rows", [NAH, 2 * KH - 1, W, 2 * W - 1], F32, kind="Internal").ap()

        cols = sb(P, 4, NK)
        k.slot[1](nc.sync.dma_start(cols[:, :, :], io["norm_columns"]))
        k.meet()
        mod = sb(P, 6 * NK)
        affine = sb(P, 4, NK)
        gate1, gate2 = sb(P, D), sb(P, D)
        gates = sb(P, NT, 2)
        where, tokens = sb(P, NT, 2, dt=U32), sb(P, BLOCKS + 1, dt=U32)
        experts = sb(P, BLOCKS + 1, dt=I32)
        hT = sb(P, NK, T)

        def with_x(source, *steps):
            with k.area([P, NT, D], F32) as x:
                loaded = load_rows(k, x, source)
                k.wait(nc.vector, loaded)
                k.wait(nc.scalar, loaded)
                for step in steps:
                    step(x)
                k.meet()

        def to(dram):
            def step(x):
                k.wait(nc.sync, *k.now(k.v, k.g))
                k.store(nc.sync.dma_start(dram.rearrange("(m p) c -> p m c", p=P), x[:, :, :]))
            return step

        x_at_first = ctx.enter_context(ExitStack())
        x = x_at_first.enter_context(k.area([P, NT, D], F32))
        load_rows(k, x, io["x"])
        modulation(k, mod, (gate1, gate2))
        for n, j in ((0, 0), (1, 3)):
            k.V(nc.vector.scalar_tensor_tensor, affine[:, 2 * n, :], mod[:, (j + 1) * NK:(j + 2) * NK], 1.0, cols[:, n, :], ALU.add, ALU.mult)
            k.V(nc.vector.tensor_copy, affine[:, 2 * n + 1, :], mod[:, j * NK:(j + 1) * NK])
        k.meet()
        norm_transpose(k, x, hT, affine[:, 0, :], affine[:, 1, :])
        x_at_first.close()
        tap("hT", hT)
        with k.area([P, NK, T], F32) as mixT:
            with k.area([P, NT, DH // 2], F32) as cos, k.area([P, NT, DH // 2], F32) as sin:
                rotary_tables(k, cos, sin)
                tap("cos", cos)
                tap("sin", sin)
                retention(k, hT, mixT, cos, sin, lambda: k.slot[9](nc.sync.dma_start(rpb_rows, wide(io["rpb"], 2, W))))
            delta(k, hT, mixT)
            tap("mixT", mixT)
            with_x(io["x"], lambda x: residual(k, mixT, io["w_out"], x, gate1), to(x_rows[0]),
                   lambda x: norm_transpose(k, x, hT, affine[:, 2, :], affine[:, 3, :], xn_dram=xn_rows))
        route(k, hT, gates, where, tokens, experts)
        for name, value in (("gates", gates), ("where", where), ("tokens", tokens), ("experts", experts)):
            tap(name, value)
        experts_pass(k, affine[:, 2, :], affine[:, 3, :], tokens, experts, xn_rows, y_rows)
        with k.area([P, D], F32) as norm_w:
            k.slot[2](nc.sync.dma_start(norm_w[:, :], spread(io["final_norm_w"], D)))
            k.meet()
            with_x(x_rows[0], lambda x: combine(k, x, gates, where, y_rows, gate2, norm_w), to(x_rows[1]), lambda x: tap("x3", x),
                   lambda x: norm_transpose(k, x, hT, cols[:, 2, :], None))
        with k.area([P, NK, T], F32) as mixT:
            neighbourhood(k, hT, mixT, rpb_rows)
            gla(k, hT, mixT)
            tap("mixT2", mixT)
            with_x(x_rows[1], lambda x: residual(k, mixT, io["w_out_2"], x, None), to(x_rows[2]),
                   lambda x: norm_transpose(k, x, hT, cols[:, 3, :], None))
        with k.area([P, NF, T], F32) as uT:
            mlp_up(k, hT, uT)
            mlp_down(k, uT, hT, x_rows[2], x_rows[3])
        with k.area([P, D], F32) as norm_w:
            k.slot[2](nc.sync.dma_start(norm_w[:, :], spread(io["ln_final_g_2"], D)))
            k.meet()
            with_x(x_rows[3], lambda x: final_norm(k, x, norm_w, out))


def arrays_of(inputs):
    a = {n: np.ascontiguousarray(v) for n, v in inputs.items()}
    by_feature = lambda v: v.reshape(NK, P).T
    vec = lambda n: a[n].reshape(-1)
    io = {n: a[n][0] for n in ("x", "w_ada", "w_in", "w_out", "w_group", "w_expert", "w1", "w3", "w2",
                               "w_in_2", "w_out_2", "w_ff1_2", "w_ff2_2")}
    io["w_ff1"], io["w_ff2"] = io.pop("w_ff1_2"), io.pop("w_ff2_2")
    io["b_ada"] = a["b_ada"].reshape(1, -1)
    io["cT"] = by_feature(a["c"].reshape(-1))
    io["positions"] = a["positions"].reshape(NT, P).T
    io["norm_columns"] = np.stack([by_feature(a[n].reshape(-1)) for n in ("norm1_w", "norm2_w", "ln_mix_g_2", "ln_ff_g_2")], 1)
    io["conv"] = a["conv_w"][0].reshape(4, 12, P).transpose(2, 1, 0)
    for n, src in (("a_log", "a_log"), ("dt_bias", "dt_bias"), ("dn_norm_w", "dn_norm_w"), ("b_group", "b_group"),
                   ("b_expert", "b_expert"), ("final_norm_w", "final_norm_w"), ("ln_final_g_2", "ln_final_g_2"),
                   ("gla_norm_g", "gla_norm_g_2"), ("gate_bias_fwd", "gla_gate_bias_fwd_2"), ("gate_bias_bwd", "gla_gate_bias_bwd_2")):
        io[n] = vec(src)
    io["gate_up_fwd"], io["gate_up_bwd"] = a["gla_gate_up_fwd_2"][0], a["gla_gate_up_bwd_2"][0]
    rpb = np.zeros((NAH, 2 * KH - 1, 2 * W - 1), np.float32)
    rpb[:, :, W - KW:W - KW + 2 * KW - 1] = a["na_rpb_2"][0]
    io["rpb"] = rpb
    io["constants"] = np.concatenate(list(shape_constants().values()), 1)
    return {n: np.ascontiguousarray(v) for n, v in io.items()}


def kernel(**inputs):
    import concourse.bacc as bacc
    from concourse.bass_utils import run_bass_kernel_spmd as run

    arrays = arrays_of({n: np.asarray(v) for n, v in inputs.items()})
    nc = bacc.Bacc("TRN2", target_bir_lowering=False, num_devices=1)
    io = {n: nc.dram_tensor(f"in_{n}", a.shape, mybir.dt.from_np(a.dtype), kind="ExternalInput").ap() for n, a in arrays.items()}
    out = nc.dram_tensor("out", [1, T, D], F32, kind="ExternalOutput").ap()
    build(nc, io, out)
    result = run(nc, [{f"in_{n}": a for n, a in arrays.items()}], core_ids=[0])
    return result.results[0]["out"]
```
